# Optimizing a Trainium2 kernel written in Bass

```python
import math
import jax, jax.numpy as jnp
from jax import lax
import numpy as np

D_MODEL = 1024
BATCH = 1
SEQ = 128
DEPTH = 2
DEC_BATCH = 1
DEC_SEQ = 512
PAST_LEN = 256

GRID_W = 64
N_EVEN = (DEPTH + 1) // 2
N_ODD = DEPTH // 2
N_MOD = 9
D_FF = 2816
EPS = 1e-6
ROPE_BASE = 10000.0
NEG = -1e30
MLA_HEADS = 8
MLA_NOPE = 64
MLA_ROPE = 32
MLA_QK = MLA_NOPE + MLA_ROPE
MLA_V = 64
MLA_Q_LORA = 256
MLA_KV_LORA = 128
M_HEADS = 4
M_DK = 64
M_DV = 128
M_CHUNK = 128
S_HEADS = 16
S_KV_HEADS = 4
S_GROUP = S_HEADS // S_KV_HEADS
S_HEAD_DIM = 64
S_WINDOW = 128
S_BLOCK = 128
DENSE_Q_BLOCK = 128
DENSE_SWEEP_KEYS = 2048

EVEN_SPLITS = (MLA_Q_LORA, MLA_KV_LORA, MLA_ROPE, M_HEADS * M_DK, M_HEADS * M_DK, M_HEADS * M_DV, M_HEADS * M_DV, 4 * M_HEADS)
EVEN_SPLIT_IDX = tuple(int(v) for v in np.cumsum(EVEN_SPLITS)[:-1])
EVEN_IN = sum(EVEN_SPLITS)
EVEN_MIX = MLA_HEADS * MLA_V + M_HEADS * M_DV
ODD_IN = (S_HEADS + 2 * S_KV_HEADS) * S_HEAD_DIM
ODD_MIX = S_HEADS * S_HEAD_DIM

kernel_name = 'hybrid_mla_mlstm_swa_flow_step'

def rmsnorm(x, g):
    x32 = x.astype(jnp.float32)
    y = x32 * lax.rsqrt(jnp.mean(x32 * x32, -1, keepdims=True) + EPS)
    return (y * g.astype(jnp.float32)).astype(x.dtype)

def swiglu(h, wg, wu, wd):
    return (jax.nn.silu(h @ wg) * (h @ wu)) @ wd

def adaln(cond, w, b):
    mod = jax.nn.silu(cond) @ w + b
    return mod.reshape(cond.shape[0], N_MOD, D_MODEL)

def modulate(x, g_pre, shift, scale):
    return (rmsnorm(x, g_pre) * (1 + scale[:, None]) + shift[:, None]).astype(x.dtype)

def add_residual(x, y, g_post, gate, weight):
    return (x + weight * gate[:, None] * rmsnorm(y, g_post)).astype(x.dtype)

def axial_rope(t_len, rot_dim):
    rows = t_len // GRID_W
    nf = rot_dim // 4
    inv = ROPE_BASE ** (-jnp.arange(nf, dtype=jnp.float32) / nf)
    row = jnp.repeat(jnp.arange(rows, dtype=jnp.float32), GRID_W)
    col = jnp.tile(jnp.arange(GRID_W, dtype=jnp.float32), rows)
    ang = jnp.stack([row[:, None] * inv, col[:, None] * inv], axis=1)
    return jnp.cos(ang), jnp.sin(ang)

def apply_rope(x, cos, sin):
    shp = x.shape
    xr = x.astype(jnp.float32).reshape(shp[:-1] + (2, 2, shp[-1] // 4))
    x1, x2 = xr[..., 0, :], xr[..., 1, :]
    out = jnp.stack([x1 * cos - x2 * sin, x2 * cos + x1 * sin], axis=-2)
    return out.reshape(shp).astype(x.dtype)

def _attend_block(qb, k, v, scale, sink):
    s = jnp.einsum('bhgqd,bhkd->bhgqk', qb, k).astype(jnp.float32) * scale
    if sink is None:
        p = jax.nn.softmax(s, axis=-1)
    else:
        sk = jnp.broadcast_to(sink.astype(jnp.float32)[None, :, :, None, None], s.shape[:-1] + (1,))
        p = jax.nn.softmax(jnp.concatenate([s, sk], -1), axis=-1)[..., :-1]
    return jnp.einsum('bhgqk,bhkd->bhgqd', p.astype(v.dtype), v)

def dense_attend(q, k, v, scale, sink=None):
    if k.shape[2] < DENSE_SWEEP_KEYS:
        return _attend_block(q, k, v, scale, sink)
    b, hk, g, tq, d = q.shape
    nq = tq // DENSE_Q_BLOCK
    qs = jnp.moveaxis(q.reshape(b, hk, g, nq, DENSE_Q_BLOCK, d), 3, 0)
    out = lax.map(lambda qb: _attend_block(qb, k, v, scale, sink), qs)
    return jnp.moveaxis(out, 0, 3).reshape(b, hk, g, tq, v.shape[-1])

def banded_attend(q, k, v, ck, cv, scale, sink):
    b, hk, g, t, d = q.shape
    nb = t // S_BLOCK
    qb = q.reshape(b, hk, g, nb, S_BLOCK, d)

    def bands(a):
        ap = jnp.pad(a, ((0, 0), (0, 0), (S_BLOCK, S_BLOCK), (0, 0))).reshape(b, hk, nb + 2, S_BLOCK, a.shape[-1])
        return jnp.concatenate([ap[:, :, :-2], ap[:, :, 1:-1], ap[:, :, 2:]], axis=3)

    kb, vb = bands(k), bands(v)
    blk = jnp.arange(nb)[:, None, None] * S_BLOCK
    qpos = blk + jnp.arange(S_BLOCK)[None, :, None]
    kpos = blk - S_BLOCK + jnp.arange(3 * S_BLOCK)[None, None, :]
    allowed = (jnp.abs(qpos - kpos) <= S_WINDOW) & (kpos >= 0) & (kpos < t)
    s_loc = jnp.where(allowed, jnp.einsum('bhgnqd,bhnkd->bhgnqk', qb, kb).astype(jnp.float32) * scale, NEG)
    s_ctx = jnp.einsum('bhgnqd,bhkd->bhgnqk', qb, ck).astype(jnp.float32) * scale
    s_sink = jnp.broadcast_to(sink.astype(jnp.float32)[None, :, :, None, None, None], s_loc.shape[:-1] + (1,))
    p = jax.nn.softmax(jnp.concatenate([s_ctx, s_loc, s_sink], -1), axis=-1)
    lc = ck.shape[2]
    p_ctx = p[..., :lc].astype(v.dtype)
    p_loc = p[..., lc:lc + 3 * S_BLOCK].astype(v.dtype)
    o = jnp.einsum('bhgnqk,bhkd->bhgnqd', p_ctx, cv) + jnp.einsum('bhgnqk,bhnkd->bhgnqd', p_loc, vb)
    return o.reshape(b, hk, g, t, d)

def mlstm_scan(q, k, v, log_i, log_f, c0, n0, m0):
    b_, h_, t_, _ = q.shape
    nc = t_ // M_CHUNK

    def chunks(a):
        return jnp.moveaxis(a.reshape((b_, h_, nc, M_CHUNK) + a.shape[3:]), 2, 0)

    causal = jnp.tril(jnp.ones((M_CHUNK, M_CHUNK), bool))

    def step(carry, inp):
        cm, nv, m = carry
        qc, kc, vc, li, lf = inp
        bcum = jnp.cumsum(lf, axis=-1)
        dmat = jnp.where(causal, bcum[..., :, None] - bcum[..., None, :] + li[..., None, :], NEG)
        inter = m[..., None] + bcum
        mt = jnp.maximum(inter, dmat.max(-1))
        w_inter = jnp.exp(inter - mt)
        a = jnp.einsum('bhtd,bhsd->bhts', qc, kc) * jnp.exp(dmat - mt[..., None])
        num = w_inter[..., None] * jnp.einsum('bhtd,bhde->bhte', qc, cm) + jnp.einsum('bhts,bhse->bhte', a, vc)
        den = w_inter * jnp.einsum('bhtd,bhd->bht', qc, nv) + a.sum(-1)
        hc = num / jnp.maximum(jnp.abs(den), jnp.exp(-mt))[..., None]
        m_new = mt[..., -1]
        w_s = jnp.exp(bcum[..., -1:] - bcum + li - m_new[..., None])
        w_c = jnp.exp(m + bcum[..., -1] - m_new)
        c_new = w_c[..., None, None] * cm + jnp.einsum('bhs,bhsd,bhse->bhde', w_s, kc, vc)
        n_new = w_c[..., None] * nv + jnp.einsum('bhs,bhsd->bhd', w_s, kc)
        return (c_new, n_new, m_new), hc

    (cm, nv, m), hs = lax.scan(step, (c0, n0, m0), tuple(chunks(a) for a in (q, k, v, log_i, log_f)))
    h = jnp.moveaxis(hs, 0, 2).reshape(b_, h_, t_, v.shape[-1])
    return h, cm, nv, m

def even_mixer(h, w_in, g_qa, g_kva, w_qb, w_kvb, gate_b, g_mout, w_out,
               ctx_ckv=None, ctx_krope=None, m_state=None, rope=None):
    bsz, t_len, _ = h.shape
    q_a, kv_a, k_rope, mq, mk, mv, mo, mg = jnp.split(h @ w_in, EVEN_SPLIT_IDX, axis=-1)
    ckv = rmsnorm(kv_a, g_kva)
    q = jnp.moveaxis((rmsnorm(q_a, g_qa) @ w_qb).reshape(bsz, t_len, MLA_HEADS, MLA_QK), 1, 2)
    if ctx_ckv is None:
        keys_ckv, keys_kr = ckv, k_rope
    else:
        q = jnp.concatenate([q[..., :MLA_NOPE], apply_rope(q[..., MLA_NOPE:], *rope)], -1)
        keys_ckv = jnp.concatenate([ctx_ckv, ckv], 1)
        keys_kr = jnp.concatenate([ctx_krope, apply_rope(k_rope, *rope)], 1)
    t_keys = keys_ckv.shape[1]
    kv = jnp.moveaxis((keys_ckv @ w_kvb).reshape(bsz, t_keys, MLA_HEADS, MLA_NOPE + MLA_V), 1, 2)
    k = jnp.concatenate([kv[..., :MLA_NOPE],
                         jnp.broadcast_to(keys_kr[:, None], (bsz, MLA_HEADS, t_keys, MLA_ROPE))], -1)
    attn = dense_attend(q[:, :, None], k, kv[..., MLA_NOPE:], MLA_QK ** -0.5)[:, :, 0]
    attn = jnp.moveaxis(attn, 1, 2).reshape(bsz, t_len, MLA_HEADS * MLA_V)
    if m_state is None:
        c0 = jnp.zeros((bsz, 2, M_HEADS, M_DK, M_DV), jnp.float32)
        n0 = jnp.zeros((bsz, 2, M_HEADS, M_DK), jnp.float32)
        m0 = jnp.zeros((bsz, 2, M_HEADS), jnp.float32)
    else:
        c0, n0, m0 = (s.astype(jnp.float32) for s in m_state)

    def heads(a, d):
        return jnp.moveaxis(a.astype(jnp.float32).reshape(bsz, t_len, M_HEADS, d), 1, 2)

    mqh, mkh, mvh = heads(mq, M_DK), heads(mk, M_DK) * (M_DK ** -0.5), heads(mv, M_DV)
    gates = jnp.transpose((mg + gate_b).astype(jnp.float32).reshape(bsz, t_len, 4, M_HEADS), (2, 0, 3, 1))
    h_f, cf, nf_, mf = mlstm_scan(mqh, mkh, mvh, gates[0], jax.nn.log_sigmoid(gates[1]),
                                  c0[:, 0], n0[:, 0], m0[:, 0])
    fl = lambda a: jnp.flip(a, axis=2)
    h_b, cb, nb_, mb = mlstm_scan(fl(mqh), fl(mkh), fl(mvh), fl(gates[2]), fl(jax.nn.log_sigmoid(gates[3])),
                                  c0[:, 1], n0[:, 1], m0[:, 1])
    hm = h_f + fl(h_b)
    hm = hm * lax.rsqrt(jnp.mean(hm * hm, -1, keepdims=True) + EPS)
    hm = jnp.moveaxis(hm, 1, 2).reshape(bsz, t_len, M_HEADS * M_DV) * g_mout.astype(jnp.float32)
    m_out = (jax.nn.sigmoid(mo.astype(jnp.float32)) * hm).astype(h.dtype)
    y = jnp.concatenate([attn, m_out], -1) @ w_out
    state = (ckv, k_rope, jnp.stack([cf, cb], 1), jnp.stack([nf_, nb_], 1), jnp.stack([mf, mb], 1))
    return y, state

def odd_mixer(h, w_in, sink, w_out, ctx_k=None, ctx_v=None, rope=None):
    bsz, t_len, _ = h.shape
    q, k, v = jnp.split(h @ w_in, [S_HEADS * S_HEAD_DIM, (S_HEADS + S_KV_HEADS) * S_HEAD_DIM], axis=-1)
    q = jnp.moveaxis(q.reshape(bsz, t_len, S_KV_HEADS, S_GROUP, S_HEAD_DIM), 1, 3)
    k = jnp.moveaxis(k.reshape(bsz, t_len, S_KV_HEADS, S_HEAD_DIM), 1, 2)
    v = jnp.moveaxis(v.reshape(bsz, t_len, S_KV_HEADS, S_HEAD_DIM), 1, 2)
    sk = sink.reshape(S_KV_HEADS, S_GROUP)
    scale = S_HEAD_DIM ** -0.5
    if ctx_k is None:
        o = dense_attend(q, k, v, scale, sk)
    else:
        q = apply_rope(q, *rope)
        k = apply_rope(k, *rope)
        o = banded_attend(q, k, v, ctx_k, ctx_v, scale, sk)
    o = jnp.moveaxis(o, 3, 1).reshape(bsz, t_len, S_HEADS * S_HEAD_DIM)
    return o @ w_out, (k, v)

def setup_inputs(seed: int = 0) -> dict:
    key = jax.random.key(seed)
    ks = iter(jax.random.split(key, 32))
    nrm = lambda shape, s=1.0: jax.random.normal(next(ks), shape, jnp.float32) * s
    gain = lambda shape: 1.0 + nrm(shape, 0.02)
    fb = jnp.linspace(3.0, 6.0, M_HEADS)
    zb = jnp.zeros((M_HEADS,))
    gate_off = jnp.concatenate([zb, fb, zb, fb])
    return {
        'x_prompt': nrm((BATCH, SEQ, D_MODEL)),
        'x_sample': nrm((DEC_BATCH, DEC_SEQ, D_MODEL)),
        'cache_mla_ckv': nrm((DEC_BATCH, N_EVEN, PAST_LEN, MLA_KV_LORA)),
        'cache_mla_krope': nrm((DEC_BATCH, N_EVEN, PAST_LEN, MLA_ROPE)),
        'state_mlstm_C': nrm((DEC_BATCH, N_EVEN, 2, M_HEADS, M_DK, M_DV)),
        'state_mlstm_n': nrm((DEC_BATCH, N_EVEN, 2, M_HEADS, M_DK)),
        'state_mlstm_m': nrm((DEC_BATCH, N_EVEN, 2, M_HEADS), 0.5),
        'cache_swa_k': nrm((DEC_BATCH, N_ODD, S_KV_HEADS, PAST_LEN, S_HEAD_DIM)),
        'cache_swa_v': nrm((DEC_BATCH, N_ODD, S_KV_HEADS, PAST_LEN, S_HEAD_DIM)),
        'c': nrm((DEC_BATCH, D_MODEL)),
        'c_ctx': nrm((D_MODEL,)),
        'ada_w': nrm((DEPTH, D_MODEL, N_MOD * D_MODEL), D_MODEL ** -0.5),
        'ada_b': nrm((DEPTH, N_MOD * D_MODEL), 0.02),
        'norm_g': gain((DEPTH, 6, D_MODEL)),
        'ffn_w_gate': nrm((DEPTH, 2, D_MODEL, D_FF), D_MODEL ** -0.5),
        'ffn_w_up': nrm((DEPTH, 2, D_MODEL, D_FF), D_MODEL ** -0.5),
        'ffn_w_down': nrm((DEPTH, 2, D_FF, D_MODEL), D_FF ** -0.5),
        'even_w_in': nrm((N_EVEN, D_MODEL, EVEN_IN), D_MODEL ** -0.5),
        'mla_g_qa': gain((N_EVEN, MLA_Q_LORA)),
        'mla_g_kva': gain((N_EVEN, MLA_KV_LORA)),
        'mla_w_qb': nrm((N_EVEN, MLA_Q_LORA, MLA_HEADS * MLA_QK), MLA_Q_LORA ** -0.5),
        'mla_w_kvb': nrm((N_EVEN, MLA_KV_LORA, MLA_HEADS * (MLA_NOPE + MLA_V)), MLA_KV_LORA ** -0.5),
        'mlstm_gate_b': gate_off[None] + nrm((N_EVEN, 4 * M_HEADS), 0.1),
        'mlstm_g_out': gain((N_EVEN, M_HEADS * M_DV)),
        'even_w_out': nrm((N_EVEN, EVEN_MIX, D_MODEL), EVEN_MIX ** -0.5),
        'odd_w_in': nrm((N_ODD, D_MODEL, ODD_IN), D_MODEL ** -0.5),
        'swa_sink': nrm((N_ODD, S_HEADS), 0.5),
        'odd_w_out': nrm((N_ODD, ODD_MIX, D_MODEL), ODD_MIX ** -0.5),
    }

def reference(x_prompt, x_sample, cache_mla_ckv, cache_mla_krope, state_mlstm_C, state_mlstm_n,
              state_mlstm_m, cache_swa_k, cache_swa_v, c, c_ctx, ada_w, ada_b, norm_g, ffn_w_gate,
              ffn_w_up, ffn_w_down, even_w_in, mla_g_qa, mla_g_kva, mla_w_qb, mla_w_kvb, mlstm_gate_b,
              mlstm_g_out, even_w_out, odd_w_in, swa_sink, odd_w_out):
    t_lat = x_sample.shape[1]
    rope_mla = axial_rope(t_lat, MLA_ROPE)
    rope_swa = axial_rope(t_lat, S_HEAD_DIM)
    xc, xl = x_prompt, x_sample
    ckv_l, kr_l, mc_l, mn_l, mm_l, sk_l, sv_l = [], [], [], [], [], [], []
    for l in range(DEPTH):
        mc = adaln(c_ctx[None], ada_w[l], ada_b[l])
        ml = adaln(c, ada_w[l], ada_b[l])
        g = norm_g[l]
        xc = add_residual(xc, swiglu(modulate(xc, g[0], mc[:, 0], mc[:, 1]), ffn_w_gate[l, 0], ffn_w_up[l, 0],
                                     ffn_w_down[l, 0]), g[1], mc[:, 2], 0.5)
        xl = add_residual(xl, swiglu(modulate(xl, g[0], ml[:, 0], ml[:, 1]), ffn_w_gate[l, 0], ffn_w_up[l, 0],
                                     ffn_w_down[l, 0]), g[1], ml[:, 2], 0.5)
        hc = modulate(xc, g[2], mc[:, 3], mc[:, 4])
        hl = modulate(xl, g[2], ml[:, 3], ml[:, 4])
        i = l // 2
        if l % 2 == 0:
            ew = (even_w_in[i], mla_g_qa[i], mla_g_kva[i], mla_w_qb[i], mla_w_kvb[i], mlstm_gate_b[i],
                  mlstm_g_out[i], even_w_out[i])
            yc, (ckv, kr, s_c, s_n, s_m) = even_mixer(hc, *ew)
            yl, _ = even_mixer(hl, *ew, ctx_ckv=cache_mla_ckv[:, i], ctx_krope=cache_mla_krope[:, i],
                               m_state=(state_mlstm_C[:, i], state_mlstm_n[:, i], state_mlstm_m[:, i]),
                               rope=rope_mla)
            ckv_l.append(ckv)
            kr_l.append(kr)
            mc_l.append(s_c)
            mn_l.append(s_n)
            mm_l.append(s_m)
        else:
            ow = (odd_w_in[i], swa_sink[i], odd_w_out[i])
            yc, (kc, vc) = odd_mixer(hc, *ow)
            yl, _ = odd_mixer(hl, *ow, ctx_k=cache_swa_k[:, i], ctx_v=cache_swa_v[:, i], rope=rope_swa)
            sk_l.append(kc)
            sv_l.append(vc)
        xc = add_residual(xc, yc, g[3], mc[:, 5], 1.0)
        xl = add_residual(xl, yl, g[3], ml[:, 5], 1.0)
        xc = add_residual(xc, swiglu(modulate(xc, g[4], mc[:, 6], mc[:, 7]), ffn_w_gate[l, 1], ffn_w_up[l, 1],
                                     ffn_w_down[l, 1]), g[5], mc[:, 8], 0.5)
        xl = add_residual(xl, swiglu(modulate(xl, g[4], ml[:, 6], ml[:, 7]), ffn_w_gate[l, 1], ffn_w_up[l, 1],
                                     ffn_w_down[l, 1]), g[5], ml[:, 8], 0.5)
    new_ckv = jnp.stack(ckv_l, 1)
    new_krope = jnp.stack(kr_l, 1)
    new_mC = jnp.stack(mc_l, 1)
    new_mn = jnp.stack(mn_l, 1)
    new_mm = jnp.stack(mm_l, 1)
    new_sk = jnp.stack(sk_l, 1)
    new_sv = jnp.stack(sv_l, 1)
    return (xc, xl, new_ckv, new_krope, new_mC, new_mn, new_mm, new_sk, new_sv)


_drawn_inputs = setup_inputs


def setup_inputs(seed=0):
    import zlib

    import numpy as np

    out = dict(_drawn_inputs(seed))
    spreads = {}
    factors = {'cache_mla_krope': 3.382,
     'mla_g_qa': 8.0,
     'mla_g_kva': 2.918,
     'mlstm_g_out': 6.566,
     'swa_sink': 8.0}
    for name, (base, spread) in spreads.items():
        noise = np.random.default_rng([zlib.crc32(name.encode()), seed]).standard_normal(out[name].shape)
        drawn = base * np.exp(spread * noise) if base else spread * noise
        out[name] = __import__('jax').numpy.asarray(drawn.astype(out[name].dtype))
    for name, factor in factors.items():
        out[name] = (out[name] * factor).astype(out[name].dtype)
    return out
```

```python
from contextlib import ExitStack

import concourse.bass as bass
from concourse import mybir

F32 = mybir.dt.float32
F32R = mybir.dt.float32r
ACT = mybir.ActivationFunctionType
ALU = mybir.AluOpType
AX = mybir.AxisListType

P = 128
D = 1024
KT = D // P
CTX, LAT = 128, 512
T = CTX + LAT
TH = T // 2
PAST = 256
FF = 2816
FT = FF // P
NMOD = 9
EPS = 1e-6
SLOT = 11 * P
MLA_HEADS, NOPE, ROPE, MLA_V, Q_LORA = 8, 64, 32, 64, 256
MLA_QK = NOPE + ROPE
M_HEADS, M_DK, M_DV = 4, 64, 128
CHUNKS = T // P
S_HEADS, KV_HEADS, HEAD = 16, 4, 64
KEYS = CTX + PAST + LAT
NEG = -1e30
ROWS = 36
PM_GATES, PM_Q, PM_K, PM_V, PM_O = 0, 1, 3, 5, 9
GROUPS = ((0, CTX), (CTX, T))



def plan_stages():
    stages, first = {}, 0
    order = [("ada", 2 * 18 * 2, 8)]
    for f in range(4):
        if f == 1:
            order += [("even_in", 8, 8), ("even_out", 4, 8)]
        if f == 3:
            order += [("odd_in", 6, 8), ("odd_out", 4, 8)]
        order += [(f"gu{f}", FT, 8), (f"dn{f}", 8, 11)]
    for i, (name, blocks, tiles) in enumerate(order):
        stages[name] = dict(name=name, blocks=blocks, tiles=tiles, base=first,
                            next_tiles=order[i + 1][2] if i + 1 < len(order) else 0)
        first += 2 * blocks
    return stages


def attention_plan():
    mla, swa = [], []
    for h in range(MLA_HEADS):
        mla.append([("mla", h, -1, 0)])
        mla.append([("mla", h, n, n) for n in range(LAT // P)])
    for g in range(KV_HEADS):
        for n in range(-1, LAT // P):
            swa.append([("swa", g, n, i) for i in range(S_HEADS // KV_HEADS)])
    return mla, swa


def build(nc, io, upto=99):
    S = plan_stages()
    N_CHUNKS = max(s["base"] + 2 * s["blocks"] for s in S.values())
    with ExitStack() as ctx:
        def sb(name, shape, dt=F32):
            return ctx.enter_context(nc.sbuf_tensor(name, shape, dt))

        def sem(name):
            return ctx.enter_context(nc.semaphore(name))

        xT = sb("xT", [P, KT, T])
        w_raw = sb("w_raw", [P, 2, SLOT])
        w_hi = sb("w_hi", [P, 2, SLOT], F32R)
        w_lo = sb("w_lo", [P, 2, SLOT], F32R)
        ones = sb("ones", [P, P])
        eps_col = sb("eps_col", [P, 1])
        mods = sb("mods", [P, 2 * NMOD * KT, 2])
        rstd = sb("rstd", [P, T])
        small = sb("small", [P, 64])
        neg_sink = sb("neg_sink", [P, 2 * S_HEADS])
        gains = sb("gains", [P, 8])
        row_bias = sb("row_bias", [P, 3])
        m_in = sb("m_in", [P, 8])
        one_col = sb("one_col", [P, 1])
        ident = sb("ident", [P, P])
        causal = sb("causal", [P, 2, P])

        ps = ctx.enter_context(nc.psum_tensor("ps", [P, 8, 512], F32))

        with ExitStack() as scope:
            def asb(name, shape, dt=F32):
                return scope.enter_context(nc.sbuf_tensor(name, shape, dt))
            cond = asb("cond", [P, KT, 2])
            cond_silu = asb("cond_silu", [P, KT, 2])
            cond_hl = asb("cond_hl", [P, KT, P], F32R)
            mod_rows = asb("mod_rows", [P, 2, 512])
            pick = asb("pick", [P, 2])
            ada_bias = asb("ada_bias", [P, 2 * NMOD * KT, 2])
            norm_g = asb("norm_g", [P, 2, 6, KT])
        with ExitStack() as scope:
            def fsb(name, shape, dt=F32):
                return scope.enter_context(nc.sbuf_tensor(name, shape, dt))
            hx_hi = fsb("hx_hi", [P, KT, T], F32R)
            hx_lo = fsb("hx_lo", [P, KT, T], F32R)
            tmp = fsb("tmp", [P, 2, T])
            silu_g = tmp
            with ExitStack() as inner:
                hh_hi = inner.enter_context(nc.sbuf_tensor("hh_hi", [P, FT, T], F32R))
                hh_lo = inner.enter_context(nc.sbuf_tensor("hh_lo", [P, FT, T], F32R))
        with ExitStack() as scope:
            y = scope.enter_context(nc.sbuf_tensor("y", [P, KT, T], F32))
            sq = scope.enter_context(nc.sbuf_tensor("sq", [P, 2, T], F32))
            ssq = scope.enter_context(nc.sbuf_tensor("ssq", [P, T], F32))

        with ExitStack() as scope:
            def esb(name, shape, dt=F32, s=scope):
                return s.enter_context(nc.sbuf_tensor(name, shape, dt))
            for name in ("hx_hi_", "hx_lo_"):
                esb(name, [P, KT, T])
            esb("tmp_", [P, 2, T])
            with ExitStack() as res:
                y_m = esb("y_m", [P, KT, T], s=res)
                sq_m = esb("sq_m", [P, 2, T], s=res)
                ssq_m = esb("ssq_m", [P, T], s=res)
            with ExitStack() as even:
                pm = esb("pm", [P, 13, T], s=even)
                with ExitStack() as mla:
                    qh = esb("qh", [P, MLA_HEADS, T], s=mla)
                    kh = esb("kh", [P, MLA_HEADS, KEYS], s=mla)
                    vtok = esb("vtok", [P, KEYS // P, MLA_HEADS * MLA_V], s=mla)
                    with ExitStack() as part:
                        pa = esb("pa", [P, 3, T], s=part)
                        w_qb = esb("w_qb", [P, 2, MLA_HEADS * MLA_QK], s=part)
                        w_kvb = esb("w_kvb", [P, 2, MLA_HEADS * 64], s=part)
                        ckv_keys = esb("ckv_keys", [P, KEYS], s=part)
                    with ExitStack() as part:
                        prob_e = esb("prob_e", [P, 2, 768], s=part)
                        probT_e = esb("probT_e", [P, 6, 512], s=part)
                with ExitStack() as ml:
                    vaug = esb("vaug", [P, CHUNKS, M_HEADS, 2 * P], s=ml)
                    ktok = esb("ktok", [P, CHUNKS, M_HEADS * M_DK], s=ml)
                    onehot = esb("onehot", [P, 8, P], s=ml)
                    rows3 = esb("rows3", [P, 3, T], s=ml)
                    acol = esb("acol", [P, CHUNKS, ROWS], s=ml)
                    decay = esb("decay", [P, T], s=ml)
                    weigh = esb("weigh", [P, T], s=ml)
                    g_inter = esb("g_inter", [P, T], s=ml)
                    floor_m = esb("floor_m", [P, T], s=ml)
                    q_inter = esb("q_inter", [P, 2, T], s=ml)
                    k_w = esb("k_w", [P, CHUNKS, M_DK], s=ml)
                    state = esb("state", [P, 5, 2 * P], s=ml)
                    state0 = esb("state0", [P, 2, 2, 2 * P], s=ml)
                    state_out = esb("state_out", [P, 2, 2, 2 * P], s=ml)
                    with ExitStack() as early:
                        rows = esb("rows", [P, 6, T], s=early)
                    hm = esb("hm", [P, M_HEADS, T], s=ml)
                    hs = esb("hs", [P, T], s=ml)
            with ExitStack() as odd:
                po = esb("po", [P, 12, T], s=odd)
                v_new = esb("v_new", [P, CHUNKS, KV_HEADS * HEAD], s=odd)
                v_old = esb("v_old", [P, PAST // P, KV_HEADS * HEAD], s=odd)
                k_old = esb("k_old", [P, 2, PAST], s=odd)
                rope_o = esb("rope_o", [P, 2, LAT], s=odd)
                swap_o = esb("swap_o", [P, P], s=odd)
                turned = esb("turned", [P, 2, LAT], s=odd)
                prob_o = esb("prob_o", [P, 2, 768], s=odd)
                probT_o = esb("probT_o", [P, 6, 512], s=odd)
        with ExitStack() as scope:
            for name, shape in (("y_", [P, KT, T]), ("sq_", [P, 2, T]), ("ssq_", [P, T])):
                scope.enter_context(nc.sbuf_tensor(name, shape, F32))
            rope_e = scope.enter_context(nc.sbuf_tensor("rope_e", [P, 2, LAT], F32))
            swap_e = scope.enter_context(nc.sbuf_tensor("swap_e", [P, ROPE], F32))
            pick_rows = scope.enter_context(nc.sbuf_tensor("pick_rows", [P, 2, ROWS], F32))

        in_loaded = sem("in_loaded")
        const_ready = sem("const_ready")
        raw_ready = [sem("raw_ready0"), sem("raw_ready1")]
        hi_done, lo_done, w_used = sem("hi_done"), sem("lo_done"), sem("w_used")
        act_chain, dve_chain, y_scaled = sem("act_chain"), sem("dve_chain"), sem("y_scaled")
        cond_act, cond_ready = sem("cond_act"), sem("cond_ready")
        row_ready, col_ready, mod_added, mods_ready = sem("row_ready"), sem("col_ready"), sem("mod_added"), sem("mods_ready")
        silu_done, mul_done, hhi_done, block_free = sem("silu_done"), sem("mul_done"), sem("hhi_done"), sem("block_free")
        sq_ready, ssq_done = sem("sq_ready"), sem("ssq_done")
        msq_ready, rstd_ready = sem("msq_ready"), sem("rstd_ready")
        x_ready, xsq_ready, xsq_used = sem("x_ready"), sem("xsq_ready"), sem("xsq_used")
        pre_ready, hxhi_ready, hx_ready = sem("pre_ready"), sem("hxhi_ready"), sem("hx_ready")
        out_stored = sem("out_stored")
        proj_done = sem("proj_done")
        mix_loaded, mix_loaded2, mix_loaded3 = sem("mix_loaded"), sem("mix_loaded2"), sem("mix_loaded3")
        lora_sq, lora_sum, lora_rstd, lora_ready = sem("lora_sq"), sem("lora_sum"), sem("lora_rstd"), sem("lora_ready")
        built, built_act, built_dve = sem("built"), sem("built_act"), sem("built_dve")
        s_ready, negm_ready, p_ready, pn_ready = sem("s_ready"), sem("negm_ready"), sem("p_ready"), sem("pn_ready")
        pt_psum, pt_ready, o_ready, ohi_done, o_done = sem("pt_psum"), sem("pt_ready"), sem("o_ready"), sem("ohi_done"), sem("o_done")
        gate_act, gate_rows, rows_ready = sem("gate_act"), sem("gate_rows"), sem("rows_ready")
        turn_ready, turn_act, turn_dve = sem("turn_ready"), sem("turn_act"), sem("turn_dve")
        kq_ready, decay_arg, decay_ready = sem("kq_ready"), sem("decay_arg"), sem("decay_ready")
        weigh_ready, gain_ready, state_ready = sem("weigh_ready"), sem("gain_ready"), sem("state_ready")
        numden_ready, head_done = sem("numden_ready"), sem("head_done")
        hm_sq, hm_sum, hm_rstd, hm_f, hm_hi, mix_ready = (sem("hm_sq"), sem("hm_sum"), sem("hm_rstd"), sem("hm_f"),
                                                         sem("hm_hi"), sem("mix_ready"))
        odd_swap, odd_rope = sem("odd_swap"), sem("odd_rope")
        chained = {}
        CONSTS = 9 * 16
        N_OUT = 4 * (upto > 1) + (upto > 4)
        MLA_GROUPS, SWA_GROUPS = attention_plan()

        def link(eng, chain, ins):
            chained[chain.name] = chained.get(chain.name, 0) + 1
            ins.then_inc(chain, 1)
            eng.wait_ge(chain, chained[chain.name])

        ada_w, ffn_gu, ffn_dn = io["ada_w"], io["ffn_gu"], io["ffn_dn"]

        def bank_pair(i):
            return ps[:, 2 * i:2 * i + 2, 0:TH]

        def halves(tile):
            return tile.rearrange("p (n t) -> p n t", n=2)

        def split_hi(act, c, slot, tiles, wait_used=True):
            act.wait_ge(raw_ready[slot], (c // 2) * 16 + 16 if isinstance(c, int) else c * 8 + (16 - 8 * slot))
            if wait_used:
                act.wait_ge(w_used, c - 1)
            nc.scalar.copy(w_hi[:, slot, 0:tiles * P], w_raw[:, slot, 0:tiles * P]).then_inc(hi_done, 1)

        def split_lo(dve, c, slot, tiles, wait_used=True):
            dve.wait_ge(hi_done, c + 1)
            if wait_used:
                dve.wait_ge(w_used, c - 1)
            nc.vector.tensor_tensor(w_lo[:, slot, 0:tiles * P], w_raw[:, slot, 0:tiles * P],
                                    w_hi[:, slot, 0:tiles * P], ALU.subtract).then_inc(lo_done, 1)

        def mod_col(layer, idx, k, cond_i):
            j = (layer * NMOD + idx) * KT + k
            return mods[:, j, cond_i:cond_i + 1]

        SUBS = []
        for layer in range(2):
            SUBS += [dict(kind="ffn", f=2 * layer, layer=layer, idx=0), dict(kind="mix", layer=layer, idx=3),
                     dict(kind="ffn", f=2 * layer + 1, layer=layer, idx=6)]
        SUBS = SUBS[:upto]
        chunk0, gu0 = S["ada"]["blocks"] * 2, 0
        for s in SUBS:
            s.update(chunk=chunk0, gu0=gu0)
            s["tiles_in"] = {"ffn": FT, "mix": 8 if s["layer"] == 0 else 6}[s["kind"]]
            s["blocks_out"] = KT if s["kind"] == "ffn" else KT // 2
            chunk0 += 2 * (s["tiles_in"] + s["blocks_out"])
            gu0 += FT if s["kind"] == "ffn" else 0

        block = ctx.enter_context(nc.Block())

        BUILD = [("kr", 0), ("gi", 0), ("gf", 0)]
        for h in range(MLA_HEADS):
            BUILD += [("q", h), ("k", h)] + ([("sw", h - 1)] if h else [])
        BUILD += [("sw", MLA_HEADS - 1)] + [("v", j) for j in range(KEYS // P)]
        BY_ACT = ("q", "v", "gi", "gf")

        def evacuated(i):
            a = sum(kind in BY_ACT for kind, _ in BUILD[:i])
            return a, i - a

        QPOS = {h: BUILD.index(("q", h)) for h in range(MLA_HEADS)}

        def pair_flat(i):
            return ps[:, 2 * i:2 * i + 2, :].rearrange("p b c -> p (b c)")

        def unit_shape(unit):
            mixer, h, n, i = unit
            if n < 0:
                return 512 - P, 512, 1, (0, 1)
            if mixer == "mla":
                return 128, 896, 6, (0, 6)
            lo, hi = max(n - 1, 0), min(n + 2, LAT // P)
            return 512 - P * (hi - lo), 512 + PAST, hi - lo + 2, (lo, hi)

        def units_of(groups):
            return [(u, g, unit, unit[3] == len(group) - 1 or len(group) == 1)
                    for g, group in enumerate(groups) for u, unit in [(0, x) for x in group]]

        def numbered(layer):
            u = sum(len(g) for g in MLA_GROUPS) * layer
            g0 = len(MLA_GROUPS) * layer
            out = []
            for g, group in enumerate((MLA_GROUPS, SWA_GROUPS)[layer]):
                for j, unit in enumerate(group):
                    out.append((u, g0 + g, unit, len(group), j == len(group) - 1))
                    u += 1
            return out

        def seq_dir(i):
            return i // 2, i % 2

        def pe_attention(pe, layer):
            units = numbered(layer)
            probT = (probT_e, probT_o)[layer]
            prob = (prob_e, prob_o)[layer]
            n_units = len(units)

            def scores(u, g, unit, size, last):
                mixer, h, n, i = unit
                a, b, blocks, (lo, hi) = unit_shape(unit)
                if u >= 2:
                    pe.wait_ge(p_ready, u - 1)
                bank = 2 * (u % 2)
                if mixer == "mla":
                    q0 = 0 if n < 0 else CTX + n * P
                    query = qh[0:MLA_QK, h, q0:q0 + P]
                    parts = [kh[0:MLA_QK, h, 0:CTX]] if n < 0 else [kh[0:MLA_QK, h, CTX:CTX + 384],
                                                                    kh[0:MLA_QK, h, CTX + 384:KEYS]]
                else:
                    p, r = h // 2, 64 * (h % 2)
                    q0 = 0 if n < 0 else CTX + n * P
                    query = po[r:r + 64, 4 * p + i, q0:q0 + P]
                    parts = ([po[r:r + 64, 8 + p, 0:CTX]] if n < 0 else
                             [po[r:r + 64, 8 + p, CTX + lo * P:CTX + hi * P], k_old[r:r + 64, p, :]])
                w0 = 512 - a
                ins = nc.tensor.matmul(ps[:, bank, a:512], query, parts[0], start=True, stop=True)
                if len(parts) > 1:
                    ins = nc.tensor.matmul(ps[:, bank + 1, 0:b - 512], query, parts[1], start=True, stop=True)
                ins.then_inc(s_ready, 1)

            def turn(u, g, unit, size, last):
                blocks = unit_shape(unit)[2]
                pe.wait_ge(pn_ready, u + 1)
                if u >= 1:
                    pe.wait_ge(pt_ready, u)
                flat = pair_flat(2)
                for j in range(blocks):
                    ins = nc.tensor.transpose(flat[:, j * P:(j + 1) * P], prob[:, u % 2, j * P:(j + 1) * P], ident[:])
                ins.then_inc(pt_psum, 1)

            def values(u, g, unit, size, last):
                mixer, h, n, i = unit
                _, _, blocks, (lo, hi) = unit_shape(unit)
                pe.wait_ge(pt_ready, u + 1)
                if g >= 2:
                    pe.wait_ge(o_done, g - 1)
                r = 64 * (h % 2)
                for j in range(blocks):
                    if mixer == "mla":
                        v = vtok[:, 0 if n < 0 else 1 + j, h * MLA_V:(h + 1) * MLA_V]
                    elif n < 0:
                        v = v_new[:, 0, h * HEAD:(h + 1) * HEAD]
                    elif j < hi - lo:
                        v = v_new[:, 1 + lo + j, h * HEAD:(h + 1) * HEAD]
                    else:
                        v = v_old[:, j - (hi - lo), h * HEAD:(h + 1) * HEAD]
                    ins = nc.tensor.matmul(ps[r:r + 64, 6 + g % 2, 0:size * P], v, probT[:, j, 0:size * P],
                                           start=(j == 0), stop=(j == blocks - 1))
                ins.then_inc(o_ready, 1)
            for t in range(n_units + 2):
                if t < n_units:
                    scores(*units[t])
                if 1 <= t <= n_units:
                    turn(*units[t - 1])
                if t >= 2 and units[t - 2][4]:
                    values(*units[t - 2])

        def act_attention(act, layer):
            units = numbered(layer)
            scale = (MLA_QK ** -0.5, HEAD ** -0.5)[layer]
            prob, probT = (prob_e, prob_o)[layer], (probT_e, probT_o)[layer]
            n_units = len(units)
            for t in range(n_units + 3):
                if t < n_units:
                    u, g, unit, size, last = units[t]
                    a, b, blocks, _ = unit_shape(unit)
                    act.wait_ge(negm_ready, u + 1)
                    if u >= 2:
                        act.wait_ge(pt_psum, u - 1)
                    c = u % 2
                    ins = nc.scalar.activation(prob[:, c, 0:b - a], pair_flat(c)[:, a:b], ACT.Exp,
                                               bias=small[:, c:c + 1], scale=scale, accum_out=small[:, 2 + c:3 + c])
                    if layer == 1:
                        head = 4 * unit[1] + unit[3]
                        ins = nc.scalar.activation(small[:, 6 + c:7 + c], small[:, c:c + 1], ACT.Exp,
                                                   bias=neg_sink[:, head:head + 1])
                    ins.then_inc(p_ready, 1)
                if 1 <= t <= n_units:
                    u, g, unit, size, last = units[t - 1]
                    blocks, i = unit_shape(unit)[2], (unit[3] if size > 1 else 0)
                    act.wait_ge(pt_psum, u + 1)
                    if i == 0 and g >= 1:
                        act.wait_ge(o_ready, g)
                    nc.scalar.copy(probT[:, 0:blocks, i * P:(i + 1) * P],
                                   pair_flat(2)[:, 0:blocks * P].rearrange("p (j q) -> p j q", q=P)).then_inc(pt_ready, 1)
                if t >= 3 and units[t - 3][4]:
                    u, g, unit, size, last = units[t - 3]
                    act.wait_ge(o_ready, g + 1)
                    dst, src = mixed(hx_hi, unit, g, size)
                    nc.scalar.copy(dst, src).then_inc(ohi_done, 1)

        def mixed(buf, unit, g, size):
            mixer, h, n, i = unit
            r = 64 * (h % 2)
            src = ps[r:r + 64, 6 + g % 2, 0:size * P]
            if mixer == "mla":
                return (buf[r:r + 64, h // 2, 0:CTX] if n < 0 else buf[r:r + 64, h // 2, CTX:T]), src
            c0 = 0 if n < 0 else CTX + n * P
            return buf[r:r + 64, 4 * (h // 2):4 * (h // 2) + 4, c0:c0 + P], src.rearrange("p (i q) -> p i q", q=P)

        def dve_attention(dve, layer):
            units = numbered(layer)
            scale = (MLA_QK ** -0.5, HEAD ** -0.5)[layer]
            prob = (prob_e, prob_o)[layer]
            n_units = len(units)
            for t in range(n_units + 3):
                if t < n_units:
                    u, g, unit, size, last = units[t]
                    a, b, blocks, (lo, hi) = unit_shape(unit)
                    c = u % 2
                    flat = pair_flat(c)
                    dve.wait_ge(s_ready, u + 1)
                    if layer == 1 and unit[2] >= 0:
                        n = unit[2]
                        ins = None
                        if lo < n:
                            ins = nc.vector.tensor_tensor(flat[:, a:a + P], flat[:, a:a + P], causal[:, 0, :], ALU.add)
                        if hi > n + 1:
                            e = 512 - P
                            ins = nc.vector.tensor_tensor(flat[:, e:e + P], flat[:, e:e + P], causal[:, 1, :], ALU.add)
                        link(dve, dve_chain, ins)
                    link(dve, dve_chain, nc.vector.tensor_reduce(small[:, 8 + c:9 + c], flat[:, a:b], AX.X, ALU.max))
                    if layer == 0:
                        ins = nc.vector.tensor_scalar(small[:, c:c + 1], small[:, 8 + c:9 + c], -scale, None, ALU.mult)
                    else:
                        head = S_HEADS + 4 * unit[1] + unit[3]
                        ins = nc.vector.tensor_scalar(small[:, c:c + 1], small[:, 8 + c:9 + c], -scale,
                                                      neg_sink[:, head:head + 1], ALU.mult, ALU.min)
                    ins.then_inc(negm_ready, 1)
                if 1 <= t <= n_units:
                    u, g, unit, size, last = units[t - 1]
                    a, b, blocks, _ = unit_shape(unit)
                    c = u % 2
                    dve.wait_ge(p_ready, u + 1)
                    if layer == 1:
                        link(dve, dve_chain, nc.vector.tensor_tensor(small[:, 2 + c:3 + c], small[:, 2 + c:3 + c],
                                                                     small[:, 6 + c:7 + c], ALU.add))
                    link(dve, dve_chain, nc.vector.reciprocal(small[:, 4 + c:5 + c], small[:, 2 + c:3 + c]))
                    nc.vector.tensor_scalar(prob[:, c, 0:b - a], prob[:, c, 0:b - a], small[:, 4 + c:5 + c], None,
                                            ALU.mult).then_inc(pn_ready, 1)
                if t >= 3 and units[t - 3][4]:
                    u, g, unit, size, last = units[t - 3]
                    dve.wait_ge(ohi_done, g + 1)
                    dst, src = mixed(hx_lo, unit, g, size)
                    hi_part, _ = mixed(hx_hi, unit, g, size)
                    nc.vector.tensor_tensor(dst, src, hi_part.bitcast(F32), ALU.subtract).then_inc(o_done, 1)

        def pe_mixer(pe, s):
            if s["layer"] == 1:
                pe.wait_ge(mix_loaded, 16 * (11 + 4))
                for t in range(10):
                    if t >= 4:
                        pe.wait_ge(odd_rope, t - 3)
                    nc.tensor.matmul(ps[:, 4 + t % 4, :], swap_o[:], po[:, t, CTX:T], start=True,
                                     stop=True).then_inc(odd_swap, 1)
                for c in range(CHUNKS):
                    if c >= 4:
                        pe.wait_ge(odd_rope, 10 + c - 3)
                    for j in range(2):
                        ins = nc.tensor.transpose(ps[:, c % 4, j * P:(j + 1) * P], po[:, 10 + j, c * P:(c + 1) * P], ident[:])
                    ins.then_inc(odd_swap, 1)
                pe.wait_ge(odd_rope, 10 + CHUNKS)
                pe_attention(pe, 1)
                pe.wait_ge(o_done, len(MLA_GROUPS) + len(SWA_GROUPS))
                return
            pe.wait_ge(lora_sq, 3)
            for j, (bank, first, last) in enumerate(((0, True, False), (0, False, True), (2, True, True))):
                for h in range(2):
                    ins = nc.tensor.matmul(ps[:, bank + h, 0:TH], ones[:], y[:, j, h * TH:(h + 1) * TH],
                                           start=first, stop=last)
            ins.then_inc(lora_sum, 1)
            pe.wait_ge(mix_loaded, 16 * 11)
            pe.wait_ge(mix_loaded2, 16 * 3)
            pe.wait_ge(lora_ready, 3)
            for i, (kind, h) in enumerate(BUILD):
                pair = i % 4
                if i >= 4:
                    a, d = evacuated(i - 3)
                    pe.wait_ge(built_act, a)
                    pe.wait_ge(built_dve, d)
                if kind == "kr":
                    ins = nc.tensor.matmul(ps[NOPE:MLA_QK, 2 * pair, :], swap_e[NOPE:MLA_QK, :],
                                           pm[NOPE:MLA_QK, PM_GATES, CTX:T], start=True, stop=True)
                elif kind in ("gi", "gf"):
                    for n in range(2):
                        ins = nc.tensor.matmul(ps[0:ROWS, 2 * pair + n, 0:TH], pick_rows[0:32, int(kind == "gf"), :],
                                               pm[0:32, PM_GATES, n * TH:(n + 1) * TH], start=True, stop=True)
                elif kind == "q":
                    for n in range(2):
                        for k in range(2):
                            ins = nc.tensor.matmul(ps[0:MLA_QK, 2 * pair + n, 0:TH],
                                                   w_qb[:, k, h * MLA_QK:(h + 1) * MLA_QK],
                                                   pa[:, k, n * TH:(n + 1) * TH], start=(k == 0), stop=(k == 1))
                elif kind == "k":
                    for n in range(2):
                        ins = nc.tensor.matmul(ps[0:NOPE, 2 * pair + n, 0:KEYS // 2], w_kvb[:, 0, h * 64:(h + 1) * 64],
                                               ckv_keys[:, n * (KEYS // 2):(n + 1) * (KEYS // 2)], start=True, stop=True)
                elif kind == "sw":
                    pe.wait_ge(built_act, evacuated(QPOS[h] + 1)[0])
                    ins = nc.tensor.matmul(ps[NOPE:MLA_QK, 2 * pair, :], swap_e[NOPE:MLA_QK, :],
                                           qh[NOPE:MLA_QK, h, CTX:T], start=True, stop=True)
                else:
                    ins = nc.tensor.matmul(ps[:, 2 * pair, :], ckv_keys[:, h * P:(h + 1) * P], w_kvb[:, 1, :],
                                           start=True, stop=True)
                ins.then_inc(built, 1)
            a, d = evacuated(len(BUILD))
            pe.wait_ge(built_act, a)
            pe.wait_ge(built_dve, d)
            pe_attention(pe, 0)
            pe.wait_ge(o_done, len(MLA_GROUPS))
            for c in range(CHUNKS):
                if c >= 4:
                    pe.wait_ge(turn_act, 2 * (c - 3))
                pair = 2 * (c % 4)
                for j in range(2):
                    ins = nc.tensor.transpose(ps[:, pair, j * P:(j + 1) * P], pm[:, PM_K + j, c * P:(c + 1) * P], ident[:])
                for j in range(M_HEADS):
                    ins = nc.tensor.transpose(ps[:, pair + 1, j * P:(j + 1) * P], pm[:, PM_V + j, c * P:(c + 1) * P], ident[:])
                ins.then_inc(turn_ready, 1)
            pe.wait_ge(turn_act, 2 * CHUNKS)
            pe.wait_ge(rows_ready, 1)
            for c in range(CHUNKS):
                ins = nc.tensor.transpose(ps[:, 0, c * ROWS:(c + 1) * ROWS], rows[0:ROWS, 1, c * P:(c + 1) * P],
                                          ident[0:ROWS, 0:ROWS])
            ins.then_inc(turn_ready, 1)
            pe.wait_ge(turn_act, 2 * CHUNKS + 1)
            pe.wait_ge(mix_loaded3, 32)
            for i in range(2 * M_HEADS):
                h, d = seq_dir(i)
                r = 64 * (h % 2)
                if i >= 1:
                    pe.wait_ge(head_done, i)
                for j, pair in ((0, 0), (1, 2), (2, 3)):
                    flat = pair_flat(pair)
                    for a, b in ((0, 512), (512, T)):
                        ins = nc.tensor.matmul(flat[:, a:b], onehot[0:ROWS, 4 * d + h, :], rows3[0:ROWS, j, a:b],
                                               start=True, stop=True)
                flat = pair_flat(1)
                for c in range(CHUNKS):
                    ins = nc.tensor.matmul(flat[:, c * P:(c + 1) * P], pm[r:r + 64, PM_K + h // 2, c * P:(c + 1) * P],
                                           pm[r:r + 64, PM_Q + h // 2, c * P:(c + 1) * P], start=True, stop=True)
                ins.then_inc(kq_ready, 1)
                pe.wait_ge(weigh_ready, i + 1)
                for j, c in enumerate((0, 1, 2, 3) if d == 0 else (0, 4, 3, 2)):
                    ins = nc.tensor.matmul(pair_flat(2)[r:r + 64, j * 2 * P:(j + 1) * 2 * P], k_w[:, c, :],
                                           vaug[:, c, h, :], start=True, stop=True)
                ins.then_inc(gain_ready, 1)
                pe.wait_ge(state_ready, i + 1)
                for c in range(CHUNKS):
                    cols = slice(c * P, (c + 1) * P)
                    for pair, vs, st in ((0, vaug[:, c, h, 0:P], state[:, c, 0:P]), (1, vaug[:, c, h, P:], state[:, c, P:])):
                        nc.tensor.matmul(pair_flat(pair)[:, cols], vs, weigh[:, cols], start=True, stop=(c == 0))
                        if c > 0:
                            ins = nc.tensor.matmul(pair_flat(pair)[:, cols], st, q_inter[:, h % 2, cols], start=False,
                                                   stop=True)
                ins.then_inc(numden_ready, 1)
            pe.wait_ge(head_done, 2 * M_HEADS)
            for h in range(M_HEADS):
                pe.wait_ge(hm_sq, h + 1)
                for n in range(2):
                    ins = nc.tensor.matmul(ps[:, 2 * h + n, 0:TH], ones[:],
                                           (decay, weigh, g_inter, floor_m)[h][:, n * TH:(n + 1) * TH],
                                           start=True, stop=True)
                ins.then_inc(hm_sum, 1)
            pe.wait_ge(mix_ready, M_HEADS)

        def act_mixer(act, s):
            if s["layer"] == 1:
                for c in range(CHUNKS):
                    act.wait_ge(odd_swap, 10 + c + 1)
                    act.wait_ge(odd_rope, 10 + c)
                    nc.scalar.copy(v_new[:, c, :], ps[:, c % 4, 0:2 * P]).then_inc(odd_rope, 1)
                act_attention(act, 1)
                return
            act.wait_ge(proj_done, 16)
            for j in range(3):
                nc.scalar.activation(y[:, j, :], pa[:, j, :], ACT.Square).then_inc(lora_sq, 1)
            act.wait_ge(lora_sum, 1)
            link(act, act_chain, nc.scalar.activation(halves(y[:, 3, :]), bank_pair(0), ACT.Ln, bias=eps_col[:, 0:1],
                                                      scale=1.0 / Q_LORA))
            link(act, act_chain, nc.scalar.activation(halves(y[:, 4, :]), bank_pair(1), ACT.Ln, bias=eps_col[:, 0:1],
                                                      scale=1.0 / P))
            nc.scalar.activation(y[:, 3:5, :], y[:, 3:5, :], ACT.Exp, scale=-0.5).then_inc(lora_rstd, 1)
            for i, (kind, h) in enumerate(BUILD):
                if kind not in BY_ACT:
                    continue
                act.wait_ge(built, i + 1)
                pair = i % 4
                if kind in ("gi", "gf"):
                    j = int(kind == "gf")
                    ins = nc.scalar.copy(halves(tmp[0:ROWS, j, :]), ps[0:ROWS, 2 * pair:2 * pair + 2, 0:TH])
                elif kind == "q":
                    ins = nc.scalar.copy(halves(qh[0:MLA_QK, h, :]), ps[0:MLA_QK, 2 * pair:2 * pair + 2, 0:TH])
                else:
                    ins = nc.scalar.copy(vtok[:, h, :], ps[:, 2 * pair, :])
                ins.then_inc(built_act, 1)
            act.wait_ge(out_stored, 32)
            act_attention(act, 0)
            act.wait_ge(o_done, len(MLA_GROUPS))
            act.wait_ge(gate_rows, 1)
            link(act, act_chain, nc.scalar.activation(rows[0:ROWS, 5, :], rows[0:ROWS, 4, :], ACT.Abs))
            link(act, act_chain, nc.scalar.activation(rows[0:ROWS, 5, :], rows[0:ROWS, 5, :], ACT.Exp, scale=-1.0))
            nc.scalar.activation(rows[0:ROWS, 5, :], rows[0:ROWS, 5, :], ACT.Ln, bias=one_col[0:ROWS, 0:1]).then_inc(gate_act, 1)
            for c in range(CHUNKS):
                act.wait_ge(turn_ready, c + 1)
                pair = 2 * (c % 4)
                nc.scalar.copy(ktok[:, c, :], ps[:, pair, 0:2 * P]).then_inc(turn_act, 1)
                nc.scalar.copy(vaug[:, c, :, 0:P], ps[:, pair + 1, :].rearrange("p (h v) -> p h v", v=P)).then_inc(turn_act, 1)
            act.wait_ge(turn_ready, CHUNKS + 1)
            nc.scalar.copy(acol[:].rearrange("p c r -> p (c r)"), ps[:, 0, 0:CHUNKS * ROWS]).then_inc(turn_act, 1)
            for i in range(2 * M_HEADS):
                act.wait_ge(kq_ready, i + 1)
                if i >= 1:
                    act.wait_ge(head_done, i)
                nc.scalar.activation(g_inter[:], pair_flat(2)[:, 0:T], ACT.Exp)
                nc.scalar.activation(floor_m[:], pair_flat(3)[:, 0:T], ACT.Exp).then_inc(gate_act, 1)
                act.wait_ge(decay_arg, i + 1)
                nc.scalar.activation(decay[:], decay[:], ACT.Exp).then_inc(decay_ready, 1)
            act.wait_ge(head_done, 2 * M_HEADS)
            for h in range(M_HEADS):
                nc.scalar.activation((decay, weigh, g_inter, floor_m)[h][:], hm[:, h, :], ACT.Square).then_inc(hm_sq, 1)
            for h in range(M_HEADS):
                act.wait_ge(hm_sum, h + 1)
                out = (decay, weigh, g_inter, floor_m)[h][:]
                link(act, act_chain, nc.scalar.activation(halves(out), bank_pair(h), ACT.Ln, bias=eps_col[:, 0:1],
                                                          scale=1.0 / M_DV))
                nc.scalar.activation(out, out, ACT.Exp, scale=-0.5).then_inc(hm_rstd, 1)
            for h in range(M_HEADS):
                act.wait_ge(hm_f, h + 1)
                nc.scalar.copy(hx_hi[:, 4 + h, :], hm[:, h, :]).then_inc(hm_hi, 1)

        def dve_mixer(dve, s):
            if s["layer"] == 1:
                dve.wait_ge(proj_done, 16 + 12)
                dve.wait_ge(mix_loaded, 16 * (11 + 4))
                for t in range(10):
                    dve.wait_ge(odd_swap, t + 1)
                    nc.vector.tensor_tensor(turned[:, t % 2, :], ps[:, 4 + t % 4, :], rope_o[:, 1, :], ALU.mult)
                    link(dve, dve_chain, nc.vector.tensor_tensor(po[:, t, CTX:T], po[:, t, CTX:T], rope_o[:, 0, :], ALU.mult))
                    nc.vector.tensor_tensor(po[:, t, CTX:T], po[:, t, CTX:T], turned[:, t % 2, :],
                                            ALU.add).then_inc(odd_rope, 1)
                dve_attention(dve, 1)
                return
            dve.wait_ge(lora_rstd, 1)
            for j in range(2):
                nc.vector.scalar_tensor_tensor(out=pa[:, j, :], in0=pa[:, j, :], scalar=gains[:, j:j + 1],
                                               in1=y[:, 3, :], op0=ALU.mult, op1=ALU.mult).then_inc(lora_ready, 1)
            nc.vector.scalar_tensor_tensor(out=ckv_keys[:, 0:CTX], in0=pa[:, 2, 0:CTX], scalar=gains[:, 2:3],
                                           in1=y[:, 4, 0:CTX], op0=ALU.mult, op1=ALU.mult)
            nc.vector.scalar_tensor_tensor(out=ckv_keys[:, CTX + PAST:KEYS], in0=pa[:, 2, CTX:T], scalar=gains[:, 2:3],
                                           in1=y[:, 4, CTX:T], op0=ALU.mult, op1=ALU.mult).then_inc(lora_ready, 1)
            dve.wait_ge(mix_loaded2, 48)
            rr = slice(NOPE, MLA_QK)

            def rotate(x, swapped, scratch):
                nc.vector.tensor_tensor(y[rr, scratch, 0:LAT], swapped, rope_e[rr, 1, :], ALU.mult)
                link(dve, dve_chain, nc.vector.tensor_tensor(x, x, rope_e[rr, 0, :], ALU.mult))
                return nc.vector.tensor_tensor(x, x, y[rr, scratch, 0:LAT], ALU.add)
            for i, (kind, h) in enumerate(BUILD):
                if kind in BY_ACT:
                    continue
                dve.wait_ge(built, i + 1)
                pair = i % 4
                if kind == "kr":
                    link(dve, dve_chain, rotate(pm[rr, PM_GATES, CTX:T], ps[rr, 2 * pair, :], 0))
                    for hh in range(MLA_HEADS):
                        nc.vector.tensor_copy(kh[rr, hh, 0:CTX], pm[rr, PM_GATES, 0:CTX])
                        ins = nc.vector.tensor_copy(kh[rr, hh, CTX + PAST:KEYS], pm[rr, PM_GATES, CTX:T])
                elif kind == "k":
                    ins = nc.vector.tensor_copy(kh[0:NOPE, h, :].rearrange("p (n t) -> p n t", n=2),
                                                ps[0:NOPE, 2 * pair:2 * pair + 2, 0:KEYS // 2])
                else:
                    ins = rotate(qh[rr, h, CTX:T], ps[rr, 2 * pair, :], 1 + h % 2)
                ins.then_inc(built_dve, 1)
            dve_attention(dve, 0)
            dve.wait_ge(o_done, len(MLA_GROUPS))
            R = slice(0, ROWS)
            B, A, M, G, F, SCR = range(6)
            nc.vector.tensor_scalar(rows[R, F, :], tmp[R, 1, :], row_bias[R, 1:2], None, ALU.add).then_inc(gate_rows, 1)
            link(dve, dve_chain, nc.vector.tensor_scalar(rows[R, A, :], tmp[R, 0, :], row_bias[R, 0:1], None, ALU.add))
            nc.vector.memset(vaug[:, :, :, P:], 1.0)
            nc.vector.memset(q_inter[:], 0.0)
            nc.vector.memset(m_in[:], 0.0)
            nc.vector.memset(rows[R, B, :], 0.0)
            nc.vector.memset(rows[R, M, :], 0.0)
            nc.vector.memset(state[:], 0.0)
            dve.wait_ge(gate_act, 1)
            link(dve, dve_chain, nc.vector.scalar_tensor_tensor(out=rows[R, F, :], in0=rows[R, F, :], scalar=0.0,
                                                                in1=rows[R, SCR, :], op0=ALU.min, op1=ALU.subtract))

            def seen(row, d, c):
                if d == 0:
                    return rows[0:M_HEADS, row, c * P:(c + 1) * P], rows[0:M_HEADS, row, (c + 1) * P - 1:(c + 1) * P]
                part = rows[32:32 + M_HEADS, row, c * P:(c + 1) * P]
                return part[:, ::-1], rows[32:32 + M_HEADS, row, c * P:c * P + 1]
            for d in range(2):
                for c in range(CHUNKS):
                    f = seen(F, d, c)[0]
                    ins = nc.vector.tensor_tensor_scan(out=seen(B, d, c)[0], data0=f, data1=seen(M, d, c)[0],
                                                       initial=0.0, op0=ALU.add, op1=ALU.add)
            link(dve, dve_chain, ins)
            nc.vector.tensor_tensor(rows[R, A, :], rows[R, A, :], rows[R, B, :], ALU.subtract)
            nc.vector.tensor_copy(m_in[0:M_HEADS, 1:2], row_bias[0:M_HEADS, 2:3])
            link(dve, dve_chain, nc.vector.tensor_copy(m_in[32:32 + M_HEADS, 4:5], row_bias[32:32 + M_HEADS, 2:3]))
            for step in range(5):
                for d, order in ((0, (1, 2, 3, 4, 0)), (1, (4, 3, 2, 1, 0))):
                    c = order[step]
                    r = slice(32 * d, 32 * d + M_HEADS)
                    a = seen(A, d, c)[0]
                    ins = nc.vector.tensor_tensor_scan(out=seen(M, d, c)[0], data0=a, data1=a,
                                                       initial=m_in[r, c:c + 1], op0=ALU.max, op1=ALU.max)
                link(dve, dve_chain, ins)
                for d, order in ((0, (2, 3, 4, 7, 6)), (1, (3, 2, 1, 7, 6))):
                    c = ((1, 2, 3, 4, 0), (4, 3, 2, 1, 0))[d][step]
                    to = order[step]
                    r = slice(32 * d, 32 * d + M_HEADS)
                    ins = nc.vector.tensor_tensor(m_in[r, to:to + 1], seen(B, d, c)[1], seen(M, d, c)[1], ALU.add)
                link(dve, dve_chain, ins)
            nc.vector.tensor_scalar(rows3[R, 0, :], rows[R, M, :], -1.0, None, ALU.mult)
            for c in range(CHUNKS):
                nc.vector.tensor_scalar(rows3[R, 1, c * P:(c + 1) * P], rows[R, M, c * P:(c + 1) * P], -1.0,
                                        m_in[R, c:c + 1], ALU.mult, ALU.add)
            nc.vector.scalar_tensor_tensor(out=rows3[R, 2, :], in0=rows[R, B, :], scalar=-1.0, in1=rows[R, M, :],
                                           op0=ALU.mult, op1=ALU.subtract).then_inc(rows_ready, 1)
            dve.wait_ge(turn_act, 2 * CHUNKS + 1)
            dve.wait_ge(mix_loaded3, 32)
            for i in range(2 * M_HEADS):
                h, d = seq_dir(i)
                r = 64 * (h % 2)
                rs = slice(r, r + 64)
                row = 32 * d + h
                dve.wait_ge(kq_ready, i + 1)
                for c in range(CHUNKS):
                    cols = slice(c * P, (c + 1) * P)
                    ins = nc.vector.scalar_tensor_tensor(out=decay[:, cols], in0=pair_flat(0)[:, cols],
                                                         scalar=acol[:, c, row:row + 1], in1=causal[:, d, :],
                                                         op0=ALU.add, op1=ALU.add)
                ins.then_inc(decay_arg, 1)
                dve.wait_ge(gate_act, 1 + i + 1)
                nc.vector.tensor_tensor(q_inter[rs, h % 2, :], pm[rs, PM_Q + h // 2, :], g_inter[rs, :], ALU.mult)
                dve.wait_ge(decay_ready, i + 1)
                nc.vector.scalar_tensor_tensor(out=weigh[:], in0=pair_flat(1)[:, 0:T], scalar=M_DK ** -0.5,
                                               in1=decay[:], op0=ALU.mult, op1=ALU.mult)
                for c in range(CHUNKS):
                    last = (c + 1) * P - 1 if d == 0 else c * P
                    ins = nc.vector.tensor_scalar(k_w[:, c, :], ktok[:, c, h * M_DK:(h + 1) * M_DK],
                                                  decay[:, last:last + 1], M_DK ** -0.5, ALU.mult, ALU.mult)
                ins.then_inc(weigh_ready, 1)
                order = (1, 2, 3, 4) if d == 0 else (4, 3, 2, 1)
                nc.vector.tensor_copy(state[rs, order[0], :], state0[rs, d, h // 2, :]).then_inc(dve_chain, 1)
                chained[dve_chain.name] += 1
                dve.wait_ge(dve_chain, chained[dve_chain.name])
                dve.wait_ge(gain_ready, i + 1)
                nc.vector.tensor_copy(state_out[rs, d, h // 2, :], pair_flat(2)[rs, 0:2 * P])
                for j in range(3):
                    c, nxt = order[j], order[j + 1]
                    last = (c + 1) * P - 1 if d == 0 else c * P
                    ins = nc.vector.scalar_tensor_tensor(out=state[rs, nxt, :], in0=state[rs, c, :],
                                                         scalar=g_inter[rs, last:last + 1],
                                                         in1=pair_flat(2)[rs, (j + 1) * 2 * P:(j + 2) * 2 * P],
                                                         op0=ALU.mult, op1=ALU.add)
                    if j < 2:
                        link(dve, dve_chain, ins)
                ins.then_inc(state_ready, 1)
                dve.wait_ge(numden_ready, i + 1)
                link(dve, dve_chain, nc.vector.tensor_tensor(hs[:], pair_flat(1)[:, 0:T], floor_m[:], ALU.max))
                link(dve, dve_chain, nc.vector.scalar_tensor_tensor(out=hs[:], in0=pair_flat(1)[:, 0:T], scalar=-1.0,
                                                                    in1=hs[:], op0=ALU.mult, op1=ALU.max))
                link(dve, dve_chain, nc.vector.reciprocal(hs[:], hs[:]))
                if d == 0:
                    nc.vector.tensor_tensor(hm[:, h, :], pair_flat(0)[:, 0:T], hs[:], ALU.mult).then_inc(head_done, 1)
                else:
                    link(dve, dve_chain, nc.vector.tensor_tensor(hs[:], pair_flat(0)[:, 0:T], hs[:], ALU.mult))
                    nc.vector.tensor_tensor(hm[:, h, :], hm[:, h, :], hs[:], ALU.add).then_inc(head_done, 1)
            for h in range(M_HEADS):
                dve.wait_ge(hm_rstd, h + 1)
                link(dve, dve_chain, nc.vector.scalar_tensor_tensor(
                    out=hm[:, h, :], in0=hm[:, h, :], scalar=gains[:, 3 + h:4 + h],
                    in1=(decay, weigh, g_inter, floor_m)[h][:], op0=ALU.mult, op1=ALU.mult))
                nc.vector.tensor_tensor(hm[:, h, :], hm[:, h, :], pm[:, PM_O + h, :], ALU.mult).then_inc(hm_f, 1)
            for h in range(M_HEADS):
                dve.wait_ge(hm_hi, h + 1)
                nc.vector.tensor_tensor(hx_lo[:, 4 + h, :], hm[:, h, :], hx_hi[:, 4 + h, :].bitcast(F32),
                                        ALU.subtract).then_inc(mix_ready, 1)

        def sp_mixer_loads(sp, s):
            sp.wait_ge(w_used, s["chunk"])
            if s["layer"] == 0:
                sp.dma_start(w_qb[:], io["w_qb"]).then_inc(mix_loaded, 16)
                sp.dma_start(w_kvb[:], io["w_kvb"]).then_inc(mix_loaded, 16)
                sp.dma_start(ckv_keys[:, CTX:CTX + PAST], io["ckv_old"]).then_inc(mix_loaded, 16)
                for h in range(MLA_HEADS):
                    sp.dma_start(kh[NOPE:MLA_QK, h, CTX:CTX + PAST], io["krope_old"]).then_inc(mix_loaded, 16)
            else:
                for dst, name in ((v_old, "v_old"), (k_old, "k_old"), (rope_o, "rope_o"), (swap_o, "swap_o")):
                    sp.dma_start(dst[:], io[name]).then_inc(mix_loaded, 16)

        def sp_mixer_loads2(sp, s):
            sp.wait_ge(w_used, s["chunk"] + 2 * s["tiles_in"])
            if s["layer"] == 0:
                for dst, name in ((rope_e, "rope_e"), (swap_e, "swap_e"), (pick_rows, "pick_rows")):
                    sp.dma_start(dst[:], io[name]).then_inc(mix_loaded2, 16)
                sp.wait_ge(lora_ready, 3)
                sp.dma_start(io["out_ckv"], ckv_keys[:, 0:CTX]).then_inc(out_stored, 16)
                sp.dma_start(io["out_krope"], pm[NOPE:MLA_QK, PM_GATES, 0:CTX]).then_inc(out_stored, 16)
                sp.wait_ge(o_done, len(MLA_GROUPS))
                sp.dma_start(onehot[0:ROWS], io["onehot"]).then_inc(mix_loaded3, 16)
                sp.dma_start(state0[:], io["state0"]).then_inc(mix_loaded3, 16)
                sp.wait_ge(head_done, 8)
                sp.dma_start(io["out_state"], state_out[:]).then_inc(out_stored, 16)
                sp.dma_start(io["out_m"], m_in[0:ROWS, 6:7]).then_inc(out_stored, 16)
            else:
                sp.wait_ge(proj_done, 16 + 12)
                sp.dma_start(io["out_kv"], po[:, 8:12, 0:CTX]).then_inc(out_stored, 16)

        @block.sync
        def _(sp):
            for dst, name in ((cond, "cond"), (norm_g, "norm_g"), (ada_bias, "ada_b"), (pick, "pick"),
                              (neg_sink[:, 0:S_HEADS], "sinks"), (gains, "gains"), (row_bias, "row_bias"), (ident, "ident"),
                              (causal, "causal")):
                sp.dma_start(dst if name == "sinks" else dst[:], io[name]).then_inc(in_loaded, 16)

            def load(c, slot, src, tiles, wait=True):
                if wait:
                    sp.wait_ge(lo_done, c - 1)
                sp.dma_start(w_raw[:, slot, 0:tiles * P], src).then_inc(raw_ready[slot], 16)

            st = S["ada"]
            for q in range(2):
                load(q, q, ada_w[q], 8, wait=False)
            with sp.Fori(1, st["blocks"]) as b:
                for q in range(2):
                    load(2 * b + q, q, ada_w[2 * b + q], 8)
            for k in range(KT):
                sp.dma_start(xT[:, k, :], io["x"][:, k, :]).then_inc(in_loaded, 16)
            chunk = st["blocks"] * 2
            for s in SUBS:
                if s["kind"] == "ffn":
                    f = s["f"]
                    with sp.Fori(0, FT) as b:
                        for q in range(2):
                            load(2 * b + (chunk + q), q, ffn_gu[f, b, q], 8)
                    chunk += 2 * FT
                    with sp.Fori(0, KT) as b:
                        for q in range(2):
                            load(2 * b + (chunk + q), q, ffn_dn[f, b, q], 11)
                    chunk += 2 * KT
                else:
                    name = ("even", "odd")[s["layer"]]
                    sp_mixer_loads(sp, s)
                    with sp.Fori(0, s["tiles_in"]) as b:
                        for q in range(2):
                            load(2 * b + (chunk + q), q, io[name + "_in"][2 * b + q], 8)
                    chunk += 2 * s["tiles_in"]
                    for q in range(2):
                        load(chunk + q, q, io[name + "_out"][q], 8)
                    sp_mixer_loads2(sp, s)
                    with sp.Fori(1, KT // 2) as b:
                        for q in range(2):
                            load(2 * b + (chunk + q), q, io[name + "_out"][2 * b + q], 8)
                    chunk += KT
            for k in range(KT):
                sp.wait_ge(x_ready, KT * (len(SUBS) - 1) + k + 1)
                sp.dma_start(io["y"][:, k, :], xT[:, k, :]).then_inc(out_stored, 16)
            sp.wait_ge(out_stored, 16 * (KT + N_OUT))

        @block.scalar
        def _(act):
            act.wait_ge(in_loaded, CONSTS)
            nc.scalar.activation(cond_silu[:], cond[:], ACT.Silu).then_inc(cond_act, 1)
            act.wait_ge(cond_act, 1)
            act.wait_ge(cond_ready, 1)
            nc.scalar.copy(cond_hl[:, :, 0:2], cond_silu[:]).then_inc(cond_act, 1)
            for q in range(2):
                split_hi(act, q, q, 8, wait_used=False)

            def ada_group(g, par, last_tiles):
                for q in (2, 3):
                    split_hi(act, 4 * g + q, q % 2, 8)
                for q in (4, 5):
                    split_hi(act, 4 * g + q, q % 2, last_tiles)
                act.wait_ge(w_used, 4 * g + 4)
                nc.scalar.copy(mod_rows[:, par, :], ps[:, par, :]).then_inc(row_ready, 1)
            with act.Fori(0, 17) as i:
                for par in range(2):
                    ada_group(2 * i + par, par, 8)
            ada_group(34, 0, 8)
            ada_group(35, 1, 8)

            chunk = S["ada"]["blocks"] * 2
            n_rstd = 0
            for si, s in enumerate(SUBS):
                n = si

                def rms(count, sums, value):
                    act.wait_ge(sums, value)
                    link(act, act_chain, nc.scalar.activation(halves(rstd[:]), bank_pair(0), ACT.Ln,
                                                              bias=eps_col[:, 0:1], scale=1.0 / D))
                    nc.scalar.activation(rstd[:], rstd[:], ACT.Exp, scale=-0.5).then_inc(rstd_ready, 1)

                def squares(n):
                    for k in range(KT):
                        if n == 0:
                            act.wait_ge(in_loaded, CONSTS + 16 * KT)
                        else:
                            act.wait_ge(x_ready, KT * (n - 1) + k + 1)
                        if KT * n + k >= 2:
                            act.wait_ge(xsq_used, KT * n + k - 1)
                        nc.scalar.activation(tmp[:, k % 2, :], xT[:, k, :], ACT.Square).then_inc(xsq_ready, 1)

                squares(n)
                rms(2 * n, xsq_used, KT * (n + 1))
                for k in range(KT):
                    act.wait_ge(pre_ready, KT * n + k + 1)
                    for ci, (a, b) in enumerate(GROUPS):
                        last = nc.scalar.activation(hx_hi[:, k, a:b], tmp[:, k % 2, a:b], ACT.Identity,
                                                    bias=mod_col(s["layer"], s["idx"], k, ci))
                    last.then_inc(hxhi_ready, 1)
                if s["kind"] == "ffn":
                    g0 = s["gu0"]

                    def gu_block(m, par, next_tiles, chunk=chunk, g0=g0):
                        for q in (2, 3):
                            split_hi(act, 2 * m + (chunk + q), q % 2, next_tiles)
                        act.wait_ge(w_used, 2 * m + (chunk + 2))
                        nc.scalar.activation(halves(silu_g[:, par, :]), bank_pair(2 * par),
                                             ACT.Silu).then_inc(silu_done, 1)
                        act.wait_ge(mul_done, m + (g0 + 1))
                        nc.scalar.copy(halves(hh_hi[:, m, :]), bank_pair(2 * par + 1)).then_inc(hhi_done, 1)
                    with act.Fori(0, FT // 2 - 1) as i:
                        for par in range(2):
                            gu_block(2 * i + par, par, 8)
                    gu_block(FT - 2, 0, 8)
                    gu_block(FT - 1, 1, 11)
                    chunk += 2 * FT

                    def dn_block(b, par, next_tiles, chunk=chunk, n=n):
                        if next_tiles:
                            for q in (2, 3):
                                split_hi(act, 2 * b + (chunk + q), q % 2, next_tiles)
                        act.wait_ge(w_used, 2 * b + (chunk + 2))
                        nc.scalar.copy(halves(y[:, b, :]), bank_pair(2 * par))
                        act.wait_ge(ssq_done, b + ((KT + 1) * n + 1))
                        nc.scalar.activation(halves(sq[:, par, :]), bank_pair(2 * par),
                                             ACT.Square).then_inc(sq_ready, 1)
                    with act.Fori(0, KT // 2 - 1) as i:
                        for par in range(2):
                            dn_block(2 * i + par, par, 11)
                    dn_block(KT - 2, 0, 11)
                    dn_block(KT - 1, 1, 8 if si + 1 < len(SUBS) else 0)
                    chunk += 2 * KT
                else:
                    nblk = s["tiles_in"]
                    for b in range(nblk):
                        for q in (2, 3):
                            split_hi(act, 2 * b + chunk + q, q % 2, 8)
                        for q in range(2):
                            t = 2 * b + q
                            act.wait_ge(w_used, chunk + t + 1)
                            func, out = ACT.Copy, None
                            if s["layer"] == 1:
                                out = po[:, t, :]
                            elif t < 3:
                                out = pa[:, t, :]
                            else:
                                out = pm[:, t - 3, :]
                                func = ACT.Sigmoid if t - 3 >= PM_O else ACT.Copy
                            nc.scalar.activation(halves(out), bank_pair(2 * (b % 2) + q), func).then_inc(proj_done, 1)
                    chunk += 2 * nblk
                    act_mixer(act, s)
                    act.wait_ge(out_stored, 16 * (4 + s["layer"]))
                    for b in range(KT // 2):
                        if b < KT // 2 - 1 or si + 1 < len(SUBS):
                            for q in (2, 3):
                                split_hi(act, 2 * b + chunk + q, q % 2, 8)
                        for q in range(2):
                            t = 2 * b + q
                            act.wait_ge(w_used, chunk + t + 1)
                            nc.scalar.copy(halves(y_m[:, t, :]), bank_pair(2 * (b % 2) + q))
                            act.wait_ge(ssq_done, t + ((KT + 1) * n + 1))
                            nc.scalar.activation(halves(sq_m[:, t % 2, :]), bank_pair(2 * (b % 2) + q),
                                                 ACT.Square).then_inc(sq_ready, 1)
                    chunk += KT
                rms(2 * n + 1, msq_ready, n + 1)

        @block.vector
        def _(dve):
            nc.vector.memset(cond_hl[:].bitcast(F32), 0.0).then_inc(cond_ready, 1)
            nc.vector.memset(ones[:], 1.0).then_inc(const_ready, 1)
            nc.vector.memset(eps_col[:], EPS).then_inc(const_ready, 1)
            nc.vector.memset(one_col[:], 1.0).then_inc(const_ready, 1)
            dve.wait_ge(cond_act, 2)
            nc.vector.tensor_tensor(cond_hl[:, :, 2:4], cond_silu[:], cond_hl[:, :, 0:2].bitcast(F32),
                                    ALU.subtract).then_inc(cond_ready, 1)
            for q in range(2):
                split_lo(dve, q, q, 8, wait_used=False)

            def ada_group(g, par, last_tiles):
                for q in (2, 3):
                    split_lo(dve, 4 * g + q, q % 2, 8)
                for q in (4, 5):
                    split_lo(dve, 4 * g + q, q % 2, last_tiles)
                dve.wait_ge(col_ready, g + 1)
                cols = ps[:, 2 + par, 0:8].rearrange("p (j c) -> p j c", c=2)
                nc.vector.tensor_tensor(mods[:, bass.ds(4 * g, 4), :], cols, ada_bias[:, bass.ds(4 * g, 4), :],
                                        ALU.add).then_inc(mod_added, 1)
            dve.wait_ge(in_loaded, CONSTS)
            with dve.Fori(0, 17) as i:
                for par in range(2):
                    ada_group(2 * i + par, par, 8)
            ada_group(34, 0, 8)
            ada_group(35, 1, 8)
            dve.wait_ge(mod_added, 36)
            nc.vector.tensor_scalar(neg_sink[:, S_HEADS:], neg_sink[:, 0:S_HEADS], -1.0, None, ALU.mult)
            for layer in range(2):
                for sub in range(3):
                    for ci in range(2):
                        j = (layer * NMOD + 3 * sub + 1) * KT
                        last = nc.vector.scalar_tensor_tensor(out=mods[:, j:j + KT, ci], in0=mods[:, j:j + KT, ci],
                                                              scalar=1.0, in1=norm_g[:, layer, 2 * sub, :],
                                                              op0=ALU.add, op1=ALU.mult)
                        j += KT
                        last = nc.vector.scalar_tensor_tensor(out=mods[:, j:j + KT, ci], in0=mods[:, j:j + KT, ci],
                                                              scalar=1.0 if sub == 1 else 0.5,
                                                              in1=norm_g[:, layer, 2 * sub + 1, :],
                                                              op0=ALU.mult, op1=ALU.mult)
            last.then_inc(mods_ready, 1)
            dve.wait_ge(mods_ready, 1)

            chunk = S["ada"]["blocks"] * 2
            for si, s in enumerate(SUBS):
                n = si
                dve.wait_ge(rstd_ready, 2 * n + 1)

                def scaled(k):
                    if k >= 2:
                        dve.wait_ge(hx_ready, KT * n + k - 1)
                    for ci, (a, b) in enumerate(GROUPS):
                        last = nc.vector.scalar_tensor_tensor(out=tmp[:, k % 2, a:b], in0=xT[:, k, a:b],
                                                              scalar=mod_col(s["layer"], s["idx"] + 1, k, ci),
                                                              in1=rstd[:, a:b], op0=ALU.mult, op1=ALU.mult)
                    last.then_inc(pre_ready, 1)

                def low(k):
                    dve.wait_ge(hxhi_ready, KT * n + k + 1)
                    for ci, (a, b) in enumerate(GROUPS):
                        last = nc.vector.scalar_tensor_tensor(out=hx_lo[:, k, a:b], in0=tmp[:, k % 2, a:b],
                                                              scalar=mod_col(s["layer"], s["idx"], k, ci),
                                                              in1=hx_hi[:, k, a:b].bitcast(F32), op0=ALU.add,
                                                              op1=ALU.subtract)
                    last.then_inc(hx_ready, 1)
                scaled(0)
                for k in range(1, KT):
                    scaled(k)
                    low(k - 1)
                low(KT - 1)
                if s["kind"] == "ffn":
                    g0 = s["gu0"]

                    def gu_block(m, par, next_tiles, chunk=chunk, g0=g0):
                        for q in (2, 3):
                            split_lo(dve, 2 * m + (chunk + q), q % 2, next_tiles)
                        dve.wait_ge(silu_done, m + (g0 + 1))
                        nc.vector.tensor_tensor(bank_pair(2 * par + 1), bank_pair(2 * par + 1),
                                                halves(silu_g[:, par, :]), ALU.mult).then_inc(mul_done, 1)
                        dve.wait_ge(hhi_done, m + (g0 + 1))
                        nc.vector.tensor_tensor(halves(hh_lo[:, m, :]), bank_pair(2 * par + 1),
                                                halves(hh_hi[:, m, :]).bitcast(F32),
                                                ALU.subtract).then_inc(block_free, 1)
                    with dve.Fori(0, FT // 2 - 1) as i:
                        for par in range(2):
                            gu_block(2 * i + par, par, 8)
                    gu_block(FT - 2, 0, 8)
                    gu_block(FT - 1, 1, 11)
                    chunk += 2 * FT
                    nc.vector.memset(ssq[:], 0.0).then_inc(ssq_done, 1)

                    def dn_block(b, par, next_tiles, chunk=chunk, n=n):
                        if next_tiles:
                            for q in (2, 3):
                                split_lo(dve, 2 * b + (chunk + q), q % 2, next_tiles)
                        dve.wait_ge(sq_ready, b + (KT * n + 1))
                        dve.wait_ge(ssq_done, b + ((KT + 1) * n + 1))
                        nc.vector.tensor_tensor(ssq[:], ssq[:], sq[:, par, :], ALU.add).then_inc(ssq_done, 1)
                    with dve.Fori(0, KT // 2 - 1) as i:
                        for par in range(2):
                            dn_block(2 * i + par, par, 11)
                    dn_block(KT - 2, 0, 11)
                    dn_block(KT - 1, 1, 8 if si + 1 < len(SUBS) else 0)
                    chunk += 2 * KT
                else:
                    nblk = s["tiles_in"]
                    for b in range(nblk):
                        for q in (2, 3):
                            split_lo(dve, 2 * b + chunk + q, q % 2, 8)
                    chunk += 2 * nblk
                    dve_mixer(dve, s)
                    for b in range(KT // 2):
                        if b < KT // 2 - 1 or si + 1 < len(SUBS):
                            for q in (2, 3):
                                split_lo(dve, 2 * b + chunk + q, q % 2, 8)
                        if b == 0:
                            dve.wait_ge(out_stored, 16 * (4 + s["layer"]))
                            nc.vector.memset(ssq_m[:], 0.0).then_inc(ssq_done, 1)
                        for q in range(2):
                            t = 2 * b + q
                            dve.wait_ge(sq_ready, KT * n + t + 1)
                            dve.wait_ge(ssq_done, t + ((KT + 1) * n + 1))
                            nc.vector.tensor_tensor(ssq_m[:], ssq_m[:], sq_m[:, t % 2, :], ALU.add).then_inc(ssq_done, 1)
                    chunk += KT
                yb = y if s["kind"] == "ffn" else y_m
                dve.wait_ge(rstd_ready, 2 * n + 2)

                def gated(k):
                    for ci, (a, b) in enumerate(GROUPS):
                        last = nc.vector.scalar_tensor_tensor(out=yb[:, k, a:b], in0=yb[:, k, a:b],
                                                              scalar=mod_col(s["layer"], s["idx"] + 2, k, ci),
                                                              in1=rstd[:, a:b], op0=ALU.mult, op1=ALU.mult)
                    last.then_inc(y_scaled, 1)

                def added(k):
                    dve.wait_ge(y_scaled, KT * n + k + 1)
                    nc.vector.tensor_tensor(xT[:, k, :], xT[:, k, :], yb[:, k, :], ALU.add).then_inc(x_ready, 1)
                gated(0)
                for k in range(1, KT):
                    gated(k)
                    added(k - 1)
                added(KT - 1)

        @block.tensor
        def _(pe):
            pe.wait_ge(const_ready, 2)
            pe.wait_ge(cond_ready, 2)

            def ada_group(g, par, first=False):
                for q in range(4):
                    pe.wait_ge(lo_done, 4 * g + (q + 1))
                    for kk in range(2):
                        k = 2 * q + kk
                        for part in (w_hi, w_lo):
                            last = nc.tensor.matmul(ps[:, par, :], cond_hl[:, k, :],
                                                    part[:, q % 2, kk * 512:(kk + 1) * 512],
                                                    start=(k == 0 and part is w_hi), stop=(k == KT - 1 and part is w_lo))
                    last.then_inc(w_used, 1)
                pe.wait_ge(row_ready, g + 1)
                if not first:
                    pe.wait_ge(mod_added, g)
                for j in range(4):
                    last = nc.tensor.matmul(ps[:, 2 + par, 2 * j:2 * j + 2], mod_rows[:, par, j * P:(j + 1) * P],
                                            pick[:], start=True, stop=True)
                last.then_inc(col_ready, 1)
            ada_group(0, 0, first=True)
            ada_group(1, 1)
            with pe.Fori(1, 18) as i:
                for par in range(2):
                    ada_group(2 * i + par, par)
            pe.wait_ge(mod_added, 36)

            def product(out_bank, q, hi, lo, k0, tiles, first, last_chunk, wait_k=None):
                for t in range(tiles):
                    if wait_k is not None:
                        pe.wait_ge(hx_ready, wait_k + t + 1)
                    wh = w_hi[:, q, t * P:(t + 1) * P]
                    wl = w_lo[:, q, t * P:(t + 1) * P]
                    k = k0 + t
                    for w, a in ((wh, hi), (wh, lo), (wl, hi)):
                        for h in range(2):
                            last = nc.tensor.matmul(ps[:, out_bank + h, 0:TH], w, a[:, k, h * TH:(h + 1) * TH],
                                                    start=(first and t == 0 and w is wh and a is hi),
                                                    stop=(last_chunk and t == tiles - 1 and w is wl))
                last.then_inc(w_used, 1)

            chunk = S["ada"]["blocks"] * 2
            n_free = 0
            for si, s in enumerate(SUBS):
                n = si
                for k in range(KT):
                    pe.wait_ge(xsq_ready, KT * n + k + 1)
                    for h in range(2):
                        last = nc.tensor.matmul(ps[:, h, 0:TH], ones[:], tmp[:, k % 2, h * TH:(h + 1) * TH],
                                                start=(k == 0), stop=(k == KT - 1))
                    last.then_inc(xsq_used, 1)
                pe.wait_ge(rstd_ready, 2 * n + 1)
                if s["kind"] == "ffn":
                    g0 = s["gu0"]

                    def gu_block(m, par, wait_free=True, chunk=chunk, g0=g0, n=n):
                        for q in range(2):
                            pe.wait_ge(lo_done, 2 * m + (chunk + q + 1))
                            if q == 0 and wait_free:
                                pe.wait_ge(block_free, m + (g0 - 1))
                            product(4 * par + 2 * q, q, hx_hi, hx_lo, 0, 8, True, True,
                                    wait_k=KT * n if not wait_free else None)
                    gu_block(0, 0, wait_free=False)
                    gu_block(1, 1, wait_free=False)
                    with pe.Fori(1, FT // 2) as i:
                        for par in range(2):
                            gu_block(2 * i + par, par)
                    chunk += 2 * FT
                    pe.wait_ge(block_free, g0 + FT)

                    def dn_block(b, par, wait_free=True, chunk=chunk, n=n):
                        for q in range(2):
                            pe.wait_ge(lo_done, 2 * b + (chunk + q + 1))
                            if q == 0 and wait_free:
                                pe.wait_ge(sq_ready, b + (KT * n - 1))
                            product(4 * par, q, hh_hi, hh_lo, 11 * q, 11, q == 0, q == 1)
                    dn_block(0, 0, wait_free=False)
                    dn_block(1, 1, wait_free=False)
                    with pe.Fori(1, KT // 2) as i:
                        for par in range(2):
                            dn_block(2 * i + par, par)
                    chunk += 2 * KT
                else:
                    for b in range(s["tiles_in"]):
                        for q in range(2):
                            pe.wait_ge(lo_done, chunk + 2 * b + q + 1)
                            if q == 0 and b >= 2:
                                pe.wait_ge(proj_done, 16 * s["layer"] + 2 * (b - 1))
                            product(4 * (b % 2) + 2 * q, q, hx_hi, hx_lo, 0, 8, True, True,
                                    wait_k=KT * n if b == 0 else None)
                    chunk += 2 * s["tiles_in"]
                    pe.wait_ge(proj_done, 16 * s["layer"] + 2 * s["tiles_in"])
                    pe_mixer(pe, s)
                    for b in range(KT // 2):
                        for q in range(2):
                            pe.wait_ge(lo_done, chunk + 2 * b + q + 1)
                            if q == 0 and b >= 2:
                                pe.wait_ge(sq_ready, KT * n + 2 * (b - 1))
                            product(4 * (b % 2) + 2 * q, q, hx_hi, hx_lo, 0, 8, True, True)
                    chunk += KT
                pe.wait_ge(ssq_done, (KT + 1) * (n + 1))
                pe.wait_ge(sq_ready, KT * (n + 1))
                sums = ssq if s["kind"] == "ffn" else ssq_m
                for h in range(2):
                    last = nc.tensor.matmul(ps[:, h, 0:TH], ones[:], sums[:, h * TH:(h + 1) * TH],
                                            start=True, stop=True)
                last.then_inc(msq_ready, 1)

    return S


def lay_out(inp):
    import numpy as np
    f = {k: np.asarray(v) for k, v in inp.items()}
    c = np.ascontiguousarray
    x = np.concatenate([f["x_prompt"][0], f["x_sample"][0]], 0)
    out = {"x": c(x.T.reshape(KT, P, T).transpose(1, 0, 2))}
    out["cond"] = c(np.stack([f["c_ctx"], f["c"][0]], -1).reshape(KT, P, 2).transpose(1, 0, 2))
    out["norm_g"] = c(f["norm_g"].reshape(2, 6, KT, P).transpose(3, 0, 1, 2))
    b = f["ada_b"].reshape(2 * NMOD * KT, P).T
    out["ada_b"] = c(np.stack([b, b], -1))
    pick = np.zeros((P, 2), np.float32)
    pick[[0, 2], 0] = 1
    pick[[1, 3], 1] = 1
    out["pick"] = pick
    w = f["ada_w"].reshape(2, 4, 2, P, 18, 512).transpose(0, 4, 1, 3, 2, 5)
    out["ada_w"] = c(w).reshape(144, P, 1024)
    def gu(w):
        return w.reshape(4, KT, P, FT, P).transpose(0, 3, 2, 1, 4)
    out["ffn_gu"] = c(np.stack([gu(f["ffn_w_gate"]), gu(f["ffn_w_up"])], 2)).reshape(4, FT, 2, P, 1024)
    w = f["ffn_w_down"].reshape(4, 2, 11, P, KT, P).transpose(0, 4, 1, 3, 2, 5)
    out["ffn_dn"] = c(w).reshape(4, KT, 2, P, SLOT)

    def tiles(w):
        n = w.shape[1] // P
        return c(w.reshape(KT, P, n, P).transpose(2, 1, 0, 3)).reshape(n, P, KT * P)

    w = f["even_w_in"][0]
    o = np.cumsum([0, Q_LORA, P, ROPE, M_HEADS * M_DK, M_HEADS * M_DK, M_HEADS * M_DV, M_HEADS * M_DV, 4 * M_HEADS])
    gates = np.zeros((D, P), np.float32)
    gates[:, 0:16] = w[:, o[7]:o[8]]
    gates[:, NOPE:MLA_QK] = w[:, o[2]:o[3]]
    out["even_in"] = tiles(np.concatenate([w[:, o[0]:o[2]], gates, w[:, o[3]:o[7]]], 1))
    out["even_out"] = tiles(f["even_w_out"][0])
    out["w_qb"] = c(f["mla_w_qb"][0].reshape(2, P, -1).transpose(1, 0, 2))
    kvb = f["mla_w_kvb"][0].reshape(P, MLA_HEADS, 2, 64)
    out["w_kvb"] = c(kvb.transpose(0, 2, 1, 3)).reshape(P, 2, -1)
    out["ckv_old"] = c(f["cache_mla_ckv"][0, 0].T)
    out["krope_old"] = c(f["cache_mla_krope"][0, 0].T)
    def rope(rot):
        nf = rot // 4
        inv = 10000.0 ** (-np.arange(nf, dtype=np.float32) / np.float32(nf))
        t = np.arange(LAT)
        cos, sin = np.zeros((rot, LAT), np.float32), np.zeros((rot, LAT), np.float32)
        swap = np.zeros((rot, rot), np.float32)
        for j in range(rot):
            axis, second, i = j // (2 * nf), j // nf % 2, j % nf
            ang = ((t // 64, t % 64)[axis]).astype(np.float32) * inv[i].astype(np.float32)
            cos[j] = np.cos(ang)
            sin[j] = np.sin(ang) * (1 if second else -1)
            swap[(j - nf) if second else (j + nf), j] = 1
        return cos, sin, swap
    cos, sin, swap = rope(ROPE)
    out["rope_e"] = np.zeros((P, 2, LAT), np.float32)
    out["rope_e"][NOPE:MLA_QK, 0], out["rope_e"][NOPE:MLA_QK, 1] = cos, sin
    out["swap_e"] = np.zeros((P, ROPE), np.float32)
    out["swap_e"][NOPE:MLA_QK] = swap
    cos, sin, swap = rope(HEAD)
    out["rope_o"] = c(np.stack([np.concatenate([cos, cos]), np.concatenate([sin, sin])], 1))
    out["swap_o"] = np.zeros((P, P), np.float32)
    out["swap_o"][0:64, 0:64] = out["swap_o"][64:128, 64:128] = swap
    pr = np.zeros((P, 2, ROWS), np.float32)
    for d in range(2):
        for h in range(M_HEADS):
            for j in range(2):
                pr[8 * d + 4 * j + h, j, 32 * d + h] = 1
    out["pick_rows"] = pr
    rb = np.zeros((P, 3), np.float32)
    gb, m0 = f["mlstm_gate_b"][0].reshape(2, 2, M_HEADS), f["state_mlstm_m"][0, 0]
    for d in range(2):
        rb[32 * d:32 * d + M_HEADS, 0] = gb[d, 0]
        rb[32 * d:32 * d + M_HEADS, 1] = gb[d, 1]
        rb[32 * d:32 * d + M_HEADS, 2] = m0[d]
    out["row_bias"] = rb
    oh = np.zeros((ROWS, 8, P), np.float32)
    for d in range(2):
        for h in range(M_HEADS):
            oh[32 * d + h, 4 * d + h] = 1
    out["onehot"] = oh
    st = np.zeros((2, M_HEADS, M_DK, 2 * P), np.float32)
    st[..., 0:P] = f["state_mlstm_C"][0, 0]
    st[..., P:] = f["state_mlstm_n"][0, 0][..., None]
    out["state0"] = c(st.reshape(2, 2, P, 2 * P).transpose(2, 0, 1, 3))
    g = np.zeros((P, 8), np.float32)
    g[:, 0:2] = f["mla_g_qa"][0].reshape(2, P).T
    g[:, 2] = f["mla_g_kva"][0]
    g[:, 3:7] = f["mlstm_g_out"][0].reshape(M_HEADS, P).T
    out["gains"] = g
    out["ident"] = np.eye(P, dtype=np.float32)
    i = np.arange(P)
    out["causal"] = c(np.stack([np.where(i[None] >= i[:, None], 0, NEG), np.where(i[None] <= i[:, None], 0, NEG)],
                               1).astype(np.float32))
    order = [4 * (2 * p + half) + m for p in range(2) for m in range(4) for half in range(2)]
    w = f["odd_w_in"][0]
    wq = w[:, 0:D].reshape(D, S_HEADS, HEAD)[:, order].reshape(D, D)
    out["odd_in"] = tiles(np.concatenate([wq, w[:, D:]], 1))
    out["odd_out"] = tiles(f["odd_w_out"][0].reshape(S_HEADS, HEAD, D)[order].reshape(D, D))
    out["k_old"] = c(f["cache_swa_k"][0, 0].reshape(2, 2, PAST, HEAD).transpose(1, 3, 0, 2)).reshape(P, 2, PAST)
    out["v_old"] = c(f["cache_swa_v"][0, 0].reshape(KV_HEADS, 2, P, HEAD).transpose(2, 1, 0, 3)).reshape(P, 2, -1)
    sk = np.broadcast_to(f["swa_sink"][0], (P, S_HEADS))
    out["sinks"] = c(sk)
    return out


OUTS = {"y": (P, KT, T), "out_ckv": (P, CTX), "out_krope": (ROPE, CTX), "out_state": (P, 2, 2, 2 * P),
        "out_m": (ROWS, 1), "out_kv": (P, 4, CTX)}


def hand_back(r):
    import numpy as np
    c = np.ascontiguousarray
    y = r["y"].transpose(1, 0, 2).reshape(D, T).T
    st = r["out_state"].reshape(2, M_DK, 2, 2, 2 * P).transpose(2, 3, 0, 1, 4).reshape(1, 1, 2, M_HEADS, M_DK, 2 * P)
    m = np.stack([r["out_m"][0:M_HEADS, 0], r["out_m"][32:32 + M_HEADS, 0]])[None, None]
    kv = r["out_kv"].reshape(2, HEAD, 2, 2, CTX).transpose(2, 3, 0, 4, 1).reshape(2, 1, 1, KV_HEADS, CTX, HEAD)
    return (c(y[0:CTX])[None], c(y[CTX:])[None], c(r["out_ckv"].T)[None, None], c(r["out_krope"].T)[None, None],
            c(st[..., 0:P]), c(st[..., P]), c(m), c(kv[0]), c(kv[1]))


def kernel(**inputs):
    import concourse.bacc as _bacc
    from concourse.bass_utils import run_bass_kernel_spmd as _run

    nc = _bacc.Bacc("TRN2", target_bir_lowering=False, num_devices=1, dynamic_dma_scratch_size=1024)
    arrays = {"in_" + k: v for k, v in lay_out(inputs).items()}
    io = {k[3:]: nc.dram_tensor(k, v.shape, mybir.dt.from_np(v.dtype), kind="ExternalInput").ap()
          for k, v in arrays.items()}
    for name, shape in OUTS.items():
        io[name] = nc.dram_tensor("res_" + name, shape, F32, kind="ExternalOutput").ap()
    build(nc, io)
    r = _run(nc, [arrays], core_ids=[0])
    return hand_back({name: r.results[0]["res_" + name] for name in OUTS})
```

```python
from contextlib import ExitStack

import concourse.bass as bass
from concourse import mybir

F32 = mybir.dt.float32
F32R = mybir.dt.float32r
BF16 = mybir.dt.bfloat16
ACT = mybir.ActivationFunctionType
ALU = mybir.AluOpType
AX = mybir.AxisListType

P = 128
D = 1024
KT = D // P
CTX, LAT = 128, 512
T = CTX + LAT
TH = T // 2
PAST = 256
FF = 2816
FT = FF // P
NMOD = 9
EPS = 1e-6
SLOT = 11 * P
MLA_HEADS, NOPE, ROPE, MLA_V, Q_LORA = 8, 64, 32, 64, 256
MLA_QK = NOPE + ROPE
M_HEADS, M_DK, M_DV = 4, 64, 128
CHUNKS = T // P
S_HEADS, KV_HEADS, HEAD = 16, 4, 64
KEYS = CTX + PAST + LAT
NEG = -1e30
ROWS = 36
PM_GATES, PM_Q, PM_K, PM_V, PM_O = 0, 1, 3, 5, 9
ADA_GROUPS = 2 * NMOD * D // 512
ADA_SLOTS = 4
GROUPS = ((0, CTX), (CTX, T))



def plan_stages():
    stages, first = {}, 0
    order = []
    for f in range(4):
        if f == 1:
            order += [("even_in", 8, 8), ("even_out", 4, 8)]
        if f == 3:
            order += [("odd_in", 6, 8), ("odd_out", 4, 8)]
        order += [(f"gu{f}", FT, 8), (f"dn{f}", 8, 11)]
    for i, (name, blocks, tiles) in enumerate(order):
        stages[name] = dict(name=name, blocks=blocks, tiles=tiles, base=first,
                            next_tiles=order[i + 1][2] if i + 1 < len(order) else 0)
        first += 2 * blocks
    return stages


def attention_plan(layer):
    steps, g, u, b = [], 0, 0, 0
    for lay in range(2):
        out = []
        for h in range((MLA_HEADS, KV_HEADS)[lay]):
            for ns in (((-1, 0),), ((-1, 0), (1,), (2,), (3,)))[lay]:
                step = []
                for n in ns:
                    if lay == 0:
                        size, local, past = (1, (0, 1), 0) if n < 0 else (LAT // P, (0, (KEYS - CTX) // P), 0)
                    else:
                        size, past = S_HEADS // KV_HEADS, 0 if n < 0 else PAST // P
                        local = (0, 1) if n < 0 else (max(n - 1, 0), min(n + 2, LAT // P))
                    keys = local[1] - local[0] + past
                    step.append(dict(g=g, u=u, b=b, h=h, n=n, size=size, local=local, keys=keys, r=64 * (h % 2)))
                    g, u, b = g + 1, u + size, b + keys
                out.append(step)
        steps.append(out)
    return steps[layer]


def build(nc, io, upto=99):
    S = plan_stages()
    N_CHUNKS = max(s["base"] + 2 * s["blocks"] for s in S.values())
    with ExitStack() as ctx:
        def sb(name, shape, dt=F32):
            return ctx.enter_context(nc.sbuf_tensor(name, shape, dt))

        def sem(name):
            return ctx.enter_context(nc.semaphore(name))

        xT = sb("xT", [P, KT, T])
        w_raw = sb("w_raw", [P, 2, SLOT])
        w_hi = sb("w_hi", [P, 2, SLOT], F32R)
        w_lo = sb("w_lo", [P, 2, SLOT], F32R)
        ones = sb("ones", [P, P])
        eps_col = sb("eps_col", [P, 1])
        mods = sb("mods", [P, 2 * NMOD * KT, 2])
        rstd = sb("rstd", [P, T])
        maxes = sb("maxes", [P, 4, 4])
        sink_e = sb("sink_e", [P, 4, 4])
        neg_sink = sb("neg_sink", [P, 2 * S_HEADS])
        gains = sb("gains", [P, 8])
        row_bias = sb("row_bias", [P, 3])
        m_in = sb("m_in", [P, 8])
        one_col = sb("one_col", [P, 1])
        ident = sb("ident", [P, P])
        causal = sb("causal", [P, 2, P])
        ones_r = sb("ones_r", [P, P], F32R)
        ident_b = sb("ident_b", [P, P], BF16)
        causal_b = sb("causal_b", [P, 2, 4, P], BF16)
        sink_half = sb("sink_half", [P, 3, 64])
        neg_m = sb("neg_m", [P, 4, 4], F32R)

        ps = ctx.enter_context(nc.psum_tensor("ps", [P, 8, 512], F32))

        with ExitStack() as scope:
            def asb(name, shape, dt=F32):
                return scope.enter_context(nc.sbuf_tensor(name, shape, dt))
            cond = asb("cond", [P, KT, 2])
            cond_silu = asb("cond_silu", [P, KT, 2])
            cond_hl = asb("cond_hl", [P, KT, P], F32R)
            mod_rows = asb("mod_rows", [P, 2, 512])
            pick = asb("pick", [P, 2])
            ada_bias = asb("ada_bias", [P, 2 * NMOD * KT, 2])
            norm_g = asb("norm_g", [P, 2, 6, KT])
            ada_raw = asb("ada_raw", [P, ADA_SLOTS, KT, 512])
            ada_hi = asb("ada_hi", [P, 2, KT, 512], F32R)
            ada_lo = asb("ada_lo", [P, 2, KT, 512], F32R)
        with ExitStack() as scope:
            def fsb(name, shape, dt=F32):
                return scope.enter_context(nc.sbuf_tensor(name, shape, dt))
            hx_hi = fsb("hx_hi", [P, KT, T], F32R)
            hx_lo = fsb("hx_lo", [P, KT, T], F32R)
            tmp = fsb("tmp", [P, 2, T])
            silu_g = tmp
            with ExitStack() as inner:
                hh_hi = inner.enter_context(nc.sbuf_tensor("hh_hi", [P, FT, T], F32R))
                hh_lo = inner.enter_context(nc.sbuf_tensor("hh_lo", [P, FT, T], F32R))
        with ExitStack() as scope:
            y = scope.enter_context(nc.sbuf_tensor("y", [P, KT, T], F32))
            sq = scope.enter_context(nc.sbuf_tensor("sq", [P, 2, T], F32))
            ssq = scope.enter_context(nc.sbuf_tensor("ssq", [P, T], F32))

        with ExitStack() as scope:
            def esb(name, shape, dt=F32, s=scope):
                return s.enter_context(nc.sbuf_tensor(name, shape, dt))
            for name in ("hx_hi_", "hx_lo_"):
                esb(name, [P, KT, T])
            esb("tmp_", [P, 2, T])
            with ExitStack() as res:
                y_m = esb("y_m", [P, KT, T], s=res)
                sq_m = esb("sq_m", [P, 2, T], s=res)
                ssq_m = esb("ssq_m", [P, T], s=res)
            with ExitStack() as even:
                pm = esb("pm", [P, 13, T], s=even)
                with ExitStack() as mla:
                    qh = esb("qh", [P, MLA_HEADS, T], s=mla)
                    kh = esb("kh", [P, MLA_HEADS, KEYS], s=mla)
                    vtok = esb("vtok", [P, KEYS // P, MLA_HEADS // 2, 3, MLA_V], s=mla)
                    with ExitStack() as part:
                        pa = esb("pa", [P, 3, T], s=part)
                        w_qb = esb("w_qb", [P, 2, MLA_HEADS * MLA_QK], s=part)
                    with ExitStack() as part:
                        prob_e = esb("prob_e", [P, 3, 512], s=part)
                with ExitStack() as ml:
                    vaug = esb("vaug", [P, CHUNKS, M_HEADS, 2 * P], s=ml)
                    ktok = esb("ktok", [P, CHUNKS, M_HEADS * M_DK], s=ml)
                    onehot = esb("onehot", [P, 8, P], s=ml)
                    rows3 = esb("rows3", [P, 3, T], s=ml)
                    acol = esb("acol", [P, CHUNKS, ROWS], s=ml)
                    decay = esb("decay", [P, T], s=ml)
                    weigh = esb("weigh", [P, T], s=ml)
                    g_inter = esb("g_inter", [P, T], s=ml)
                    floor_m = esb("floor_m", [P, T], s=ml)
                    q_inter = esb("q_inter", [P, 2, T], s=ml)
                    k_w = esb("k_w", [P, CHUNKS, M_DK], s=ml)
                    state = esb("state", [P, 5, 2 * P], s=ml)
                    state0 = esb("state0", [P, 2, 2, 2 * P], s=ml)
                    state_out = esb("state_out", [P, 2, 2, 2 * P], s=ml)
                    with ExitStack() as early:
                        rows = esb("rows", [P, 6, T], s=early)
                    hm = esb("hm", [P, M_HEADS, T], s=ml)
                    hs = esb("hs", [P, T], s=ml)
            with ExitStack() as odd:
                po = esb("po", [P, 12, T], s=odd)
                v_new = esb("v_new", [P, CHUNKS, KV_HEADS // 2, 3, HEAD], s=odd)
                v_old = esb("v_old", [P, PAST // P, KV_HEADS // 2, 3, HEAD], s=odd)
                k_old = esb("k_old", [P, 2, PAST], s=odd)
                rope_o = esb("rope_o", [P, 2, LAT], s=odd)
                swap_o = esb("swap_o", [P, P], s=odd)
                turned = esb("turned", [P, 2, LAT], s=odd)
                prob_o = esb("prob_o", [P, 3, 512], s=odd)
                diag_o = odd.enter_context(nc.sbuf_tensor("diag_o", [P, 4, 4, P], F32R))
                sink_diag = esb("sink_diag", [P, 4, 4, P], s=odd)
                out_o = esb("out_o", [P, 2, 2, 512], s=odd)
        with ExitStack() as scope:
            for name, shape in (("y_", [P, KT, T]), ("sq_", [P, 2, T]), ("ssq_", [P, T])):
                scope.enter_context(nc.sbuf_tensor(name, shape, F32))
            rope_e = scope.enter_context(nc.sbuf_tensor("rope_e", [P, 2, LAT], F32))
            swap_e = scope.enter_context(nc.sbuf_tensor("swap_e", [P, ROPE], F32))
            pick_rows = scope.enter_context(nc.sbuf_tensor("pick_rows", [P, 2, ROWS], F32))
            w_kvb = scope.enter_context(nc.sbuf_tensor("w_kvb", [P, 2, MLA_HEADS * 64], F32))
            ckv_keys = scope.enter_context(nc.sbuf_tensor("ckv_keys", [P, KEYS], F32))

        with ExitStack() as scope:
            scope.enter_context(nc.sbuf_tensor("hx_hi_mla", [P, KT // 2, T], F32))
            with ExitStack() as part:
                out_e = part.enter_context(nc.sbuf_tensor("out_e", [P, 2, 2, 512], F32))
            scope.enter_context(nc.sbuf_tensor("hx_rest", [P, KT, T], F32))
            diag_e = scope.enter_context(nc.sbuf_tensor("diag_e", [P, 4, 4, P], F32R))

        in_loaded, x_loaded = sem("in_loaded"), sem("x_loaded")
        const_ready = sem("const_ready")
        raw_ready = [sem("raw_ready0"), sem("raw_ready1")]
        hi_done, lo_done, w_used = sem("hi_done"), sem("lo_done"), sem("w_used")
        act_chain, dve_chain, y_scaled = sem("act_chain"), sem("dve_chain"), sem("y_scaled")
        cond_act, cond_ready = sem("cond_act"), sem("cond_ready")
        ada_loaded = [sem(f"ada_loaded{q}") for q in range(ADA_SLOTS)]
        ada_hi_done, ada_lo_done, ada_used = sem("ada_hi_done"), sem("ada_lo_done"), sem("ada_used")
        row_ready, col_ready, mod_added, mods_ready = sem("row_ready"), sem("col_ready"), sem("mod_added"), sem("mods_ready")
        silu_done, mul_done, hhi_done, block_free = sem("silu_done"), sem("mul_done"), sem("hhi_done"), sem("block_free")
        sq_ready, ssq_done = sem("sq_ready"), sem("ssq_done")
        msq_ready, rstd_ready = sem("msq_ready"), sem("rstd_ready")
        x_ready, xsq_ready, xsq_used = sem("x_ready"), sem("xsq_ready"), sem("xsq_used")
        pre_ready, hxhi_ready, hx_ready = sem("pre_ready"), sem("hxhi_ready"), sem("hx_ready")
        out_stored = sem("out_stored")
        proj_done = sem("proj_done")
        mix_loaded, mix_loaded2, mix_loaded3 = sem("mix_loaded"), sem("mix_loaded2"), sem("mix_loaded3")
        lora_sq, lora_sum, lora_rstd, lora_ready = sem("lora_sq"), sem("lora_sum"), sem("lora_rstd"), sem("lora_ready")
        built, built_act, built_dve = sem("built"), sem("built_act"), sem("built_dve")
        s_ready, max_done, diag_ready, st_ready = sem("s_ready"), sem("max_done"), sem("diag_ready"), sem("st_ready")
        sink_arg, sink_exp, sink_ready, attn_const = sem("sink_arg"), sem("sink_exp"), sem("sink_ready"), sem("attn_const")
        p_ready, pv_done, o_ready, o_scaled = sem("p_ready"), sem("pv_done"), sem("o_ready"), sem("o_scaled")
        ohi_done, o_done = sem("ohi_done"), sem("o_done")
        gate_act, gate_rows, rows_ready = sem("gate_act"), sem("gate_rows"), sem("rows_ready")
        turn_ready, turn_act, turn_dve = sem("turn_ready"), sem("turn_act"), sem("turn_dve")
        kq_ready, decay_arg, decay_ready = sem("kq_ready"), sem("decay_arg"), sem("decay_ready")
        weigh_ready, gain_ready, state_ready = sem("weigh_ready"), sem("gain_ready"), sem("state_ready")
        numden_ready, head_done = sem("numden_ready"), sem("head_done")
        hm_sq, hm_sum, hm_rstd, hm_f, hm_hi, mix_ready = (sem("hm_sq"), sem("hm_sum"), sem("hm_rstd"), sem("hm_f"),
                                                         sem("hm_hi"), sem("mix_ready"))
        odd_swap, odd_rope = sem("odd_swap"), sem("odd_rope")
        chained = {}
        CONSTS = 9 * 16
        N_OUT = 4 * (upto > 1) + (upto > 4)
        MLA_GROUPS, SWA_GROUPS = [sum(attention_plan(layer), []) for layer in range(2)]
        KB = KEYS // P

        def link(eng, chain, ins):
            chained[chain.name] = chained.get(chain.name, 0) + 1
            ins.then_inc(chain, 1)
            eng.wait_ge(chain, chained[chain.name])

        ada_w, ffn_gu, ffn_dn = io["ada_w"], io["ffn_gu"], io["ffn_dn"]

        def bank_pair(i):
            return ps[:, 2 * i:2 * i + 2, 0:TH]

        def halves(tile):
            return tile.rearrange("p (n t) -> p n t", n=2)

        def split_hi(act, c, slot, tiles, wait_used=True):
            act.wait_ge(raw_ready[slot], (c // 2) * 16 + 16 if isinstance(c, int) else c * 8 + (16 - 8 * slot))
            if wait_used:
                act.wait_ge(w_used, c - 1)
            nc.scalar.copy(w_hi[:, slot, 0:tiles * P], w_raw[:, slot, 0:tiles * P]).then_inc(hi_done, 1)

        def split_lo(dve, c, slot, tiles, wait_used=True):
            dve.wait_ge(hi_done, c + 1)
            if wait_used:
                dve.wait_ge(w_used, c - 1)
            nc.vector.tensor_tensor(w_lo[:, slot, 0:tiles * P], w_raw[:, slot, 0:tiles * P],
                                    w_hi[:, slot, 0:tiles * P], ALU.subtract).then_inc(lo_done, 1)

        def mod_col(layer, idx, k, cond_i):
            j = (layer * NMOD + idx) * KT + k
            return mods[:, j, cond_i:cond_i + 1]

        SUBS = []
        for layer in range(2):
            SUBS += [dict(kind="ffn", f=2 * layer, layer=layer, idx=0), dict(kind="mix", layer=layer, idx=3),
                     dict(kind="ffn", f=2 * layer + 1, layer=layer, idx=6)]
        SUBS = SUBS[:upto]
        chunk0, gu0 = 0, 0
        for s in SUBS:
            s.update(chunk=chunk0, gu0=gu0)
            s["tiles_in"] = {"ffn": FT, "mix": 8 if s["layer"] == 0 else 6}[s["kind"]]
            s["blocks_out"] = KT if s["kind"] == "ffn" else KT // 2
            chunk0 += 2 * (s["tiles_in"] + s["blocks_out"])
            gu0 += FT if s["kind"] == "ffn" else 0

        block = ctx.enter_context(nc.Block())

        BUILD = [("kr", 0), ("gi", 0), ("gf", 0)]
        for h in range(MLA_HEADS):
            BUILD += [("q", h), ("k", h)] + ([("sw", h - 1)] if h else [])
        BUILD += [("sw", MLA_HEADS - 1)] + [("v", j) for j in range(KEYS // P)]
        BY_ACT = ("q", "v", "gi", "gf")

        def evacuated(i):
            a = sum(kind in BY_ACT for kind, _ in BUILD[:i])
            return a, i - a

        QPOS = {h: BUILD.index(("q", h)) for h in range(MLA_HEADS)}

        def pair_flat(i):
            return ps[:, 2 * i:2 * i + 2, :].rearrange("p b c -> p (b c)")

        def seq_dir(i):
            return i // 2, i % 2

        def pe_attention(pe, layer):
            steps = attention_plan(layer)
            prob, diag = (prob_e, prob_o)[layer], (diag_e, diag_o)[layer]

            def key_block(g, j):
                if layer == 0:
                    c = 0 if g["n"] < 0 else CTX + j * P
                    return kh[0:MLA_QK, g["h"], c:c + P]
                rs, p, local = slice(g["r"], g["r"] + 64), g["h"] // 2, g["local"][1] - g["local"][0]
                if g["n"] < 0:
                    return po[rs, 8 + p, 0:CTX]
                if j < local:
                    c = CTX + (g["local"][0] + j) * P
                    return po[rs, 8 + p, c:c + P]
                return k_old[rs, p, (j - local) * P:(j - local + 1) * P]

            def unit_scores(g, i):
                u = g["u"] + i
                if u >= 2:
                    pe.wait_ge(max_done, u - 1)
                bank = 2 * (u % 2)
                q0 = 0 if g["n"] < 0 else CTX + g["n"] * P
                a, b = score_columns(layer, g)
                if layer == 0:
                    q0 += i * P
                    query = qh[0:MLA_QK, g["h"], q0:q0 + P]
                    k0 = 0 if g["n"] < 0 else CTX
                    parts = [kh[0:MLA_QK, g["h"], k0:k0 + 512 - a], kh[0:MLA_QK, g["h"], CTX + 512 - a:CTX + b - a]]
                else:
                    rs, p, (lo, hi) = slice(g["r"], g["r"] + 64), g["h"] // 2, g["local"]
                    query = po[rs, 4 * p + i, q0:q0 + P]
                    k0 = 0 if g["n"] < 0 else CTX + lo * P
                    parts = [po[rs, 8 + p, k0:k0 + 512 - a], k_old[rs, p, :]]
                masks = []
                if layer == 1 and g["n"] >= 0:
                    if lo < g["n"]:
                        masks.append((a, 0))
                    if hi > g["n"] + 1:
                        masks.append((512 - P, 1))
                ins = nc.tensor.matmul(ps[:, bank, a:512], query, parts[0], start=True, stop=not masks)
                for c, side in masks:
                    ins = nc.tensor.matmul(ps[:, bank, c:c + P], ident_b[:], causal_b[:, side, 0, :], start=False,
                                           stop=(c, side) == masks[-1])
                if b > 512:
                    ins = nc.tensor.matmul(ps[:, bank + 1, 0:b - 512], query, parts[1], start=True, stop=True)
                ins.then_inc(s_ready, 1)

            def block_scores(g, j):
                b, width = g["b"] + j, g["size"] * P
                if j == 0:
                    pe.wait_ge(diag_ready, g["g"] + 1)
                if b >= 2:
                    pe.wait_ge(p_ready, b - 1)
                out = ps[:, 4 + b % 2, 0:width]
                nc.tensor.matmul(out, ones_r[:], diag[:, g["g"] % 4, 0:g["size"], :].rearrange("p i q -> p (i q)"),
                                 start=True, stop=False)
                if layer == 0:
                    q0 = 0 if g["n"] < 0 else CTX
                    ins = nc.tensor.matmul(out, key_block(g, j), qh[0:MLA_QK, g["h"], q0:q0 + width], start=False,
                                           stop=True)
                else:
                    rs, p, n, c = slice(g["r"], g["r"] + 64), g["h"] // 2, g["n"], g["local"][0] + j
                    q0 = 0 if n < 0 else CTX + n * P
                    side = {n - 1: 1, n + 1: 0}.get(c) if n >= 0 and c < g["local"][1] else None
                    ins = nc.tensor.matmul(out.rearrange("p (i q) -> p i q", q=P), key_block(g, j),
                                           po[rs, 4 * p:4 * p + 4, q0:q0 + P], start=False, stop=side is None)
                    if side is not None:
                        ins = nc.tensor.matmul(out, ident_b[:], causal_b[:, side].rearrange("p i q -> p (i q)"),
                                               start=False, stop=True)
                ins.then_inc(st_ready, 1)

            def block_values(g, j):
                h, n, width, b = g["h"], g["n"], g["size"] * P, g["b"] + j
                pe.wait_ge(p_ready, b + 1)
                if j == 0 and g["g"] >= 2:
                    pe.wait_ge(o_scaled, g["g"] - 1)
                if layer == 0:
                    v = vtok[:, 0 if n < 0 else 1 + j, h // 2]
                elif n < 0:
                    v = v_new[:, 0, h // 2]
                elif j < g["local"][1] - g["local"][0]:
                    v = v_new[:, 1 + g["local"][0] + j, h // 2]
                else:
                    v = v_old[:, j - (g["local"][1] - g["local"][0]), h // 2]
                out, last = ps[:, 6 + g["g"] % 2, 0:width], j == g["keys"] - 1
                cols = slice(64 * (h % 2), 64 * (h % 2) + P)
                ins = nc.tensor.matmul(out, v.rearrange("p a d -> p (a d)")[:, cols], prob[:, b % 3, 0:width],
                                       start=(j == 0), stop=last and layer == 0)
                ins.then_inc(pv_done, 1)
                if last and layer == 1:
                    pe.wait_ge(sink_ready, g["g"] - len(MLA_GROUPS) + 1)
                    ins = nc.tensor.matmul(out, sink_half[:].rearrange("p a d -> p (a d)")[:, cols],
                                           sink_diag[:, g["g"] % 4].rearrange("p i q -> p (i q)"), start=False, stop=True)
                    ins.then_inc(o_ready, 1)

            pe.wait_ge(attn_const, 6)
            for unit in units_of(steps[0]):
                unit_scores(*unit)
            blocks = []
            for t, step in enumerate(steps):
                own = [(g, j) for g in step for j in range(g["keys"])]
                ahead = units_of(steps[t + 1]) if t + 1 < len(steps) else []
                per = -(-len(ahead) // max(len(own) - 2, 1))
                for i, (g, j) in enumerate(own):
                    blocks.append((g, j, ahead[i * per:(i + 1) * per]))
            for i, (g, j, ahead) in enumerate(blocks):
                block_scores(g, j)
                if i:
                    block_values(*blocks[i - 1][0:2])
                for unit in ahead:
                    unit_scores(*unit)
            block_values(*blocks[-1][0:2])

        def units_of(step):
            return [(g, i) for g in step for i in range(g["size"])]

        def score_columns(layer, g):
            if g["n"] < 0:
                return 512 - P, 512
            if layer == 0:
                return 128, 896
            return 512 - P * (g["local"][1] - g["local"][0]), 512 + PAST

        def act_attention(act, layer):
            steps = attention_plan(layer)
            scale = (MLA_QK ** -0.5, HEAD ** -0.5)[layer]
            prob, outs = (prob_e, prob_o)[layer], (out_e, out_o)[layer]

            def round_output(g):
                act.wait_ge(o_scaled, g["g"] + 1)
                dst, src = mixed(hx_hi, g, outs)
                nc.scalar.copy(dst, src).then_inc(ohi_done, 1)
            waiting = []
            for step in steps:
                if layer == 1:
                    for g in step:
                        act.wait_ge(sink_arg, g["g"] - len(MLA_GROUPS) + 1)
                        nc.scalar.activation(sink_e[:, g["g"] % 4, :], sink_e[:, g["g"] % 4, :],
                                             ACT.Exp).then_inc(sink_exp, 1)
                for i, (g, j) in enumerate((g, j) for g in step for j in range(g["keys"])):
                    b, width = g["b"] + j, g["size"] * P
                    act.wait_ge(st_ready, b + 1)
                    if b >= 3:
                        act.wait_ge(pv_done, b - 2)
                    nc.scalar.activation(prob[:, b % 3, 0:width], ps[:, 4 + b % 2, 0:width], ACT.Exp,
                                         scale=scale).then_inc(p_ready, 1)
                    if i >= 3 and waiting:
                        round_output(waiting.pop(0))
                for g in waiting:
                    round_output(g)
                waiting = list(step)
            for g in waiting:
                round_output(g)

        def mixed(buf, g, outs):
            h, n, r = g["h"], g["n"], g["r"]
            src = outs[r:r + 64, g["g"] % 2, 1, 0:g["size"] * P]
            if g["g"] < len(MLA_GROUPS):
                return (buf[r:r + 64, h // 2, 0:CTX] if n < 0 else buf[r:r + 64, h // 2, CTX:T]), src
            c0 = 0 if n < 0 else CTX + n * P
            return buf[r:r + 64, 4 * (h // 2):4 * (h // 2) + 4, c0:c0 + P], src.rearrange("p (i q) -> p i q", q=P)

        def dve_attention(dve, layer):
            steps = attention_plan(layer)
            scale = (MLA_QK ** -0.5, HEAD ** -0.5)[layer]
            diag, outs = (diag_e, diag_o)[layer], (out_e, out_o)[layer]

            def diagonal(out, column, slot, size=4):
                shape = (P, size, P)
                return nc.vector.tensor_tensor(out[:, slot, 0:size], ident[:].unsqueeze(1).broadcast_to(shape),
                                               column[:, slot, 0:size].unsqueeze(2).broadcast_to(shape), ALU.mult)

            def maxima(step):
                for g in step:
                    a, b = score_columns(layer, g)
                    slot, size = g["g"] % 4, g["size"]
                    for i in range(size):
                        u = g["u"] + i
                        dve.wait_ge(s_ready, u + 1)
                        nc.vector.tensor_reduce(maxes[:, slot, i:i + 1], pair_flat(u % 2)[:, a:b], AX.X,
                                                ALU.max).then_inc(max_done, 1)
                    dve.wait_ge(max_done, g["u"] + size)
                    if layer == 0:
                        ins = nc.vector.tensor_scalar(neg_m[:, slot, 0:size], maxes[:, slot, 0:size], -1.0, None, ALU.mult)
                    else:
                        heads = slice(S_HEADS + 4 * g["h"], S_HEADS + 4 * g["h"] + 4)
                        ins = nc.vector.scalar_tensor_tensor(out=neg_m[:, slot, :], in0=maxes[:, slot, :], scalar=-1.0,
                                                             in1=neg_sink[:, heads], op0=ALU.mult, op1=ALU.min)
                    link(dve, dve_chain, ins)
                    if layer == 1:
                        heads = slice(4 * g["h"], 4 * g["h"] + 4)
                        nc.vector.scalar_tensor_tensor(out=sink_e[:, slot, :], in0=neg_m[:, slot, :].bitcast(F32),
                                                       scalar=scale, in1=neg_sink[:, heads], op0=ALU.mult,
                                                       op1=ALU.add).then_inc(sink_arg, 1)
                    diagonal(diag, neg_m, slot, size).then_inc(diag_ready, 1)

            def low_output(g):
                dve.wait_ge(ohi_done, g["g"] + 1)
                dst, src = mixed(hx_lo, g, outs)
                nc.vector.tensor_tensor(dst, src, mixed(hx_hi, g, outs)[0].bitcast(F32),
                                        ALU.subtract).then_inc(o_done, 1)
            maxima(steps[0])
            waiting = []
            for t, step in enumerate(steps):
                if layer == 1:
                    for g in step:
                        dve.wait_ge(sink_exp, g["g"] - len(MLA_GROUPS) + 1)
                        diagonal(sink_diag, sink_e, g["g"] % 4).then_inc(sink_ready, 1)
                if t + 1 < len(steps):
                    maxima(steps[t + 1])
                for g in waiting:
                    low_output(g)
                for g in step:
                    r, width, par = g["r"], g["size"] * P, g["g"] % 2
                    if layer == 0:
                        dve.wait_ge(pv_done, g["b"] + g["keys"])
                    else:
                        dve.wait_ge(o_ready, g["g"] - len(MLA_GROUPS) + 1)
                    link(dve, dve_chain, nc.vector.reciprocal(outs[r:r + 64, par, 0, 0:width],
                                                              ps[64 - r:P - r, 6 + par, 0:width]))
                    nc.vector.tensor_tensor(outs[r:r + 64, par, 1, 0:width], ps[r:r + 64, 6 + par, 0:width],
                                            outs[r:r + 64, par, 0, 0:width], ALU.mult).then_inc(o_scaled, 1)
                waiting = step
            for g in waiting:
                low_output(g)

        def pe_mixer(pe, s):
            if s["layer"] == 1:
                pe.wait_ge(mix_loaded, 16 * (9 + 5))
                for t in range(10):
                    if t >= 4:
                        pe.wait_ge(odd_rope, t - 3)
                    nc.tensor.matmul(ps[:, 4 + t % 4, :], swap_o[:], po[:, t, CTX:T], start=True,
                                     stop=True).then_inc(odd_swap, 1)
                for c in range(CHUNKS):
                    if c >= 4:
                        pe.wait_ge(odd_rope, 10 + c - 3)
                    for j in range(2):
                        ins = nc.tensor.transpose(ps[:, c % 4, j * P:(j + 1) * P], po[:, 10 + j, c * P:(c + 1) * P], ident[:])
                    ins.then_inc(odd_swap, 1)
                pe.wait_ge(odd_rope, 10 + CHUNKS)
                pe_attention(pe, 1)
                pe.wait_ge(o_done, len(MLA_GROUPS) + len(SWA_GROUPS))
                return
            pe.wait_ge(lora_sq, 3)
            for j, (bank, first, last) in enumerate(((0, True, False), (0, False, True), (2, True, True))):
                for h in range(2):
                    ins = nc.tensor.matmul(ps[:, bank + h, 0:TH], ones[:], y[:, j, h * TH:(h + 1) * TH],
                                           start=first, stop=last)
            ins.then_inc(lora_sum, 1)
            pe.wait_ge(mix_loaded, 16 * 9)
            pe.wait_ge(mix_loaded2, 16 * 5)
            pe.wait_ge(lora_ready, 3)
            for i, (kind, h) in enumerate(BUILD):
                pair = i % 4
                if i >= 4:
                    a, d = evacuated(i - 3)
                    pe.wait_ge(built_act, a)
                    pe.wait_ge(built_dve, d)
                if kind == "kr":
                    ins = nc.tensor.matmul(ps[NOPE:MLA_QK, 2 * pair, :], swap_e[NOPE:MLA_QK, :],
                                           pm[NOPE:MLA_QK, PM_GATES, CTX:T], start=True, stop=True)
                elif kind in ("gi", "gf"):
                    for n in range(2):
                        ins = nc.tensor.matmul(ps[0:ROWS, 2 * pair + n, 0:TH], pick_rows[0:32, int(kind == "gf"), :],
                                               pm[0:32, PM_GATES, n * TH:(n + 1) * TH], start=True, stop=True)
                elif kind == "q":
                    for n in range(2):
                        for k in range(2):
                            ins = nc.tensor.matmul(ps[0:MLA_QK, 2 * pair + n, 0:TH],
                                                   w_qb[:, k, h * MLA_QK:(h + 1) * MLA_QK],
                                                   pa[:, k, n * TH:(n + 1) * TH], start=(k == 0), stop=(k == 1))
                elif kind == "k":
                    for n in range(2):
                        ins = nc.tensor.matmul(ps[0:NOPE, 2 * pair + n, 0:KEYS // 2], w_kvb[:, 0, h * 64:(h + 1) * 64],
                                               ckv_keys[:, n * (KEYS // 2):(n + 1) * (KEYS // 2)], start=True, stop=True)
                elif kind == "sw":
                    pe.wait_ge(built_act, evacuated(QPOS[h] + 1)[0])
                    ins = nc.tensor.matmul(ps[NOPE:MLA_QK, 2 * pair, :], swap_e[NOPE:MLA_QK, :],
                                           qh[NOPE:MLA_QK, h, CTX:T], start=True, stop=True)
                else:
                    ins = nc.tensor.matmul(ps[:, 2 * pair, :], ckv_keys[:, h * P:(h + 1) * P], w_kvb[:, 1, :],
                                           start=True, stop=True)
                ins.then_inc(built, 1)
            a, d = evacuated(len(BUILD))
            pe.wait_ge(built_act, a)
            pe.wait_ge(built_dve, d)
            pe_attention(pe, 0)
            pe.wait_ge(o_done, len(MLA_GROUPS))
            for c in range(CHUNKS):
                if c >= 4:
                    pe.wait_ge(turn_act, 2 * (c - 3))
                pair = 2 * (c % 4)
                for j in range(2):
                    ins = nc.tensor.transpose(ps[:, pair, j * P:(j + 1) * P], pm[:, PM_K + j, c * P:(c + 1) * P], ident[:])
                for j in range(M_HEADS):
                    ins = nc.tensor.transpose(ps[:, pair + 1, j * P:(j + 1) * P], pm[:, PM_V + j, c * P:(c + 1) * P], ident[:])
                ins.then_inc(turn_ready, 1)
            pe.wait_ge(turn_act, 2 * CHUNKS)
            pe.wait_ge(rows_ready, 1)
            for c in range(CHUNKS):
                ins = nc.tensor.transpose(ps[:, 0, c * ROWS:(c + 1) * ROWS], rows[0:ROWS, 1, c * P:(c + 1) * P],
                                          ident[0:ROWS, 0:ROWS])
            ins.then_inc(turn_ready, 1)
            pe.wait_ge(turn_act, 2 * CHUNKS + 1)
            pe.wait_ge(mix_loaded3, 32)
            for i in range(2 * M_HEADS):
                h, d = seq_dir(i)
                r = 64 * (h % 2)
                if i >= 1:
                    pe.wait_ge(head_done, i)
                for j, pair in ((0, 0), (1, 2), (2, 3)):
                    flat = pair_flat(pair)
                    for a, b in ((0, 512), (512, T)):
                        ins = nc.tensor.matmul(flat[:, a:b], onehot[0:ROWS, 4 * d + h, :], rows3[0:ROWS, j, a:b],
                                               start=True, stop=True)
                flat = pair_flat(1)
                for c in range(CHUNKS):
                    ins = nc.tensor.matmul(flat[:, c * P:(c + 1) * P], pm[r:r + 64, PM_K + h // 2, c * P:(c + 1) * P],
                                           pm[r:r + 64, PM_Q + h // 2, c * P:(c + 1) * P], start=True, stop=True)
                ins.then_inc(kq_ready, 1)
                pe.wait_ge(weigh_ready, i + 1)
                for j, c in enumerate((0, 1, 2, 3) if d == 0 else (0, 4, 3, 2)):
                    ins = nc.tensor.matmul(pair_flat(2)[r:r + 64, j * 2 * P:(j + 1) * 2 * P], k_w[:, c, :],
                                           vaug[:, c, h, :], start=True, stop=True)
                ins.then_inc(gain_ready, 1)
                pe.wait_ge(state_ready, i + 1)
                for c in range(CHUNKS):
                    cols = slice(c * P, (c + 1) * P)
                    for pair, vs, st in ((0, vaug[:, c, h, 0:P], state[:, c, 0:P]), (1, vaug[:, c, h, P:], state[:, c, P:])):
                        nc.tensor.matmul(pair_flat(pair)[:, cols], vs, weigh[:, cols], start=True, stop=(c == 0))
                        if c > 0:
                            ins = nc.tensor.matmul(pair_flat(pair)[:, cols], st, q_inter[:, h % 2, cols], start=False,
                                                   stop=True)
                ins.then_inc(numden_ready, 1)
            pe.wait_ge(head_done, 2 * M_HEADS)
            for h in range(M_HEADS):
                pe.wait_ge(hm_sq, h + 1)
                for n in range(2):
                    ins = nc.tensor.matmul(ps[:, 2 * h + n, 0:TH], ones[:],
                                           (decay, weigh, g_inter, floor_m)[h][:, n * TH:(n + 1) * TH],
                                           start=True, stop=True)
                ins.then_inc(hm_sum, 1)
            pe.wait_ge(mix_ready, M_HEADS)

        def act_mixer(act, s):
            if s["layer"] == 1:
                for c in range(CHUNKS):
                    act.wait_ge(odd_swap, 10 + c + 1)
                    act.wait_ge(odd_rope, 10 + c)
                    nc.scalar.copy(v_new[:, c, :, 0:3:2, :],
                                   ps[:, c % 4, 0:2 * P].rearrange("p (a e d) -> p a e d", e=2, d=HEAD)).then_inc(odd_rope, 1)
                act_attention(act, 1)
                return
            act.wait_ge(proj_done, 16)
            for j in range(3):
                nc.scalar.activation(y[:, j, :], pa[:, j, :], ACT.Square).then_inc(lora_sq, 1)
            act.wait_ge(lora_sum, 1)
            link(act, act_chain, nc.scalar.activation(halves(y[:, 3, :]), bank_pair(0), ACT.Ln, bias=eps_col[:, 0:1],
                                                      scale=1.0 / Q_LORA))
            link(act, act_chain, nc.scalar.activation(halves(y[:, 4, :]), bank_pair(1), ACT.Ln, bias=eps_col[:, 0:1],
                                                      scale=1.0 / P))
            nc.scalar.activation(y[:, 3:5, :], y[:, 3:5, :], ACT.Exp, scale=-0.5).then_inc(lora_rstd, 1)
            for i, (kind, h) in enumerate(BUILD):
                if kind not in BY_ACT:
                    continue
                act.wait_ge(built, i + 1)
                pair = i % 4
                if kind in ("gi", "gf"):
                    j = int(kind == "gf")
                    ins = nc.scalar.copy(halves(tmp[0:ROWS, j, :]), ps[0:ROWS, 2 * pair:2 * pair + 2, 0:TH])
                elif kind == "q":
                    ins = nc.scalar.copy(halves(qh[0:MLA_QK, h, :]), ps[0:MLA_QK, 2 * pair:2 * pair + 2, 0:TH])
                else:
                    ins = nc.scalar.copy(vtok[:, h, :, 0:3:2, :],
                                         ps[:, 2 * pair, :].rearrange("p (a e d) -> p a e d", e=2, d=MLA_V))
                ins.then_inc(built_act, 1)
            act.wait_ge(out_stored, 32)
            act_attention(act, 0)
            act.wait_ge(o_done, len(MLA_GROUPS))
            act.wait_ge(gate_rows, 1)
            link(act, act_chain, nc.scalar.activation(rows[0:ROWS, 5, :], rows[0:ROWS, 4, :], ACT.Abs))
            link(act, act_chain, nc.scalar.activation(rows[0:ROWS, 5, :], rows[0:ROWS, 5, :], ACT.Exp, scale=-1.0))
            nc.scalar.activation(rows[0:ROWS, 5, :], rows[0:ROWS, 5, :], ACT.Ln, bias=one_col[0:ROWS, 0:1]).then_inc(gate_act, 1)
            for c in range(CHUNKS):
                act.wait_ge(turn_ready, c + 1)
                pair = 2 * (c % 4)
                nc.scalar.copy(ktok[:, c, :], ps[:, pair, 0:2 * P]).then_inc(turn_act, 1)
                nc.scalar.copy(vaug[:, c, :, 0:P], ps[:, pair + 1, :].rearrange("p (h v) -> p h v", v=P)).then_inc(turn_act, 1)
            act.wait_ge(turn_ready, CHUNKS + 1)
            nc.scalar.copy(acol[:].rearrange("p c r -> p (c r)"), ps[:, 0, 0:CHUNKS * ROWS]).then_inc(turn_act, 1)
            for i in range(2 * M_HEADS):
                act.wait_ge(kq_ready, i + 1)
                if i >= 1:
                    act.wait_ge(head_done, i)
                nc.scalar.activation(g_inter[:], pair_flat(2)[:, 0:T], ACT.Exp)
                nc.scalar.activation(floor_m[:], pair_flat(3)[:, 0:T], ACT.Exp).then_inc(gate_act, 1)
                act.wait_ge(decay_arg, i + 1)
                nc.scalar.activation(decay[:], decay[:], ACT.Exp).then_inc(decay_ready, 1)
            act.wait_ge(head_done, 2 * M_HEADS)
            for h in range(M_HEADS):
                nc.scalar.activation((decay, weigh, g_inter, floor_m)[h][:], hm[:, h, :], ACT.Square).then_inc(hm_sq, 1)
            for h in range(M_HEADS):
                act.wait_ge(hm_sum, h + 1)
                out = (decay, weigh, g_inter, floor_m)[h][:]
                link(act, act_chain, nc.scalar.activation(halves(out), bank_pair(h), ACT.Ln, bias=eps_col[:, 0:1],
                                                          scale=1.0 / M_DV))
                nc.scalar.activation(out, out, ACT.Exp, scale=-0.5).then_inc(hm_rstd, 1)
            for h in range(M_HEADS):
                act.wait_ge(hm_f, h + 1)
                nc.scalar.copy(hx_hi[:, 4 + h, :], hm[:, h, :]).then_inc(hm_hi, 1)

        def dve_mixer(dve, s):
            if s["layer"] == 1:
                dve.wait_ge(proj_done, 16 + 12)
                dve.wait_ge(mix_loaded, 16 * (9 + 5))
                for t in range(10):
                    dve.wait_ge(odd_swap, t + 1)
                    nc.vector.tensor_tensor(turned[:, t % 2, :], ps[:, 4 + t % 4, :], rope_o[:, 1, :], ALU.mult)
                    link(dve, dve_chain, nc.vector.tensor_tensor(po[:, t, CTX:T], po[:, t, CTX:T], rope_o[:, 0, :], ALU.mult))
                    nc.vector.tensor_tensor(po[:, t, CTX:T], po[:, t, CTX:T], turned[:, t % 2, :],
                                            ALU.add).then_inc(odd_rope, 1)
                nc.vector.memset(v_new[:, :, :, 1, :], 1.0)
                nc.vector.memset(v_old[:, :, :, 1, :], 1.0)
                dve_attention(dve, 1)
                return
            nc.vector.memset(vtok[:, :, :, 1, :], 1.0)
            dve.wait_ge(lora_rstd, 1)
            for j in range(2):
                nc.vector.scalar_tensor_tensor(out=pa[:, j, :], in0=pa[:, j, :], scalar=gains[:, j:j + 1],
                                               in1=y[:, 3, :], op0=ALU.mult, op1=ALU.mult).then_inc(lora_ready, 1)
            nc.vector.scalar_tensor_tensor(out=ckv_keys[:, 0:CTX], in0=pa[:, 2, 0:CTX], scalar=gains[:, 2:3],
                                           in1=y[:, 4, 0:CTX], op0=ALU.mult, op1=ALU.mult)
            nc.vector.scalar_tensor_tensor(out=ckv_keys[:, CTX + PAST:KEYS], in0=pa[:, 2, CTX:T], scalar=gains[:, 2:3],
                                           in1=y[:, 4, CTX:T], op0=ALU.mult, op1=ALU.mult).then_inc(lora_ready, 1)
            dve.wait_ge(mix_loaded2, 16 * 5)
            rr = slice(NOPE, MLA_QK)

            def rotate(x, swapped, scratch):
                nc.vector.tensor_tensor(y[rr, scratch, 0:LAT], swapped, rope_e[rr, 1, :], ALU.mult)
                link(dve, dve_chain, nc.vector.tensor_tensor(x, x, rope_e[rr, 0, :], ALU.mult))
                return nc.vector.tensor_tensor(x, x, y[rr, scratch, 0:LAT], ALU.add)
            for i, (kind, h) in enumerate(BUILD):
                if kind in BY_ACT:
                    continue
                dve.wait_ge(built, i + 1)
                pair = i % 4
                if kind == "kr":
                    link(dve, dve_chain, rotate(pm[rr, PM_GATES, CTX:T], ps[rr, 2 * pair, :], 0))
                    for hh in range(MLA_HEADS):
                        nc.vector.tensor_copy(kh[rr, hh, 0:CTX], pm[rr, PM_GATES, 0:CTX])
                        ins = nc.vector.tensor_copy(kh[rr, hh, CTX + PAST:KEYS], pm[rr, PM_GATES, CTX:T])
                elif kind == "k":
                    ins = nc.vector.tensor_copy(kh[0:NOPE, h, :].rearrange("p (n t) -> p n t", n=2),
                                                ps[0:NOPE, 2 * pair:2 * pair + 2, 0:KEYS // 2])
                else:
                    ins = rotate(qh[rr, h, CTX:T], ps[rr, 2 * pair, :], 1 + h % 2)
                ins.then_inc(built_dve, 1)
            dve.wait_ge(out_stored, 32)
            dve_attention(dve, 0)
            dve.wait_ge(o_done, len(MLA_GROUPS))
            R = slice(0, ROWS)
            B, A, M, G, F, SCR = range(6)
            nc.vector.tensor_scalar(rows[R, F, :], tmp[R, 1, :], row_bias[R, 1:2], None, ALU.add).then_inc(gate_rows, 1)
            link(dve, dve_chain, nc.vector.tensor_scalar(rows[R, A, :], tmp[R, 0, :], row_bias[R, 0:1], None, ALU.add))
            nc.vector.memset(vaug[:, :, :, P:], 1.0)
            nc.vector.memset(q_inter[:], 0.0)
            nc.vector.memset(m_in[:], 0.0)
            nc.vector.memset(rows[R, B, :], 0.0)
            nc.vector.memset(rows[R, M, :], 0.0)
            nc.vector.memset(state[:], 0.0)
            dve.wait_ge(gate_act, 1)
            link(dve, dve_chain, nc.vector.scalar_tensor_tensor(out=rows[R, F, :], in0=rows[R, F, :], scalar=0.0,
                                                                in1=rows[R, SCR, :], op0=ALU.min, op1=ALU.subtract))

            def seen(row, d, c):
                if d == 0:
                    return rows[0:M_HEADS, row, c * P:(c + 1) * P], rows[0:M_HEADS, row, (c + 1) * P - 1:(c + 1) * P]
                part = rows[32:32 + M_HEADS, row, c * P:(c + 1) * P]
                return part[:, ::-1], rows[32:32 + M_HEADS, row, c * P:c * P + 1]
            for d in range(2):
                for c in range(CHUNKS):
                    f = seen(F, d, c)[0]
                    ins = nc.vector.tensor_tensor_scan(out=seen(B, d, c)[0], data0=f, data1=seen(M, d, c)[0],
                                                       initial=0.0, op0=ALU.add, op1=ALU.add)
            link(dve, dve_chain, ins)
            nc.vector.tensor_tensor(rows[R, A, :], rows[R, A, :], rows[R, B, :], ALU.subtract)
            nc.vector.tensor_copy(m_in[0:M_HEADS, 1:2], row_bias[0:M_HEADS, 2:3])
            link(dve, dve_chain, nc.vector.tensor_copy(m_in[32:32 + M_HEADS, 4:5], row_bias[32:32 + M_HEADS, 2:3]))
            for step in range(5):
                for d, order in ((0, (1, 2, 3, 4, 0)), (1, (4, 3, 2, 1, 0))):
                    c = order[step]
                    r = slice(32 * d, 32 * d + M_HEADS)
                    a = seen(A, d, c)[0]
                    ins = nc.vector.tensor_tensor_scan(out=seen(M, d, c)[0], data0=a, data1=a,
                                                       initial=m_in[r, c:c + 1], op0=ALU.max, op1=ALU.max)
                link(dve, dve_chain, ins)
                for d, order in ((0, (2, 3, 4, 7, 6)), (1, (3, 2, 1, 7, 6))):
                    c = ((1, 2, 3, 4, 0), (4, 3, 2, 1, 0))[d][step]
                    to = order[step]
                    r = slice(32 * d, 32 * d + M_HEADS)
                    ins = nc.vector.tensor_tensor(m_in[r, to:to + 1], seen(B, d, c)[1], seen(M, d, c)[1], ALU.add)
                link(dve, dve_chain, ins)
            nc.vector.tensor_scalar(rows3[R, 0, :], rows[R, M, :], -1.0, None, ALU.mult)
            for c in range(CHUNKS):
                nc.vector.tensor_scalar(rows3[R, 1, c * P:(c + 1) * P], rows[R, M, c * P:(c + 1) * P], -1.0,
                                        m_in[R, c:c + 1], ALU.mult, ALU.add)
            nc.vector.scalar_tensor_tensor(out=rows3[R, 2, :], in0=rows[R, B, :], scalar=-1.0, in1=rows[R, M, :],
                                           op0=ALU.mult, op1=ALU.subtract).then_inc(rows_ready, 1)
            dve.wait_ge(turn_act, 2 * CHUNKS + 1)
            dve.wait_ge(mix_loaded3, 32)
            for i in range(2 * M_HEADS):
                h, d = seq_dir(i)
                r = 64 * (h % 2)
                rs = slice(r, r + 64)
                row = 32 * d + h
                dve.wait_ge(kq_ready, i + 1)
                for c in range(CHUNKS):
                    cols = slice(c * P, (c + 1) * P)
                    ins = nc.vector.scalar_tensor_tensor(out=decay[:, cols], in0=pair_flat(0)[:, cols],
                                                         scalar=acol[:, c, row:row + 1], in1=causal[:, d, :],
                                                         op0=ALU.add, op1=ALU.add)
                ins.then_inc(decay_arg, 1)
                dve.wait_ge(gate_act, 1 + i + 1)
                nc.vector.tensor_tensor(q_inter[rs, h % 2, :], pm[rs, PM_Q + h // 2, :], g_inter[rs, :], ALU.mult)
                dve.wait_ge(decay_ready, i + 1)
                nc.vector.scalar_tensor_tensor(out=weigh[:], in0=pair_flat(1)[:, 0:T], scalar=M_DK ** -0.5,
                                               in1=decay[:], op0=ALU.mult, op1=ALU.mult)
                for c in range(CHUNKS):
                    last = (c + 1) * P - 1 if d == 0 else c * P
                    ins = nc.vector.tensor_scalar(k_w[:, c, :], ktok[:, c, h * M_DK:(h + 1) * M_DK],
                                                  decay[:, last:last + 1], M_DK ** -0.5, ALU.mult, ALU.mult)
                ins.then_inc(weigh_ready, 1)
                order = (1, 2, 3, 4) if d == 0 else (4, 3, 2, 1)
                nc.vector.tensor_copy(state[rs, order[0], :], state0[rs, d, h // 2, :]).then_inc(dve_chain, 1)
                chained[dve_chain.name] += 1
                dve.wait_ge(dve_chain, chained[dve_chain.name])
                dve.wait_ge(gain_ready, i + 1)
                nc.vector.tensor_copy(state_out[rs, d, h // 2, :], pair_flat(2)[rs, 0:2 * P])
                for j in range(3):
                    c, nxt = order[j], order[j + 1]
                    last = (c + 1) * P - 1 if d == 0 else c * P
                    ins = nc.vector.scalar_tensor_tensor(out=state[rs, nxt, :], in0=state[rs, c, :],
                                                         scalar=g_inter[rs, last:last + 1],
                                                         in1=pair_flat(2)[rs, (j + 1) * 2 * P:(j + 2) * 2 * P],
                                                         op0=ALU.mult, op1=ALU.add)
                    if j < 2:
                        link(dve, dve_chain, ins)
                ins.then_inc(state_ready, 1)
                dve.wait_ge(numden_ready, i + 1)
                link(dve, dve_chain, nc.vector.tensor_tensor(hs[:], pair_flat(1)[:, 0:T], floor_m[:], ALU.max))
                link(dve, dve_chain, nc.vector.scalar_tensor_tensor(out=hs[:], in0=pair_flat(1)[:, 0:T], scalar=-1.0,
                                                                    in1=hs[:], op0=ALU.mult, op1=ALU.max))
                link(dve, dve_chain, nc.vector.reciprocal(hs[:], hs[:]))
                if d == 0:
                    nc.vector.tensor_tensor(hm[:, h, :], pair_flat(0)[:, 0:T], hs[:], ALU.mult).then_inc(head_done, 1)
                else:
                    link(dve, dve_chain, nc.vector.tensor_tensor(hs[:], pair_flat(0)[:, 0:T], hs[:], ALU.mult))
                    nc.vector.tensor_tensor(hm[:, h, :], hm[:, h, :], hs[:], ALU.add).then_inc(head_done, 1)
            for h in range(M_HEADS):
                dve.wait_ge(hm_rstd, h + 1)
                link(dve, dve_chain, nc.vector.scalar_tensor_tensor(
                    out=hm[:, h, :], in0=hm[:, h, :], scalar=gains[:, 3 + h:4 + h],
                    in1=(decay, weigh, g_inter, floor_m)[h][:], op0=ALU.mult, op1=ALU.mult))
                nc.vector.tensor_tensor(hm[:, h, :], hm[:, h, :], pm[:, PM_O + h, :], ALU.mult).then_inc(hm_f, 1)
            for h in range(M_HEADS):
                dve.wait_ge(hm_hi, h + 1)
                nc.vector.tensor_tensor(hx_lo[:, 4 + h, :], hm[:, h, :], hx_hi[:, 4 + h, :].bitcast(F32),
                                        ALU.subtract).then_inc(mix_ready, 1)

        def sp_mixer_loads(sp, s):
            sp.wait_ge(w_used, s["chunk"])
            if s["layer"] == 0:
                sp.dma_start(w_qb[:], io["w_qb"]).then_inc(mix_loaded, 16)
                for h in range(MLA_HEADS):
                    sp.dma_start(kh[NOPE:MLA_QK, h, CTX:CTX + PAST], io["krope_old"]).then_inc(mix_loaded, 16)
            else:
                for e in range(2):
                    sp.dma_start(v_old[:, :, :, 2 * e, :], io["v_old"][:, e]).then_inc(mix_loaded, 16)
                for dst, name in ((k_old, "k_old"), (rope_o, "rope_o"), (swap_o, "swap_o")):
                    sp.dma_start(dst[:], io[name]).then_inc(mix_loaded, 16)

        def sp_mixer_loads2(sp, s):
            sp.wait_ge(w_used, s["chunk"] + 2 * s["tiles_in"])
            if s["layer"] == 0:
                for dst, name in ((rope_e, "rope_e"), (swap_e, "swap_e"), (pick_rows, "pick_rows"), (w_kvb, "w_kvb")):
                    sp.dma_start(dst[:], io[name]).then_inc(mix_loaded2, 16)
                sp.dma_start(ckv_keys[:, CTX:CTX + PAST], io["ckv_old"]).then_inc(mix_loaded2, 16)
                sp.wait_ge(lora_ready, 3)
                sp.dma_start(io["out_ckv"], ckv_keys[:, 0:CTX]).then_inc(out_stored, 16)
                sp.dma_start(io["out_krope"], pm[NOPE:MLA_QK, PM_GATES, 0:CTX]).then_inc(out_stored, 16)
                sp.wait_ge(o_done, len(MLA_GROUPS))
                sp.dma_start(onehot[0:ROWS], io["onehot"]).then_inc(mix_loaded3, 16)
                sp.dma_start(state0[:], io["state0"]).then_inc(mix_loaded3, 16)
                sp.wait_ge(head_done, 8)
                sp.dma_start(io["out_state"], state_out[:]).then_inc(out_stored, 16)
                sp.dma_start(io["out_m"], m_in[0:ROWS, 6:7]).then_inc(out_stored, 16)
            else:
                sp.wait_ge(proj_done, 16 + 12)
                sp.dma_start(io["out_kv"], po[:, 8:12, 0:CTX]).then_inc(out_stored, 16)

        @block.sync
        def _(sp):
            for dst, name in ((cond, "cond"), (norm_g, "norm_g"), (ada_bias, "ada_b"), (pick, "pick"),
                              (neg_sink[:, 0:S_HEADS], "sinks"), (gains, "gains"), (row_bias, "row_bias"), (ident, "ident"),
                              (causal, "causal")):
                sp.dma_start(dst if name == "sinks" else dst[:], io[name]).then_inc(in_loaded, 16)

            def load(c, slot, src, tiles, wait=True):
                if wait:
                    sp.wait_ge(lo_done, c - 1)
                sp.dma_start(w_raw[:, slot, 0:tiles * P], src).then_inc(raw_ready[slot], 16)

            for q in range(ADA_SLOTS):
                sp.dma_start(ada_raw[:, q], ada_w[q]).then_inc(ada_loaded[q], 16)
            for k in range(KT):
                sp.dma_start(xT[:, k, :], io["x"][:, k, :]).then_inc(x_loaded, 16)
            with sp.Fori(1, ADA_GROUPS // ADA_SLOTS) as i:
                for q in range(ADA_SLOTS):
                    sp.wait_ge(ada_lo_done, 8 * i + (2 * q - 6))
                    sp.dma_start(ada_raw[:, q], ada_w[4 * i + q]).then_inc(ada_loaded[q], 16)
            chunk = 0
            for s in SUBS:
                if s["kind"] == "ffn":
                    f = s["f"]
                    if chunk == 0:
                        for q in range(2):
                            load(q, q, ffn_gu[f, 0, q], 8, wait=False)
                    with sp.Fori(int(chunk == 0), FT) as b:
                        for q in range(2):
                            load(2 * b + (chunk + q), q, ffn_gu[f, b, q], 8)
                    chunk += 2 * FT
                    with sp.Fori(0, KT) as b:
                        for q in range(2):
                            load(2 * b + (chunk + q), q, ffn_dn[f, b, q], 11)
                    chunk += 2 * KT
                else:
                    name = ("even", "odd")[s["layer"]]
                    sp_mixer_loads(sp, s)
                    with sp.Fori(0, s["tiles_in"]) as b:
                        for q in range(2):
                            load(2 * b + (chunk + q), q, io[name + "_in"][2 * b + q], 8)
                    chunk += 2 * s["tiles_in"]
                    for q in range(2):
                        load(chunk + q, q, io[name + "_out"][q], 8)
                    sp_mixer_loads2(sp, s)
                    with sp.Fori(1, KT // 2) as b:
                        for q in range(2):
                            load(2 * b + (chunk + q), q, io[name + "_out"][2 * b + q], 8)
                    chunk += KT
            for k in range(KT):
                sp.wait_ge(x_ready, KT * (len(SUBS) - 1) + k + 1)
                sp.dma_start(io["y"][:, k, :], xT[:, k, :]).then_inc(out_stored, 16)
            sp.wait_ge(out_stored, 16 * (KT + N_OUT))

        @block.scalar
        def _(act):
            act.wait_ge(in_loaded, CONSTS)
            act.wait_ge(const_ready, 1)
            nc.scalar.copy(ones_r[:], ones[:]).then_inc(attn_const, 1)
            nc.scalar.copy(ident_b[:], ident[:]).then_inc(attn_const, 1)
            for i in range(4):
                nc.scalar.copy(causal_b[:, :, i, :], causal[:]).then_inc(attn_const, 1)
            nc.scalar.activation(cond_silu[:], cond[:], ACT.Silu).then_inc(cond_act, 1)
            act.wait_ge(cond_act, 1)
            act.wait_ge(cond_ready, 1)
            nc.scalar.copy(cond_hl[:, :, 0:2], cond_silu[:]).then_inc(cond_act, 1)

            def ada_split(g, q, peeled=False):
                act.wait_ge(ada_loaded[q], 16 if peeled else 4 * g + (16 - 4 * q))
                if not (peeled and q < 2):
                    act.wait_ge(ada_used, g - 1)
                for e in range(2):
                    ks = slice(4 * e, 4 * e + 4)
                    nc.scalar.copy(ada_hi[:, q % 2, ks, :], ada_raw[:, q, ks, :]).then_inc(ada_hi_done, 1)

            def ada_rows(g, q, peeled=False):
                act.wait_ge(ada_used, g + 1)
                if not (peeled and q < 2):
                    act.wait_ge(col_ready, g - 1)
                nc.scalar.copy(mod_rows[:, q % 2, :], ps[:, q % 2, :]).then_inc(row_ready, 1)
            for q in range(ADA_SLOTS):
                ada_split(q, q, peeled=True)
                if q:
                    ada_rows(q - 1, q - 1, peeled=True)
            with act.Fori(1, ADA_GROUPS // ADA_SLOTS) as i:
                for q in range(ADA_SLOTS):
                    ada_split(4 * i + q, q)
                    ada_rows(4 * i + (q - 1), (q - 1) % 4)
            ada_rows(ADA_GROUPS - 1, 3)
            for q in range(2):
                split_hi(act, q, q, 8, wait_used=False)

            chunk = 0
            n_rstd = 0
            for si, s in enumerate(SUBS):
                n = si

                def rms(count, sums, value):
                    act.wait_ge(sums, value)
                    link(act, act_chain, nc.scalar.activation(halves(rstd[:]), bank_pair(0), ACT.Ln,
                                                              bias=eps_col[:, 0:1], scale=1.0 / D))
                    nc.scalar.activation(rstd[:], rstd[:], ACT.Exp, scale=-0.5).then_inc(rstd_ready, 1)

                def squares(n):
                    for k in range(KT):
                        if n == 0:
                            act.wait_ge(x_loaded, 16 * KT)
                        else:
                            act.wait_ge(x_ready, KT * (n - 1) + k + 1)
                        if KT * n + k >= 2:
                            act.wait_ge(xsq_used, KT * n + k - 1)
                        nc.scalar.activation(tmp[:, k % 2, :], xT[:, k, :], ACT.Square).then_inc(xsq_ready, 1)

                squares(n)
                rms(2 * n, xsq_used, KT * (n + 1))
                for k in range(KT):
                    act.wait_ge(pre_ready, KT * n + k + 1)
                    for ci, (a, b) in enumerate(GROUPS):
                        last = nc.scalar.activation(hx_hi[:, k, a:b], tmp[:, k % 2, a:b], ACT.Identity,
                                                    bias=mod_col(s["layer"], s["idx"], k, ci))
                    last.then_inc(hxhi_ready, 1)
                if s["kind"] == "ffn":
                    g0 = s["gu0"]

                    def gu_block(m, par, next_tiles, chunk=chunk, g0=g0):
                        for q in (2, 3):
                            split_hi(act, 2 * m + (chunk + q), q % 2, next_tiles)
                        act.wait_ge(w_used, 2 * m + (chunk + 2))
                        nc.scalar.activation(halves(silu_g[:, par, :]), bank_pair(2 * par),
                                             ACT.Silu).then_inc(silu_done, 1)
                        act.wait_ge(mul_done, m + (g0 + 1))
                        nc.scalar.copy(halves(hh_hi[:, m, :]), bank_pair(2 * par + 1)).then_inc(hhi_done, 1)
                    with act.Fori(0, FT // 2 - 1) as i:
                        for par in range(2):
                            gu_block(2 * i + par, par, 8)
                    gu_block(FT - 2, 0, 8)
                    gu_block(FT - 1, 1, 11)
                    chunk += 2 * FT

                    def dn_block(b, par, next_tiles, chunk=chunk, n=n):
                        if next_tiles:
                            for q in (2, 3):
                                split_hi(act, 2 * b + (chunk + q), q % 2, next_tiles)
                        act.wait_ge(w_used, 2 * b + (chunk + 2))
                        nc.scalar.copy(halves(y[:, b, :]), bank_pair(2 * par))
                        act.wait_ge(ssq_done, b + ((KT + 1) * n + 1))
                        nc.scalar.activation(halves(sq[:, par, :]), bank_pair(2 * par),
                                             ACT.Square).then_inc(sq_ready, 1)
                    with act.Fori(0, KT // 2 - 1) as i:
                        for par in range(2):
                            dn_block(2 * i + par, par, 11)
                    dn_block(KT - 2, 0, 11)
                    dn_block(KT - 1, 1, 8 if si + 1 < len(SUBS) else 0)
                    chunk += 2 * KT
                else:
                    nblk = s["tiles_in"]
                    for b in range(nblk):
                        for q in (2, 3):
                            split_hi(act, 2 * b + chunk + q, q % 2, 8)
                        for q in range(2):
                            t = 2 * b + q
                            act.wait_ge(w_used, chunk + t + 1)
                            func, out = ACT.Copy, None
                            if s["layer"] == 1:
                                out = po[:, t, :]
                            elif t < 3:
                                out = pa[:, t, :]
                            else:
                                out = pm[:, t - 3, :]
                                func = ACT.Sigmoid if t - 3 >= PM_O else ACT.Copy
                            nc.scalar.activation(halves(out), bank_pair(2 * (b % 2) + q), func).then_inc(proj_done, 1)
                    chunk += 2 * nblk
                    act_mixer(act, s)
                    act.wait_ge(out_stored, 16 * (4 + s["layer"]))
                    for b in range(KT // 2):
                        if b < KT // 2 - 1 or si + 1 < len(SUBS):
                            for q in (2, 3):
                                split_hi(act, 2 * b + chunk + q, q % 2, 8)
                        for q in range(2):
                            t = 2 * b + q
                            act.wait_ge(w_used, chunk + t + 1)
                            nc.scalar.copy(halves(y_m[:, t, :]), bank_pair(2 * (b % 2) + q))
                            act.wait_ge(ssq_done, t + ((KT + 1) * n + 1))
                            nc.scalar.activation(halves(sq_m[:, t % 2, :]), bank_pair(2 * (b % 2) + q),
                                                 ACT.Square).then_inc(sq_ready, 1)
                    chunk += KT
                rms(2 * n + 1, msq_ready, n + 1)

        @block.vector
        def _(dve):
            nc.vector.memset(cond_hl[:].bitcast(F32), 0.0).then_inc(cond_ready, 1)
            nc.vector.memset(ones[:], 1.0).then_inc(const_ready, 1)
            nc.vector.memset(eps_col[:], EPS).then_inc(const_ready, 1)
            nc.vector.memset(sink_half[:], 0.0).then_inc(dve_chain, 1)
            chained[dve_chain.name] = 1
            dve.wait_ge(dve_chain, 1)
            nc.vector.memset(sink_half[:, 1, :], 1.0)
            nc.vector.memset(one_col[:], 1.0).then_inc(const_ready, 1)
            dve.wait_ge(cond_act, 2)
            nc.vector.tensor_tensor(cond_hl[:, :, 2:4], cond_silu[:], cond_hl[:, :, 0:2].bitcast(F32),
                                    ALU.subtract).then_inc(cond_ready, 1)

            def ada_split(g, q):
                for e in range(2):
                    dve.wait_ge(ada_hi_done, 2 * g + (e + 1))
                    ks = slice(4 * e, 4 * e + 4)
                    nc.vector.tensor_tensor(ada_lo[:, q % 2, ks, :], ada_raw[:, q, ks, :],
                                            ada_hi[:, q % 2, ks, :].bitcast(F32), ALU.subtract).then_inc(ada_lo_done, 1)

            def ada_add(g, q):
                dve.wait_ge(col_ready, g + 1)
                cols = ps[:, 2 + q % 2, 0:8].rearrange("p (j c) -> p j c", c=2)
                nc.vector.tensor_tensor(mods[:, bass.ds(4 * g, 4), :], cols, ada_bias[:, bass.ds(4 * g, 4), :],
                                        ALU.add).then_inc(mod_added, 1)
            dve.wait_ge(in_loaded, CONSTS)
            for q in range(ADA_SLOTS):
                ada_split(q, q)
                if q >= 2:
                    ada_add(q - 2, q)
            with dve.Fori(1, ADA_GROUPS // ADA_SLOTS) as i:
                for q in range(ADA_SLOTS):
                    ada_split(4 * i + q, q)
                    ada_add(4 * i + (q - 2), q)
            for q in range(2):
                ada_add(ADA_GROUPS - 2 + q, q)
            for q in range(2):
                split_lo(dve, q, q, 8, wait_used=False)
            dve.wait_ge(mod_added, ADA_GROUPS)
            nc.vector.tensor_scalar(neg_sink[:, S_HEADS:], neg_sink[:, 0:S_HEADS], -HEAD ** 0.5, None, ALU.mult)
            for layer in range(2):
                for sub in range(3):
                    for ci in range(2):
                        j = (layer * NMOD + 3 * sub + 1) * KT
                        last = nc.vector.scalar_tensor_tensor(out=mods[:, j:j + KT, ci], in0=mods[:, j:j + KT, ci],
                                                              scalar=1.0, in1=norm_g[:, layer, 2 * sub, :],
                                                              op0=ALU.add, op1=ALU.mult)
                        j += KT
                        last = nc.vector.scalar_tensor_tensor(out=mods[:, j:j + KT, ci], in0=mods[:, j:j + KT, ci],
                                                              scalar=1.0 if sub == 1 else 0.5,
                                                              in1=norm_g[:, layer, 2 * sub + 1, :],
                                                              op0=ALU.mult, op1=ALU.mult)
            last.then_inc(mods_ready, 1)
            dve.wait_ge(mods_ready, 1)

            chunk = 0
            for si, s in enumerate(SUBS):
                n = si
                dve.wait_ge(rstd_ready, 2 * n + 1)

                def scaled(k):
                    if k >= 2:
                        dve.wait_ge(hx_ready, KT * n + k - 1)
                    for ci, (a, b) in enumerate(GROUPS):
                        last = nc.vector.scalar_tensor_tensor(out=tmp[:, k % 2, a:b], in0=xT[:, k, a:b],
                                                              scalar=mod_col(s["layer"], s["idx"] + 1, k, ci),
                                                              in1=rstd[:, a:b], op0=ALU.mult, op1=ALU.mult)
                    last.then_inc(pre_ready, 1)

                def low(k):
                    dve.wait_ge(hxhi_ready, KT * n + k + 1)
                    for ci, (a, b) in enumerate(GROUPS):
                        last = nc.vector.scalar_tensor_tensor(out=hx_lo[:, k, a:b], in0=tmp[:, k % 2, a:b],
                                                              scalar=mod_col(s["layer"], s["idx"], k, ci),
                                                              in1=hx_hi[:, k, a:b].bitcast(F32), op0=ALU.add,
                                                              op1=ALU.subtract)
                    last.then_inc(hx_ready, 1)
                scaled(0)
                for k in range(1, KT):
                    scaled(k)
                    low(k - 1)
                low(KT - 1)
                if s["kind"] == "ffn":
                    g0 = s["gu0"]

                    def gu_block(m, par, next_tiles, chunk=chunk, g0=g0):
                        for q in (2, 3):
                            split_lo(dve, 2 * m + (chunk + q), q % 2, next_tiles)
                        dve.wait_ge(silu_done, m + (g0 + 1))
                        nc.vector.tensor_tensor(bank_pair(2 * par + 1), bank_pair(2 * par + 1),
                                                halves(silu_g[:, par, :]), ALU.mult).then_inc(mul_done, 1)
                        dve.wait_ge(hhi_done, m + (g0 + 1))
                        nc.vector.tensor_tensor(halves(hh_lo[:, m, :]), bank_pair(2 * par + 1),
                                                halves(hh_hi[:, m, :]).bitcast(F32),
                                                ALU.subtract).then_inc(block_free, 1)
                    with dve.Fori(0, FT // 2 - 1) as i:
                        for par in range(2):
                            gu_block(2 * i + par, par, 8)
                    gu_block(FT - 2, 0, 8)
                    gu_block(FT - 1, 1, 11)
                    chunk += 2 * FT
                    nc.vector.memset(ssq[:], 0.0).then_inc(ssq_done, 1)

                    def dn_block(b, par, next_tiles, chunk=chunk, n=n):
                        if next_tiles:
                            for q in (2, 3):
                                split_lo(dve, 2 * b + (chunk + q), q % 2, next_tiles)
                        dve.wait_ge(sq_ready, b + (KT * n + 1))
                        dve.wait_ge(ssq_done, b + ((KT + 1) * n + 1))
                        nc.vector.tensor_tensor(ssq[:], ssq[:], sq[:, par, :], ALU.add).then_inc(ssq_done, 1)
                    with dve.Fori(0, KT // 2 - 1) as i:
                        for par in range(2):
                            dn_block(2 * i + par, par, 11)
                    dn_block(KT - 2, 0, 11)
                    dn_block(KT - 1, 1, 8 if si + 1 < len(SUBS) else 0)
                    chunk += 2 * KT
                else:
                    nblk = s["tiles_in"]
                    for b in range(nblk):
                        for q in (2, 3):
                            split_lo(dve, 2 * b + chunk + q, q % 2, 8)
                    chunk += 2 * nblk
                    dve_mixer(dve, s)
                    for b in range(KT // 2):
                        if b < KT // 2 - 1 or si + 1 < len(SUBS):
                            for q in (2, 3):
                                split_lo(dve, 2 * b + chunk + q, q % 2, 8)
                        if b == 0:
                            dve.wait_ge(out_stored, 16 * (4 + s["layer"]))
                            nc.vector.memset(ssq_m[:], 0.0).then_inc(ssq_done, 1)
                        for q in range(2):
                            t = 2 * b + q
                            dve.wait_ge(sq_ready, KT * n + t + 1)
                            dve.wait_ge(ssq_done, t + ((KT + 1) * n + 1))
                            nc.vector.tensor_tensor(ssq_m[:], ssq_m[:], sq_m[:, t % 2, :], ALU.add).then_inc(ssq_done, 1)
                    chunk += KT
                yb = y if s["kind"] == "ffn" else y_m
                dve.wait_ge(rstd_ready, 2 * n + 2)

                def gated(k):
                    for ci, (a, b) in enumerate(GROUPS):
                        last = nc.vector.scalar_tensor_tensor(out=yb[:, k, a:b], in0=yb[:, k, a:b],
                                                              scalar=mod_col(s["layer"], s["idx"] + 2, k, ci),
                                                              in1=rstd[:, a:b], op0=ALU.mult, op1=ALU.mult)
                    last.then_inc(y_scaled, 1)

                def added(k):
                    dve.wait_ge(y_scaled, KT * n + k + 1)
                    nc.vector.tensor_tensor(xT[:, k, :], xT[:, k, :], yb[:, k, :], ALU.add).then_inc(x_ready, 1)
                gated(0)
                for k in range(1, KT):
                    gated(k)
                    added(k - 1)
                added(KT - 1)

        @block.tensor
        def _(pe):
            pe.wait_ge(const_ready, 2)
            pe.wait_ge(cond_ready, 2)

            def ada_products(g, q, peeled=False):
                if not (peeled and q < 2):
                    pe.wait_ge(row_ready, g - 1)
                for k in range(KT):
                    if k % 4 == 0:
                        pe.wait_ge(ada_lo_done, 2 * g + (k // 4 + 1))
                    for part in (ada_hi, ada_lo):
                        last = nc.tensor.matmul(ps[:, q % 2, :], cond_hl[:, k, :], part[:, q % 2, k, :],
                                                start=(k == 0 and part is ada_hi),
                                                stop=(k == KT - 1 and part is ada_lo))
                last.then_inc(ada_used, 1)

            def ada_columns(g, q, peeled=False):
                pe.wait_ge(row_ready, g + 1)
                if not (peeled and q < 2):
                    pe.wait_ge(mod_added, g - 1)
                for j in range(4):
                    last = nc.tensor.matmul(ps[:, 2 + q % 2, 2 * j:2 * j + 2], mod_rows[:, q % 2, j * P:(j + 1) * P],
                                            pick[:], start=True, stop=True)
                last.then_inc(col_ready, 1)
            for q in range(ADA_SLOTS):
                ada_products(q, q, peeled=True)
                if q:
                    ada_columns(q - 1, q - 1, peeled=True)
            with pe.Fori(1, ADA_GROUPS // ADA_SLOTS) as i:
                for q in range(ADA_SLOTS):
                    ada_products(4 * i + q, q)
                    ada_columns(4 * i + (q - 1), (q - 1) % 4)
            ada_columns(ADA_GROUPS - 1, 3)
            pe.wait_ge(mod_added, ADA_GROUPS)

            def product(out_bank, q, hi, lo, k0, tiles, first, last_chunk, wait_k=None):
                for t in range(tiles):
                    if wait_k is not None:
                        pe.wait_ge(hx_ready, wait_k + t + 1)
                    wh = w_hi[:, q, t * P:(t + 1) * P]
                    wl = w_lo[:, q, t * P:(t + 1) * P]
                    k = k0 + t
                    for w, a in ((wh, hi), (wh, lo), (wl, hi)):
                        for h in range(2):
                            last = nc.tensor.matmul(ps[:, out_bank + h, 0:TH], w, a[:, k, h * TH:(h + 1) * TH],
                                                    start=(first and t == 0 and w is wh and a is hi),
                                                    stop=(last_chunk and t == tiles - 1 and w is wl))
                last.then_inc(w_used, 1)

            chunk = 0
            n_free = 0
            for si, s in enumerate(SUBS):
                n = si
                for k in range(KT):
                    pe.wait_ge(xsq_ready, KT * n + k + 1)
                    for h in range(2):
                        last = nc.tensor.matmul(ps[:, h, 0:TH], ones[:], tmp[:, k % 2, h * TH:(h + 1) * TH],
                                                start=(k == 0), stop=(k == KT - 1))
                    last.then_inc(xsq_used, 1)
                pe.wait_ge(rstd_ready, 2 * n + 1)
                if s["kind"] == "ffn":
                    g0 = s["gu0"]

                    def gu_block(m, par, wait_free=True, chunk=chunk, g0=g0, n=n):
                        for q in range(2):
                            pe.wait_ge(lo_done, 2 * m + (chunk + q + 1))
                            if q == 0 and wait_free:
                                pe.wait_ge(block_free, m + (g0 - 1))
                            product(4 * par + 2 * q, q, hx_hi, hx_lo, 0, 8, True, True,
                                    wait_k=KT * n if not wait_free else None)
                    gu_block(0, 0, wait_free=False)
                    gu_block(1, 1, wait_free=False)
                    with pe.Fori(1, FT // 2) as i:
                        for par in range(2):
                            gu_block(2 * i + par, par)
                    chunk += 2 * FT
                    pe.wait_ge(block_free, g0 + FT)

                    def dn_block(b, par, wait_free=True, chunk=chunk, n=n):
                        for q in range(2):
                            pe.wait_ge(lo_done, 2 * b + (chunk + q + 1))
                            if q == 0 and wait_free:
                                pe.wait_ge(sq_ready, b + (KT * n - 1))
                            product(4 * par, q, hh_hi, hh_lo, 11 * q, 11, q == 0, q == 1)
                    dn_block(0, 0, wait_free=False)
                    dn_block(1, 1, wait_free=False)
                    with pe.Fori(1, KT // 2) as i:
                        for par in range(2):
                            dn_block(2 * i + par, par)
                    chunk += 2 * KT
                else:
                    for b in range(s["tiles_in"]):
                        for q in range(2):
                            pe.wait_ge(lo_done, chunk + 2 * b + q + 1)
                            if q == 0 and b >= 2:
                                pe.wait_ge(proj_done, 16 * s["layer"] + 2 * (b - 1))
                            product(4 * (b % 2) + 2 * q, q, hx_hi, hx_lo, 0, 8, True, True,
                                    wait_k=KT * n if b == 0 else None)
                    chunk += 2 * s["tiles_in"]
                    pe.wait_ge(proj_done, 16 * s["layer"] + 2 * s["tiles_in"])
                    pe_mixer(pe, s)
                    for b in range(KT // 2):
                        for q in range(2):
                            pe.wait_ge(lo_done, chunk + 2 * b + q + 1)
                            if q == 0 and b >= 2:
                                pe.wait_ge(sq_ready, KT * n + 2 * (b - 1))
                            product(4 * (b % 2) + 2 * q, q, hx_hi, hx_lo, 0, 8, True, True)
                    chunk += KT
                pe.wait_ge(ssq_done, (KT + 1) * (n + 1))
                pe.wait_ge(sq_ready, KT * (n + 1))
                sums = ssq if s["kind"] == "ffn" else ssq_m
                for h in range(2):
                    last = nc.tensor.matmul(ps[:, h, 0:TH], ones[:], sums[:, h * TH:(h + 1) * TH],
                                            start=True, stop=True)
                last.then_inc(msq_ready, 1)

    return S


def lay_out(inp):
    import numpy as np
    f = {k: np.asarray(v) for k, v in inp.items()}
    c = np.ascontiguousarray
    x = np.concatenate([f["x_prompt"][0], f["x_sample"][0]], 0)
    out = {"x": c(x.T.reshape(KT, P, T).transpose(1, 0, 2))}
    out["cond"] = c(np.stack([f["c_ctx"], f["c"][0]], -1).reshape(KT, P, 2).transpose(1, 0, 2))
    out["norm_g"] = c(f["norm_g"].reshape(2, 6, KT, P).transpose(3, 0, 1, 2))
    b = f["ada_b"].reshape(2 * NMOD * KT, P).T
    out["ada_b"] = c(np.stack([b, b], -1))
    pick = np.zeros((P, 2), np.float32)
    pick[[0, 2], 0] = 1
    pick[[1, 3], 1] = 1
    out["pick"] = pick
    w = f["ada_w"].reshape(2, KT, P, ADA_GROUPS // 2, 512).transpose(0, 3, 2, 1, 4)
    out["ada_w"] = c(w).reshape(ADA_GROUPS, P, KT, 512)
    def gu(w):
        return w.reshape(4, KT, P, FT, P).transpose(0, 3, 2, 1, 4)
    out["ffn_gu"] = c(np.stack([gu(f["ffn_w_gate"]), gu(f["ffn_w_up"])], 2)).reshape(4, FT, 2, P, 1024)
    w = f["ffn_w_down"].reshape(4, 2, 11, P, KT, P).transpose(0, 4, 1, 3, 2, 5)
    out["ffn_dn"] = c(w).reshape(4, KT, 2, P, SLOT)

    def tiles(w):
        n = w.shape[1] // P
        return c(w.reshape(KT, P, n, P).transpose(2, 1, 0, 3)).reshape(n, P, KT * P)

    w = f["even_w_in"][0]
    o = np.cumsum([0, Q_LORA, P, ROPE, M_HEADS * M_DK, M_HEADS * M_DK, M_HEADS * M_DV, M_HEADS * M_DV, 4 * M_HEADS])
    gates = np.zeros((D, P), np.float32)
    gates[:, 0:16] = w[:, o[7]:o[8]]
    gates[:, NOPE:MLA_QK] = w[:, o[2]:o[3]]
    out["even_in"] = tiles(np.concatenate([w[:, o[0]:o[2]], gates, w[:, o[3]:o[7]]], 1))
    out["even_out"] = tiles(f["even_w_out"][0])
    out["w_qb"] = c(f["mla_w_qb"][0].reshape(2, P, -1).transpose(1, 0, 2))
    kvb = f["mla_w_kvb"][0].reshape(P, MLA_HEADS, 2, 64)
    out["w_kvb"] = c(kvb.transpose(0, 2, 1, 3)).reshape(P, 2, -1)
    out["ckv_old"] = c(f["cache_mla_ckv"][0, 0].T)
    out["krope_old"] = c(f["cache_mla_krope"][0, 0].T)
    def rope(rot):
        nf = rot // 4
        inv = 10000.0 ** (-np.arange(nf, dtype=np.float32) / np.float32(nf))
        t = np.arange(LAT)
        cos, sin = np.zeros((rot, LAT), np.float32), np.zeros((rot, LAT), np.float32)
        swap = np.zeros((rot, rot), np.float32)
        for j in range(rot):
            axis, second, i = j // (2 * nf), j // nf % 2, j % nf
            ang = ((t // 64, t % 64)[axis]).astype(np.float32) * inv[i].astype(np.float32)
            cos[j] = np.cos(ang)
            sin[j] = np.sin(ang) * (1 if second else -1)
            swap[(j - nf) if second else (j + nf), j] = 1
        return cos, sin, swap
    cos, sin, swap = rope(ROPE)
    out["rope_e"] = np.zeros((P, 2, LAT), np.float32)
    out["rope_e"][NOPE:MLA_QK, 0], out["rope_e"][NOPE:MLA_QK, 1] = cos, sin
    out["swap_e"] = np.zeros((P, ROPE), np.float32)
    out["swap_e"][NOPE:MLA_QK] = swap
    cos, sin, swap = rope(HEAD)
    out["rope_o"] = c(np.stack([np.concatenate([cos, cos]), np.concatenate([sin, sin])], 1))
    out["swap_o"] = np.zeros((P, P), np.float32)
    out["swap_o"][0:64, 0:64] = out["swap_o"][64:128, 64:128] = swap
    pr = np.zeros((P, 2, ROWS), np.float32)
    for d in range(2):
        for h in range(M_HEADS):
            for j in range(2):
                pr[8 * d + 4 * j + h, j, 32 * d + h] = 1
    out["pick_rows"] = pr
    rb = np.zeros((P, 3), np.float32)
    gb, m0 = f["mlstm_gate_b"][0].reshape(2, 2, M_HEADS), f["state_mlstm_m"][0, 0]
    for d in range(2):
        rb[32 * d:32 * d + M_HEADS, 0] = gb[d, 0]
        rb[32 * d:32 * d + M_HEADS, 1] = gb[d, 1]
        rb[32 * d:32 * d + M_HEADS, 2] = m0[d]
    out["row_bias"] = rb
    oh = np.zeros((ROWS, 8, P), np.float32)
    for d in range(2):
        for h in range(M_HEADS):
            oh[32 * d + h, 4 * d + h] = 1
    out["onehot"] = oh
    st = np.zeros((2, M_HEADS, M_DK, 2 * P), np.float32)
    st[..., 0:P] = f["state_mlstm_C"][0, 0]
    st[..., P:] = f["state_mlstm_n"][0, 0][..., None]
    out["state0"] = c(st.reshape(2, 2, P, 2 * P).transpose(2, 0, 1, 3))
    g = np.zeros((P, 8), np.float32)
    g[:, 0:2] = f["mla_g_qa"][0].reshape(2, P).T
    g[:, 2] = f["mla_g_kva"][0]
    g[:, 3:7] = f["mlstm_g_out"][0].reshape(M_HEADS, P).T
    out["gains"] = g
    out["ident"] = np.eye(P, dtype=np.float32)
    i = np.arange(P)
    out["causal"] = c(np.stack([np.where(i[None] >= i[:, None], 0, NEG), np.where(i[None] <= i[:, None], 0, NEG)],
                               1).astype(np.float32))
    order = [4 * (2 * p + half) + m for p in range(2) for m in range(4) for half in range(2)]
    w = f["odd_w_in"][0]
    wq = w[:, 0:D].reshape(D, S_HEADS, HEAD)[:, order].reshape(D, D)
    out["odd_in"] = tiles(np.concatenate([wq, w[:, D:]], 1))
    out["odd_out"] = tiles(f["odd_w_out"][0].reshape(S_HEADS, HEAD, D)[order].reshape(D, D))
    out["k_old"] = c(f["cache_swa_k"][0, 0].reshape(2, 2, PAST, HEAD).transpose(1, 3, 0, 2)).reshape(P, 2, PAST)
    v = f["cache_swa_v"][0, 0].reshape(2, 2, PAST // P, P, HEAD)
    out["v_old"] = c(v.transpose(3, 1, 2, 0, 4))
    sk = np.broadcast_to(f["swa_sink"][0], (P, S_HEADS))
    out["sinks"] = c(sk)
    return out


OUTS = {"y": (P, KT, T), "out_ckv": (P, CTX), "out_krope": (ROPE, CTX), "out_state": (P, 2, 2, 2 * P),
        "out_m": (ROWS, 1), "out_kv": (P, 4, CTX)}


def hand_back(r):
    import numpy as np
    c = np.ascontiguousarray
    y = r["y"].transpose(1, 0, 2).reshape(D, T).T
    st = r["out_state"].reshape(2, M_DK, 2, 2, 2 * P).transpose(2, 3, 0, 1, 4).reshape(1, 1, 2, M_HEADS, M_DK, 2 * P)
    m = np.stack([r["out_m"][0:M_HEADS, 0], r["out_m"][32:32 + M_HEADS, 0]])[None, None]
    kv = r["out_kv"].reshape(2, HEAD, 2, 2, CTX).transpose(2, 3, 0, 4, 1).reshape(2, 1, 1, KV_HEADS, CTX, HEAD)
    return (c(y[0:CTX])[None], c(y[CTX:])[None], c(r["out_ckv"].T)[None, None], c(r["out_krope"].T)[None, None],
            c(st[..., 0:P]), c(st[..., P]), c(m), c(kv[0]), c(kv[1]))


def kernel(**inputs):
    import concourse.bacc as _bacc
    from concourse.bass_utils import run_bass_kernel_spmd as _run

    nc = _bacc.Bacc("TRN2", target_bir_lowering=False, num_devices=1, dynamic_dma_scratch_size=1024)
    arrays = {"in_" + k: v for k, v in lay_out(inputs).items()}
    io = {k[3:]: nc.dram_tensor(k, v.shape, mybir.dt.from_np(v.dtype), kind="ExternalInput").ap()
          for k, v in arrays.items()}
    for name, shape in OUTS.items():
        io[name] = nc.dram_tensor("res_" + name, shape, F32, kind="ExternalOutput").ap()
    build(nc, io)
    r = _run(nc, [arrays], core_ids=[0])
    return hand_back({name: r.results[0]["res_" + name] for name in OUTS})
```

```python
from contextlib import ExitStack

import concourse.bass as bass
from concourse import mybir

F32 = mybir.dt.float32
F32R = mybir.dt.float32r
BF16 = mybir.dt.bfloat16
ACT = mybir.ActivationFunctionType
ALU = mybir.AluOpType
AX = mybir.AxisListType

P = 128
D = 1024
KT = D // P
CTX, LAT = 128, 512
T = CTX + LAT
TH = T // 2
PAST = 256
FF = 2816
FT = FF // P
NMOD = 9
EPS = 1e-6
SLOT = 11 * P
MLA_HEADS, NOPE, ROPE, MLA_V, Q_LORA = 8, 64, 32, 64, 256
MLA_QK = NOPE + ROPE
M_HEADS, M_DK, M_DV = 4, 64, 128
CHUNKS = T // P
S_HEADS, KV_HEADS, HEAD = 16, 4, 64
KEYS = CTX + PAST + LAT
NEG = -1e30
ROWS = 36
PM_GATES, PM_Q, PM_K, PM_V, PM_O = 0, 1, 3, 5, 9
ADA_GROUPS = 2 * NMOD * D // 512
ADA_SLOTS = 4
GROUPS = ((0, CTX), (CTX, T))



def attention_plan(layer):
    steps, g, u, b = [], 0, 0, 0
    for lay in range(2):
        out = []
        for h in range((MLA_HEADS, KV_HEADS)[lay]):
            for ns in (((-1, 0),), ((-1, 0), (1,), (2,), (3,)))[lay]:
                step = []
                for n in ns:
                    if lay == 0:
                        size, local, past = (1, (0, 1), 0) if n < 0 else (LAT // P, (0, (KEYS - CTX) // P), 0)
                    else:
                        size, past = S_HEADS // KV_HEADS, 0 if n < 0 else PAST // P
                        local = (0, 1) if n < 0 else (max(n - 1, 0), min(n + 2, LAT // P))
                    keys = local[1] - local[0] + past
                    step.append(dict(g=g, u=u, b=b, h=h, n=n, size=size, local=local, keys=keys, r=64 * (h % 2)))
                    g, u, b = g + 1, u + size, b + keys
                out.append(step)
        steps.append(out)
    return steps[layer]


def build(nc, io, upto=6):
    with ExitStack() as ctx:
        def sb(name, shape, dt=F32):
            return ctx.enter_context(nc.sbuf_tensor(name, shape, dt))

        def sem(name):
            return ctx.enter_context(nc.semaphore(name))

        xT = sb("xT", [P, KT, T])
        w_raw = sb("w_raw", [P, 2, SLOT])
        w_hi = sb("w_hi", [P, 2, SLOT], F32R)
        w_lo = sb("w_lo", [P, 2, SLOT], F32R)
        ones = sb("ones", [P, P])
        eps_col = sb("eps_col", [P, 1])
        mods = sb("mods", [P, 2 * NMOD * KT, 2])
        rstd = sb("rstd", [P, T])
        maxes = sb("maxes", [P, 4, 4])
        sink_e = sb("sink_e", [P, 4, 4])
        neg_sink = sb("neg_sink", [P, 2 * S_HEADS])
        gains = sb("gains", [P, 8])
        row_bias = sb("row_bias", [P, 3])
        m_in = sb("m_in", [P, 8])
        one_col = sb("one_col", [P, 1])
        ident = sb("ident", [P, P])
        causal = sb("causal", [P, 2, P])
        ones_r = sb("ones_r", [P, P], F32R)
        ident_b = sb("ident_b", [P, P], BF16)
        causal_b = sb("causal_b", [P, 2, 4, P], BF16)
        sink_half = sb("sink_half", [P, 3, 64])
        neg_m = sb("neg_m", [P, 4, 4], F32R)

        ps = ctx.enter_context(nc.psum_tensor("ps", [P, 8, 512], F32))

        with ExitStack() as scope:
            def asb(name, shape, dt=F32):
                return scope.enter_context(nc.sbuf_tensor(name, shape, dt))
            cond = asb("cond", [P, KT, 2])
            cond_silu = asb("cond_silu", [P, KT, 2])
            cond_hl = asb("cond_hl", [P, KT, P], F32R)
            mod_rows = asb("mod_rows", [P, 2, 512])
            pick = asb("pick", [P, 2])
            ada_bias = asb("ada_bias", [P, 2 * NMOD * KT, 2])
            norm_g = asb("norm_g", [P, 2, 6, KT])
            ada_raw = asb("ada_raw", [P, ADA_SLOTS, KT, 512])
            ada_hi = asb("ada_hi", [P, 2, KT, 512], F32R)
            ada_lo = asb("ada_lo", [P, 2, KT, 512], F32R)
        with ExitStack() as scope:
            def fsb(name, shape, dt=F32):
                return scope.enter_context(nc.sbuf_tensor(name, shape, dt))
            hx_hi = fsb("hx_hi", [P, KT, T], F32R)
            hx_lo = fsb("hx_lo", [P, KT, T], F32R)
            tmp = fsb("tmp", [P, 2, T])
            silu_g = tmp
            with ExitStack() as inner:
                hh_hi = inner.enter_context(nc.sbuf_tensor("hh_hi", [P, FT, T], F32R))
                hh_lo = inner.enter_context(nc.sbuf_tensor("hh_lo", [P, FT, T], F32R))
        with ExitStack() as scope:
            y = scope.enter_context(nc.sbuf_tensor("y", [P, KT, T], F32))
            sq = scope.enter_context(nc.sbuf_tensor("sq", [P, 2, T], F32))
            ssq = scope.enter_context(nc.sbuf_tensor("ssq", [P, T], F32))

        with ExitStack() as scope:
            def esb(name, shape, dt=F32, s=scope):
                return s.enter_context(nc.sbuf_tensor(name, shape, dt))
            for name in ("below_hx_hi", "below_hx_lo"):
                esb(name, [P, KT, T])
            esb("below_tmp", [P, 2, T])
            with ExitStack() as res:
                y_m = esb("y_m", [P, KT, T], s=res)
                sq_m = esb("sq_m", [P, 2, T], s=res)
                ssq_m = esb("ssq_m", [P, T], s=res)
            with ExitStack() as even:
                pm = esb("pm", [P, 13, T], s=even)
                with ExitStack() as mla:
                    qh = esb("qh", [P, MLA_HEADS, T], s=mla)
                    kh = esb("kh", [P, MLA_HEADS, KEYS], s=mla)
                    vtok = esb("vtok", [P, KEYS // P, MLA_HEADS // 2, 3, MLA_V], s=mla)
                    with ExitStack() as part:
                        pa = esb("pa", [P, 3, T], s=part)
                        w_qb = esb("w_qb", [P, 2, MLA_HEADS * MLA_QK], s=part)
                    with ExitStack() as part:
                        prob_e = esb("prob_e", [P, 3, 512], s=part)
                        qk_r = part.enter_context(nc.sbuf_tensor("qk_r", [P, T + KEYS], F32R))
                with ExitStack() as ml:
                    vaug = esb("vaug", [P, CHUNKS, M_HEADS, 2 * P], s=ml)
                    ktok = esb("ktok", [P, CHUNKS, M_HEADS * M_DK], s=ml)
                    onehot = esb("onehot", [P, 8, P], s=ml)
                    rows3 = esb("rows3", [P, 3, T], s=ml)
                    acol = esb("acol", [P, CHUNKS, ROWS], s=ml)
                    decay = esb("decay", [P, LAT], s=ml)
                    q_inter = esb("q_inter", [P, 2, 2, LAT], s=ml)
                    k_w = esb("k_w", [P, 4, M_DK], s=ml)
                    state = esb("state", [P, 5, 2 * P], s=ml)
                    state0 = esb("state0", [P, 2, 2, 2 * P], s=ml)
                    state_out = esb("state_out", [P, 2, 2, 2 * P], s=ml)
                    with ExitStack() as early:
                        rows = esb("rows", [P, 6, T], s=early)
                    hm = esb("hm", [P, M_HEADS, T], s=ml)
                    hs = esb("hs", [P, LAT], s=ml)
            with ExitStack() as odd:
                po = esb("po", [P, 12, T], s=odd)
                v_new = esb("v_new", [P, CHUNKS, KV_HEADS // 2, 3, HEAD], s=odd)
                v_old = esb("v_old", [P, PAST // P, KV_HEADS // 2, 3, HEAD], s=odd)
                k_old = esb("k_old", [P, 2, PAST], s=odd)
                rope_o = esb("rope_o", [P, 2, LAT], s=odd)
                swap_o = esb("swap_o", [P, P], s=odd)
                turned = esb("turned", [P, 2, LAT], s=odd)
                po_r = odd.enter_context(nc.sbuf_tensor("po_r", [P, 10, T], F32R))
                k_old_r = odd.enter_context(nc.sbuf_tensor("k_old_r", [P, 2, PAST], F32R))
                prob_o = esb("prob_o", [P, 3, 512], s=odd)
                diag_o = odd.enter_context(nc.sbuf_tensor("diag_o", [P, 4, 4, P], F32R))
                sink_diag = esb("sink_diag", [P, 4, 4, P], s=odd)
                out_o = esb("out_o", [P, 2, 2, 512], s=odd)
        with ExitStack() as scope:
            for name, shape in (("past_y", [P, KT, T]), ("past_sq", [P, 2, T]), ("past_ssq", [P, T])):
                scope.enter_context(nc.sbuf_tensor(name, shape, F32))
            rope_e = scope.enter_context(nc.sbuf_tensor("rope_e", [P, 2, LAT], F32))
            swap_e = scope.enter_context(nc.sbuf_tensor("swap_e", [P, ROPE], F32))
            pick_rows = scope.enter_context(nc.sbuf_tensor("pick_rows", [P, 2, ROWS], F32))
            w_kvb = scope.enter_context(nc.sbuf_tensor("w_kvb", [P, 2, MLA_HEADS * 64], F32))
            ckv_keys = scope.enter_context(nc.sbuf_tensor("ckv_keys", [P, KEYS], F32))

        with ExitStack() as scope:
            scope.enter_context(nc.sbuf_tensor("hx_hi_mla", [P, KT // 2, T], F32))
            with ExitStack() as part:
                out_e = part.enter_context(nc.sbuf_tensor("out_e", [P, 2, 2, 512], F32))
            with ExitStack() as part:
                weigh = part.enter_context(nc.sbuf_tensor("weigh", [P, 2, LAT], F32))
            scope.enter_context(nc.sbuf_tensor("hx_rest", [P, KT, T], F32))
            with ExitStack() as part:
                diag_e = part.enter_context(nc.sbuf_tensor("diag_e", [P, 4, 4, P], F32R))
            with ExitStack() as part:
                g_inter = part.enter_context(nc.sbuf_tensor("g_inter", [P, 2, LAT], F32))
                floor_m = part.enter_context(nc.sbuf_tensor("floor_m", [P, 2, LAT], F32))

        in_loaded, x_loaded, out_stored = sem("in_loaded"), sem("x_loaded"), sem("out_stored")
        mix_loaded, mix_loaded2, mix_loaded3 = sem("mix_loaded"), sem("mix_loaded2"), sem("mix_loaded3")
        const_ready, attn_const = sem("const_ready"), sem("attn_const")
        act_chain, dve_chain = sem("act_chain"), sem("dve_chain")
        raw_ready = [sem("raw_ready0"), sem("raw_ready1")]
        hi_done, lo_done, w_used = sem("hi_done"), sem("lo_done"), sem("w_used")
        cond_act, cond_ready = sem("cond_act"), sem("cond_ready")
        ada_loaded = [sem(f"ada_loaded{q}") for q in range(ADA_SLOTS)]
        ada_hi_done, ada_lo_done, ada_used = sem("ada_hi_done"), sem("ada_lo_done"), sem("ada_used")
        row_ready, col_ready, mod_added, mods_ready = sem("row_ready"), sem("col_ready"), sem("mod_added"), sem("mods_ready")
        silu_done, mul_done, hhi_done, block_free = sem("silu_done"), sem("mul_done"), sem("hhi_done"), sem("block_free")
        sq_ready, ssq_done, msq_ready, y_scaled = sem("sq_ready"), sem("ssq_done"), sem("msq_ready"), sem("y_scaled")
        x_ready = [sem("x_ready_even"), sem("x_ready_odd")]
        xsq_ready, xsq_used, rstd_ready = sem("xsq_ready"), sem("xsq_used"), sem("rstd_ready")
        pre_ready, hxhi_ready, hx_ready = sem("pre_ready"), sem("hxhi_ready"), sem("hx_ready")
        proj_done = sem("proj_done")
        lora_sq, lora_sum, lora_rstd, lora_ready = sem("lora_sq"), sem("lora_sum"), sem("lora_rstd"), sem("lora_ready")
        built, built_act, built_dve = sem("built"), sem("built_act"), sem("built_dve")
        odd_swap, odd_rope = sem("odd_swap"), sem("odd_rope")
        rounded, s_ready, max_done = sem("rounded"), sem("s_ready"), sem("max_done")
        diag_ready, sink_arg, sink_exp, sink_ready = sem("diag_ready"), sem("sink_arg"), sem("sink_exp"), sem("sink_ready")
        st_ready, p_ready, pv_done = sem("st_ready"), sem("p_ready"), sem("pv_done")
        o_ready, o_scaled, ohi_done, o_done = sem("o_ready"), sem("o_scaled"), sem("ohi_done"), sem("o_done")
        gate_rows, gate_act, rows_ready = sem("gate_rows"), sem("gate_act"), sem("rows_ready")
        turn_ready, turn_act, ml_filled = sem("turn_ready"), sem("turn_act"), sem("ml_filled")
        m_ready, kq_ready, decay_arg, decay_ready = sem("m_ready"), sem("kq_ready"), sem("decay_arg"), sem("decay_ready")
        weigh_ready, gain_ready, state_ready = sem("weigh_ready"), sem("gain_ready"), sem("state_ready")
        numden_ready, head_done = sem("numden_ready"), sem("head_done")
        hm_sq, hm_sum, hm_ln, hm_rstd = sem("hm_sq"), sem("hm_sum"), sem("hm_ln"), sem("hm_rstd")
        hm_f, hm_hi, mix_ready = sem("hm_f"), sem("hm_hi"), sem("mix_ready")
        chained = {}
        CONSTS = 9 * 16
        N_OUT = 4 * (upto > 1) + (upto > 4)
        MLA_GROUPS, SWA_GROUPS = [sum(attention_plan(layer), []) for layer in range(2)]

        def link(eng, chain, ins):
            chained[chain.name] = chained.get(chain.name, 0) + 1
            ins.then_inc(chain, 1)
            eng.wait_ge(chain, chained[chain.name])

        ada_w, ffn_gu, ffn_dn = io["ada_w"], io["ffn_gu"], io["ffn_dn"]

        def bank_pair(i):
            return ps[:, 2 * i:2 * i + 2, 0:TH]

        def halves(tile):
            return tile.rearrange("p (n t) -> p n t", n=2)

        def split_hi(act, c, slot, tiles, wait_used=True):
            act.wait_ge(raw_ready[slot], (c // 2) * 16 + 16 if isinstance(c, int) else c * 8 + (16 - 8 * slot))
            if wait_used:
                act.wait_ge(w_used, c - 1)
            nc.scalar.copy(w_hi[:, slot, 0:tiles * P], w_raw[:, slot, 0:tiles * P]).then_inc(hi_done, 1)

        def split_lo(dve, c, slot, tiles, wait_used=True):
            dve.wait_ge(hi_done, c + 1)
            if wait_used:
                dve.wait_ge(w_used, c - 1)
            nc.vector.tensor_tensor(w_lo[:, slot, 0:tiles * P], w_raw[:, slot, 0:tiles * P],
                                    w_hi[:, slot, 0:tiles * P], ALU.subtract).then_inc(lo_done, 1)

        def mod_col(layer, idx, k, cond_i):
            j = (layer * NMOD + idx) * KT + k
            return mods[:, j, cond_i:cond_i + 1]

        SUBS = []
        for layer in range(2):
            SUBS += [dict(kind="ffn", f=2 * layer, layer=layer, idx=0), dict(kind="mix", layer=layer, idx=3),
                     dict(kind="ffn", f=2 * layer + 1, layer=layer, idx=6)]
        SUBS = SUBS[:upto]
        chunk0, gu0 = 0, 0
        for s in SUBS:
            s.update(chunk=chunk0, gu0=gu0)
            s["tiles_in"] = {"ffn": FT, "mix": 8 if s["layer"] == 0 else 6}[s["kind"]]
            s["blocks_out"] = KT if s["kind"] == "ffn" else KT // 2
            chunk0 += 2 * (s["tiles_in"] + s["blocks_out"])
            gu0 += FT if s["kind"] == "ffn" else 0

        block = ctx.enter_context(nc.Block())

        BUILD = [("kr", 0), ("gi", 0), ("gf", 0)]
        for h in range(MLA_HEADS):
            BUILD += [("q", h), ("k", h)] + ([("sw", h - 1)] if h else [])
        BUILD += [("sw", MLA_HEADS - 1)] + [("v", j) for j in range(KEYS // P)]
        BY_ACT = ("q", "v", "gi", "gf")

        def evacuated(i):
            a = sum(kind in BY_ACT for kind, _ in BUILD[:i])
            return a, i - a

        QPOS = {h: BUILD.index(("q", h)) for h in range(MLA_HEADS)}

        def pair_flat(i):
            return ps[:, 2 * i:2 * i + 2, :].rearrange("p b c -> p (b c)")

        ML_UNITS = [(None, parity) for parity in range(2)] + [(h, d) for h in range(M_HEADS) for d in range(2)]

        def ml_blocks(unit):
            if unit[0] is None:
                return [(h, d, 0) for d in range(2) for h in (unit[1], unit[1] + 2)]
            return [(unit[0], unit[1], c) for c in range(1, CHUNKS)]

        def ml_rows(unit):
            r = 64 * ((unit[1] if unit[0] is None else unit[0]) % 2)
            return slice(r, r + 64)

        def ml_order(d):
            return (1, 2, 3, 4) if d == 0 else (4, 3, 2, 1)

        M_BANK, G_BANK, FLOOR_BANK, KQ_BANK, NUM_BANK = 0, 1, 2, 3, 4

        def gain_cols(j):
            return ps[:, G_BANK + j // 2, (j % 2) * 2 * P:(j % 2 + 1) * 2 * P]

        def scratch(h):
            if h < 3:
                return q_inter[:].rearrange("p a b t -> p (a b t)")[:, h * T:(h + 1) * T]
            return g_inter[:].rearrange("p a t -> p (a t)")[:, 0:T]

        def pe_attention(pe, layer):
            steps = attention_plan(layer)
            prob, diag = (prob_e, prob_o)[layer], (diag_e, diag_o)[layer]

            def key_block(g, j):
                if layer == 0:
                    c = 0 if g["n"] < 0 else CTX + j * P
                    return kh[0:MLA_QK, g["h"], c:c + P]
                rs, p, local = slice(g["r"], g["r"] + 64), g["h"] // 2, g["local"][1] - g["local"][0]
                if g["n"] < 0:
                    return po[rs, 8 + p, 0:CTX]
                if j < local:
                    c = CTX + (g["local"][0] + j) * P
                    return po[rs, 8 + p, c:c + P]
                return k_old[rs, p, (j - local) * P:(j - local + 1) * P]

            def unit_scores(g, i):
                u = g["u"] + i
                if u >= 2:
                    pe.wait_ge(max_done, u - 1)
                bank = 2 * (u % 2)
                q0 = 0 if g["n"] < 0 else CTX + g["n"] * P
                a, b = score_columns(layer, g)
                if layer == 0:
                    q0 += i * P
                    pe.wait_ge(rounded, g["h"] + 1)
                    query = qk_r[0:MLA_QK, q0:q0 + P]
                    k0 = T + (0 if g["n"] < 0 else CTX)
                    parts = [qk_r[0:MLA_QK, k0:k0 + 512 - a], qk_r[0:MLA_QK, k0 + 512 - a:k0 + b - a]]
                else:
                    rs, p, (lo, hi) = slice(g["r"], g["r"] + 64), g["h"] // 2, g["local"]
                    query = po_r[rs, 4 * p + i, q0:q0 + P]
                    k0 = 0 if g["n"] < 0 else CTX + lo * P
                    parts = [po_r[rs, 8 + p, k0:k0 + 512 - a], k_old_r[rs, p, :]]
                masks = []
                if layer == 1 and g["n"] >= 0:
                    if lo < g["n"]:
                        masks.append((a, 0))
                    if hi > g["n"] + 1:
                        masks.append((512 - P, 1))
                ins = nc.tensor.matmul(ps[:, bank, a:512], query, parts[0], start=True, stop=not masks)
                for c, side in masks:
                    ins = nc.tensor.matmul(ps[:, bank, c:c + P], ident_b[:], causal_b[:, side, 0, :], start=False,
                                           stop=(c, side) == masks[-1])
                if b > 512:
                    ins = nc.tensor.matmul(ps[:, bank + 1, 0:b - 512], query, parts[1], start=True, stop=True)
                ins.then_inc(s_ready, 1)

            def block_scores(g, j):
                b, width = g["b"] + j, g["size"] * P
                if j == 0:
                    pe.wait_ge(diag_ready, g["g"] + 1)
                if b >= 2:
                    pe.wait_ge(p_ready, b - 1)
                out = ps[:, 4 + b % 2, 0:width]
                nc.tensor.matmul(out, ones_r[:], diag[:, g["g"] % 4, 0:g["size"], :].rearrange("p i q -> p (i q)"),
                                 start=True, stop=False)
                if layer == 0:
                    q0 = 0 if g["n"] < 0 else CTX
                    ins = nc.tensor.matmul(out, key_block(g, j), qh[0:MLA_QK, g["h"], q0:q0 + width], start=False,
                                           stop=True)
                else:
                    rs, p, n, c = slice(g["r"], g["r"] + 64), g["h"] // 2, g["n"], g["local"][0] + j
                    q0 = 0 if n < 0 else CTX + n * P
                    side = {n - 1: 1, n + 1: 0}.get(c) if n >= 0 and c < g["local"][1] else None
                    ins = nc.tensor.matmul(out.rearrange("p (i q) -> p i q", q=P), key_block(g, j),
                                           po[rs, 4 * p:4 * p + 4, q0:q0 + P], start=False, stop=side is None)
                    if side is not None:
                        ins = nc.tensor.matmul(out, ident_b[:], causal_b[:, side].rearrange("p i q -> p (i q)"),
                                               start=False, stop=True)
                ins.then_inc(st_ready, 1)

            def block_values(g, j):
                h, n, width, b = g["h"], g["n"], g["size"] * P, g["b"] + j
                pe.wait_ge(p_ready, b + 1)
                if j == 0 and g["g"] >= 2:
                    pe.wait_ge(o_scaled, g["g"] - 1)
                if layer == 0:
                    v = vtok[:, 0 if n < 0 else 1 + j, h // 2]
                elif n < 0:
                    v = v_new[:, 0, h // 2]
                elif j < g["local"][1] - g["local"][0]:
                    v = v_new[:, 1 + g["local"][0] + j, h // 2]
                else:
                    v = v_old[:, j - (g["local"][1] - g["local"][0]), h // 2]
                out, last = ps[:, 6 + g["g"] % 2, 0:width], j == g["keys"] - 1
                cols = slice(64 * (h % 2), 64 * (h % 2) + P)
                ins = nc.tensor.matmul(out, v.rearrange("p a d -> p (a d)")[:, cols], prob[:, b % 3, 0:width],
                                       start=(j == 0), stop=last and layer == 0)
                ins.then_inc(pv_done, 1)
                if last and layer == 1:
                    pe.wait_ge(sink_ready, g["g"] - len(MLA_GROUPS) + 1)
                    ins = nc.tensor.matmul(out, sink_half[:].rearrange("p a d -> p (a d)")[:, cols],
                                           sink_diag[:, g["g"] % 4].rearrange("p i q -> p (i q)"), start=False, stop=True)
                    ins.then_inc(o_ready, 1)

            pe.wait_ge(attn_const, 6)
            for unit in units_of(steps[0]):
                unit_scores(*unit)
            blocks = []
            for t, step in enumerate(steps):
                own = [(g, j) for g in step for j in range(g["keys"])]
                ahead = units_of(steps[t + 1]) if t + 1 < len(steps) else []
                per = -(-len(ahead) // (len(own) - 2))
                for i, (g, j) in enumerate(own):
                    blocks.append((g, j, ahead[(i - 1) * per:i * per] if i else []))
            for i, (g, j, ahead) in enumerate(blocks):
                block_scores(g, j)
                if i:
                    block_values(*blocks[i - 1][0:2])
                for unit in ahead:
                    unit_scores(*unit)
            block_values(*blocks[-1][0:2])

        def units_of(step):
            return [(g, i) for g in step for i in range(g["size"])]

        def score_columns(layer, g):
            if g["n"] < 0:
                return 512 - P, 512
            if layer == 0:
                return 128, 896
            return 512 - P * (g["local"][1] - g["local"][0]), 512 + PAST

        def act_attention(act, layer):
            steps = attention_plan(layer)
            scale = (MLA_QK ** -0.5, HEAD ** -0.5)[layer]
            prob, outs = (prob_e, prob_o)[layer], (out_e, out_o)[layer]

            def round_output(g):
                act.wait_ge(o_scaled, g["g"] + 1)
                dst, src = mixed(hx_hi, g, outs)
                nc.scalar.copy(dst, src).then_inc(ohi_done, 1)

            def round_head(h):
                if h:
                    act.wait_ge(max_done, steps[h][0]["u"])
                nc.scalar.copy(qk_r[0:MLA_QK, 0:T], qh[0:MLA_QK, h, :])
                nc.scalar.copy(qk_r[0:MLA_QK, T:], kh[0:MLA_QK, h, :]).then_inc(rounded, 1)
            if layer == 0:
                a, d = evacuated(len(BUILD))
                act.wait_ge(built_act, a)
                act.wait_ge(built_dve, d)
                round_head(0)
                round_head(1)
            waiting = []
            for t, step in enumerate(steps):
                if layer == 1:
                    for g in step:
                        act.wait_ge(sink_arg, g["g"] - len(MLA_GROUPS) + 1)
                        nc.scalar.activation(sink_e[:, g["g"] % 4, :], sink_e[:, g["g"] % 4, :],
                                             ACT.Exp).then_inc(sink_exp, 1)
                for i, (g, j) in enumerate((g, j) for g in step for j in range(g["keys"])):
                    b, width = g["b"] + j, g["size"] * P
                    act.wait_ge(st_ready, b + 1)
                    if b >= 3:
                        act.wait_ge(pv_done, b - 2)
                    nc.scalar.activation(prob[:, b % 3, 0:width], ps[:, 4 + b % 2, 0:width], ACT.Exp,
                                         scale=scale).then_inc(p_ready, 1)
                    if i >= 1 and waiting:
                        round_output(waiting.pop(0))
                if layer == 0 and t + 2 < MLA_HEADS:
                    round_head(t + 2)
                for g in waiting:
                    round_output(g)
                waiting = list(step)
            for g in waiting:
                round_output(g)

        def mixed(buf, g, outs):
            h, n, r = g["h"], g["n"], g["r"]
            src = outs[r:r + 64, g["g"] % 2, 1, 0:g["size"] * P]
            if g["g"] < len(MLA_GROUPS):
                return (buf[r:r + 64, h // 2, 0:CTX] if n < 0 else buf[r:r + 64, h // 2, CTX:T]), src
            c0 = 0 if n < 0 else CTX + n * P
            return buf[r:r + 64, 4 * (h // 2):4 * (h // 2) + 4, c0:c0 + P], src.rearrange("p (i q) -> p i q", q=P)

        def dve_attention(dve, layer):
            steps = attention_plan(layer)
            scale = (MLA_QK ** -0.5, HEAD ** -0.5)[layer]
            diag, outs = (diag_e, diag_o)[layer], (out_e, out_o)[layer]

            def diagonal(out, column, slot, size=4):
                shape = (P, size, P)
                return nc.vector.tensor_tensor(out[:, slot, 0:size], ident[:].unsqueeze(1).broadcast_to(shape),
                                               column[:, slot, 0:size].unsqueeze(2).broadcast_to(shape), ALU.mult)

            def maxima(step):
                for g in step:
                    a, b = score_columns(layer, g)
                    slot, size = g["g"] % 4, g["size"]
                    for i in range(size):
                        u = g["u"] + i
                        dve.wait_ge(s_ready, u + 1)
                        nc.vector.tensor_reduce(maxes[:, slot, i:i + 1], pair_flat(u % 2)[:, a:b], AX.X,
                                                ALU.max).then_inc(max_done, 1)
                    dve.wait_ge(max_done, g["u"] + size)
                    if layer == 0:
                        ins = nc.vector.tensor_scalar(neg_m[:, slot, 0:size], maxes[:, slot, 0:size], -1.0, None, ALU.mult)
                    else:
                        heads = slice(S_HEADS + 4 * g["h"], S_HEADS + 4 * g["h"] + 4)
                        ins = nc.vector.scalar_tensor_tensor(out=neg_m[:, slot, :], in0=maxes[:, slot, :], scalar=-1.0,
                                                             in1=neg_sink[:, heads], op0=ALU.mult, op1=ALU.min)
                    link(dve, dve_chain, ins)
                    if layer == 1:
                        heads = slice(4 * g["h"], 4 * g["h"] + 4)
                        nc.vector.scalar_tensor_tensor(out=sink_e[:, slot, :], in0=neg_m[:, slot, :].bitcast(F32),
                                                       scalar=scale, in1=neg_sink[:, heads], op0=ALU.mult,
                                                       op1=ALU.add).then_inc(sink_arg, 1)
                    diagonal(diag, neg_m, slot, size).then_inc(diag_ready, 1)

            def low_output(g):
                dve.wait_ge(ohi_done, g["g"] + 1)
                dst, src = mixed(hx_lo, g, outs)
                nc.vector.tensor_tensor(dst, src, mixed(hx_hi, g, outs)[0].bitcast(F32),
                                        ALU.subtract).then_inc(o_done, 1)

            def scaled_output(g):
                r, width, par = g["r"], g["size"] * P, g["g"] % 2
                if layer == 0:
                    dve.wait_ge(pv_done, g["b"] + g["keys"])
                else:
                    dve.wait_ge(o_ready, g["g"] - len(MLA_GROUPS) + 1)
                link(dve, dve_chain, nc.vector.reciprocal(outs[r:r + 64, par, 0, 0:width],
                                                          ps[64 - r:P - r, 6 + par, 0:width]))
                nc.vector.tensor_tensor(outs[r:r + 64, par, 1, 0:width], ps[r:r + 64, 6 + par, 0:width],
                                        outs[r:r + 64, par, 0, 0:width], ALU.mult).then_inc(o_scaled, 1)
            maxima(steps[0])
            waiting = []
            for t, step in enumerate(steps):
                if layer == 1:
                    for g in step:
                        dve.wait_ge(sink_exp, g["g"] - len(MLA_GROUPS) + 1)
                        diagonal(sink_diag, sink_e, g["g"] % 4).then_inc(sink_ready, 1)
                if len(step) > 1:
                    for g in waiting:
                        low_output(g)
                    waiting = []
                    scaled_output(step[0])
                if t + 1 < len(steps):
                    maxima(steps[t + 1])
                for g in waiting:
                    low_output(g)
                scaled_output(step[-1])
                waiting = step
            for g in waiting:
                low_output(g)

        def pe_mixer(pe, s):
            if s["layer"] == 1:
                pe.wait_ge(mix_loaded, 16 * (9 + 5))
                for t in range(10):
                    if t >= 4:
                        pe.wait_ge(odd_rope, t - 3)
                    nc.tensor.matmul(ps[:, 4 + t % 4, :], swap_o[:], po[:, t, CTX:T], start=True,
                                     stop=True).then_inc(odd_swap, 1)
                for c in range(CHUNKS):
                    if c >= 4:
                        pe.wait_ge(odd_rope, 10 + c - 3)
                    for j in range(2):
                        ins = nc.tensor.transpose(ps[:, c % 4, j * P:(j + 1) * P], po[:, 10 + j, c * P:(c + 1) * P], ident[:])
                    ins.then_inc(odd_swap, 1)
                pe.wait_ge(odd_rope, 10 + CHUNKS)
                pe.wait_ge(rounded, MLA_HEADS + 11)
                pe_attention(pe, 1)
                last = SWA_GROUPS[-1]
                pe.wait_ge(max_done, last["u"] + last["size"])
                return
            pe.wait_ge(lora_sq, 3)
            for j, (bank, first, last) in enumerate(((0, True, False), (0, False, True), (2, True, True))):
                for h in range(2):
                    ins = nc.tensor.matmul(ps[:, bank + h, 0:TH], ones[:], y[:, j, h * TH:(h + 1) * TH],
                                           start=first, stop=last)
            ins.then_inc(lora_sum, 1)
            pe.wait_ge(mix_loaded, 16 * 9)
            pe.wait_ge(mix_loaded2, 16 * 5)
            pe.wait_ge(lora_ready, 3)
            for i, (kind, h) in enumerate(BUILD):
                pair = i % 4
                if i >= 4:
                    a, d = evacuated(i - 3)
                    pe.wait_ge(built_act, a)
                    pe.wait_ge(built_dve, d)
                if kind == "kr":
                    ins = nc.tensor.matmul(ps[NOPE:MLA_QK, 2 * pair, :], swap_e[NOPE:MLA_QK, :],
                                           pm[NOPE:MLA_QK, PM_GATES, CTX:T], start=True, stop=True)
                elif kind in ("gi", "gf"):
                    for n in range(2):
                        ins = nc.tensor.matmul(ps[0:ROWS, 2 * pair + n, 0:TH], pick_rows[0:32, int(kind == "gf"), :],
                                               pm[0:32, PM_GATES, n * TH:(n + 1) * TH], start=True, stop=True)
                elif kind == "q":
                    for n in range(2):
                        for k in range(2):
                            ins = nc.tensor.matmul(ps[0:MLA_QK, 2 * pair + n, 0:TH],
                                                   w_qb[:, k, h * MLA_QK:(h + 1) * MLA_QK],
                                                   pa[:, k, n * TH:(n + 1) * TH], start=(k == 0), stop=(k == 1))
                elif kind == "k":
                    for n in range(2):
                        ins = nc.tensor.matmul(ps[0:NOPE, 2 * pair + n, 0:KEYS // 2], w_kvb[:, 0, h * 64:(h + 1) * 64],
                                               ckv_keys[:, n * (KEYS // 2):(n + 1) * (KEYS // 2)], start=True, stop=True)
                elif kind == "sw":
                    pe.wait_ge(built_act, evacuated(QPOS[h] + 1)[0])
                    ins = nc.tensor.matmul(ps[NOPE:MLA_QK, 2 * pair, :], swap_e[NOPE:MLA_QK, :],
                                           qh[NOPE:MLA_QK, h, CTX:T], start=True, stop=True)
                else:
                    ins = nc.tensor.matmul(ps[:, 2 * pair, :], ckv_keys[:, h * P:(h + 1) * P], w_kvb[:, 1, :],
                                           start=True, stop=True)
                ins.then_inc(built, 1)
            a, d = evacuated(len(BUILD))
            pe.wait_ge(built_act, a)
            pe.wait_ge(built_dve, d)
            pe_attention(pe, 0)
            pe.wait_ge(o_done, len(MLA_GROUPS))
            for c in range(CHUNKS):
                if c >= 4:
                    pe.wait_ge(turn_act, 2 * (c - 3))
                pair = 2 * (c % 4)
                for j in range(2):
                    ins = nc.tensor.transpose(ps[:, pair, j * P:(j + 1) * P], pm[:, PM_K + j, c * P:(c + 1) * P], ident[:])
                for j in range(M_HEADS):
                    ins = nc.tensor.transpose(ps[:, pair + 1, j * P:(j + 1) * P], pm[:, PM_V + j, c * P:(c + 1) * P], ident[:])
                ins.then_inc(turn_ready, 1)
            pe.wait_ge(turn_act, 2 * CHUNKS)
            pe.wait_ge(rows_ready, 1)
            for c in range(CHUNKS):
                ins = nc.tensor.transpose(ps[:, 0, c * ROWS:(c + 1) * ROWS], rows[0:ROWS, 1, c * P:(c + 1) * P],
                                          ident[0:ROWS, 0:ROWS])
            ins.then_inc(turn_ready, 1)
            pe.wait_ge(turn_act, 2 * CHUNKS + 1)
            pe.wait_ge(mix_loaded3, 32)

            def first(u):
                (head, d), rs = ML_UNITS[u], ml_rows(ML_UNITS[u])

                def spread(row, bank):
                    if head is None:
                        for b, (h, d_b, _) in enumerate(ml_blocks(ML_UNITS[u])):
                            ins = nc.tensor.matmul(ps[:, bank, b * P:(b + 1) * P], onehot[0:ROWS, 4 * d_b + h, :],
                                                   rows3[0:ROWS, row, 0:CTX], start=True, stop=True)
                        return ins
                    return nc.tensor.matmul(ps[:, bank, :], onehot[0:ROWS, 4 * d + head, :], rows3[0:ROWS, row, CTX:T],
                                            start=True, stop=True)
                if u:
                    pe.wait_ge(decay_arg, u)
                spread(0, M_BANK).then_inc(m_ready, 1)
                if u:
                    pe.wait_ge(weigh_ready, u)
                for b, (h, _, c) in enumerate(ml_blocks(ML_UNITS[u])):
                    nc.tensor.matmul(ps[:, KQ_BANK, b * P:(b + 1) * P], pm[rs, PM_K + h // 2, c * P:(c + 1) * P],
                                     pm[rs, PM_Q + h // 2, c * P:(c + 1) * P], start=True, stop=True)
                if u:
                    pe.wait_ge(state_ready, u)
                spread(1, G_BANK)
                spread(2, FLOOR_BANK).then_inc(kq_ready, 1)
            first(0)
            pe.wait_ge(ml_filled, 1)
            for u, (head, d) in enumerate(ML_UNITS):
                rs = ml_rows(ML_UNITS[u])
                pe.wait_ge(weigh_ready, u + 1)
                if head is None:
                    gains_of = [(h, 0, b, b) for b, (h, _, _) in enumerate(ml_blocks(ML_UNITS[u]))]
                else:
                    gains_of = [(head, c, c - 1, j) for j, c in enumerate(ml_order(d)[0:3])]
                for h, c, b, j in gains_of:
                    ins = nc.tensor.matmul(gain_cols(j)[rs], k_w[:, b, :], vaug[:, c, h, :], start=True, stop=True)
                ins.then_inc(gain_ready, 1)
                if u + 1 < len(ML_UNITS):
                    first(u + 1)
                pe.wait_ge(state_ready, u + 1)
                if u >= 2:
                    pe.wait_ge(head_done, u - 1)
                for b, (h, _, c) in enumerate(ml_blocks(ML_UNITS[u])):
                    cols = slice(b * P, (b + 1) * P)
                    for which in range(2):
                        part = slice(which * P, (which + 1) * P)
                        out = ps[:, NUM_BANK + 2 * (u % 2) + which, cols]
                        ins = nc.tensor.matmul(out, vaug[:, c, h, part], weigh[:, u % 2, cols], start=True, stop=(c == 0))
                        if c > 0:
                            ins = nc.tensor.matmul(out, state[:, c, part], q_inter[:, h % 2, d, cols], start=False,
                                                   stop=True)
                ins.then_inc(numden_ready, 1)
            pe.wait_ge(head_done, len(ML_UNITS))
            for h in range(M_HEADS):
                pe.wait_ge(hm_sq, h + 1)
                if h >= 2:
                    pe.wait_ge(hm_ln, h - 1)
                for n in range(2):
                    ins = nc.tensor.matmul(ps[:, 4 + 2 * (h % 2) + n, 0:TH], ones[:],
                                           scratch(h)[:, n * TH:(n + 1) * TH],
                                           start=True, stop=True)
                ins.then_inc(hm_sum, 1)

        def act_mixer(act, s):
            if s["layer"] == 1:
                act.wait_ge(mix_loaded, 16 * (9 + 5))
                nc.scalar.copy(k_old_r[:], k_old[:]).then_inc(rounded, 1)
                for t in range(10):
                    act.wait_ge(odd_rope, t + 1)
                    nc.scalar.copy(po_r[:, t, :], po[:, t, :]).then_inc(rounded, 1)
                for c in range(CHUNKS):
                    act.wait_ge(odd_swap, 10 + c + 1)
                    act.wait_ge(odd_rope, 10 + c)
                    nc.scalar.copy(v_new[:, c, :, 0:3:2, :],
                                   ps[:, c % 4, 0:2 * P].rearrange("p (a e d) -> p a e d", e=2, d=HEAD)).then_inc(odd_rope, 1)
                act_attention(act, 1)
                return
            act.wait_ge(proj_done, 16)
            for j in range(3):
                nc.scalar.activation(y[:, j, :], pa[:, j, :], ACT.Square).then_inc(lora_sq, 1)
            act.wait_ge(lora_sum, 1)
            link(act, act_chain, nc.scalar.activation(halves(y[:, 3, :]), bank_pair(0), ACT.Ln, bias=eps_col[:, 0:1],
                                                      scale=1.0 / Q_LORA))
            link(act, act_chain, nc.scalar.activation(halves(y[:, 4, :]), bank_pair(1), ACT.Ln, bias=eps_col[:, 0:1],
                                                      scale=1.0 / P))
            nc.scalar.activation(y[:, 3:5, :], y[:, 3:5, :], ACT.Exp, scale=-0.5).then_inc(lora_rstd, 1)
            for i, (kind, h) in enumerate(BUILD):
                if kind not in BY_ACT:
                    continue
                act.wait_ge(built, i + 1)
                pair = i % 4
                if kind in ("gi", "gf"):
                    j = int(kind == "gf")
                    ins = nc.scalar.copy(halves(tmp[0:ROWS, j, :]), ps[0:ROWS, 2 * pair:2 * pair + 2, 0:TH])
                elif kind == "q":
                    ins = nc.scalar.copy(halves(qh[0:MLA_QK, h, :]), ps[0:MLA_QK, 2 * pair:2 * pair + 2, 0:TH])
                else:
                    ins = nc.scalar.copy(vtok[:, h, :, 0:3:2, :],
                                         ps[:, 2 * pair, :].rearrange("p (a e d) -> p a e d", e=2, d=MLA_V))
                ins.then_inc(built_act, 1)
            act.wait_ge(out_stored, 32)
            act_attention(act, 0)
            act.wait_ge(o_done, len(MLA_GROUPS))
            act.wait_ge(gate_rows, 1)
            link(act, act_chain, nc.scalar.activation(rows[0:ROWS, 5, :], rows[0:ROWS, 4, :], ACT.Abs))
            link(act, act_chain, nc.scalar.activation(rows[0:ROWS, 5, :], rows[0:ROWS, 5, :], ACT.Exp, scale=-1.0))
            nc.scalar.activation(rows[0:ROWS, 5, :], rows[0:ROWS, 5, :], ACT.Ln, bias=one_col[0:ROWS, 0:1]).then_inc(gate_act, 1)
            for c in range(CHUNKS):
                act.wait_ge(turn_ready, c + 1)
                pair = 2 * (c % 4)
                nc.scalar.copy(ktok[:, c, :], ps[:, pair, 0:2 * P]).then_inc(turn_act, 1)
                nc.scalar.copy(vaug[:, c, :, 0:P], ps[:, pair + 1, :].rearrange("p (h v) -> p h v", v=P)).then_inc(turn_act, 1)
            act.wait_ge(turn_ready, CHUNKS + 1)
            nc.scalar.copy(acol[:].rearrange("p c r -> p (c r)"), ps[:, 0, 0:CHUNKS * ROWS]).then_inc(turn_act, 1)
            for u in range(len(ML_UNITS)):
                act.wait_ge(decay_arg, u + 1)
                nc.scalar.activation(decay[:], decay[:], ACT.Exp).then_inc(decay_ready, 1)
                act.wait_ge(kq_ready, u + 1)
                if u >= 2:
                    act.wait_ge(head_done, u - 1)
                nc.scalar.activation(g_inter[:, u % 2, :], ps[:, G_BANK, :], ACT.Exp)
                nc.scalar.activation(floor_m[:, u % 2, :], ps[:, FLOOR_BANK, :], ACT.Exp).then_inc(gate_act, 1)
            act.wait_ge(head_done, len(ML_UNITS))
            for h in range(M_HEADS):
                nc.scalar.activation(scratch(h), hm[:, h, :], ACT.Square).then_inc(hm_sq, 1)
            for h in range(M_HEADS):
                act.wait_ge(hm_sum, h + 1)
                out = scratch(h)
                nc.scalar.activation(halves(out), bank_pair(2 + h % 2), ACT.Ln, bias=eps_col[:, 0:1],
                                     scale=1.0 / M_DV).then_inc(hm_ln, 1)
            for h in range(M_HEADS):
                act.wait_ge(hm_ln, h + 1)
                nc.scalar.activation(scratch(h), scratch(h), ACT.Exp, scale=-0.5).then_inc(hm_rstd, 1)
            for h in range(M_HEADS):
                act.wait_ge(hm_f, h + 1)
                nc.scalar.copy(hx_hi[:, 4 + h, :], hm[:, h, :]).then_inc(hm_hi, 1)

        def dve_mixer(dve, s):
            if s["layer"] == 1:
                dve.wait_ge(proj_done, 16 + 12)
                dve.wait_ge(mix_loaded, 16 * (9 + 5))
                for t in range(10):
                    dve.wait_ge(odd_swap, t + 1)
                    nc.vector.tensor_tensor(turned[:, t % 2, :], ps[:, 4 + t % 4, :], rope_o[:, 1, :], ALU.mult)
                    link(dve, dve_chain, nc.vector.tensor_tensor(po[:, t, CTX:T], po[:, t, CTX:T], rope_o[:, 0, :], ALU.mult))
                    nc.vector.tensor_tensor(po[:, t, CTX:T], po[:, t, CTX:T], turned[:, t % 2, :],
                                            ALU.add).then_inc(odd_rope, 1)
                nc.vector.memset(v_new[:, :, :, 1, :], 1.0)
                nc.vector.memset(v_old[:, :, :, 1, :], 1.0)
                dve_attention(dve, 1)
                return
            nc.vector.memset(vtok[:, :, :, 1, :], 1.0)
            dve.wait_ge(lora_rstd, 1)
            for j in range(2):
                nc.vector.scalar_tensor_tensor(out=pa[:, j, :], in0=pa[:, j, :], scalar=gains[:, j:j + 1],
                                               in1=y[:, 3, :], op0=ALU.mult, op1=ALU.mult).then_inc(lora_ready, 1)
            nc.vector.scalar_tensor_tensor(out=ckv_keys[:, 0:CTX], in0=pa[:, 2, 0:CTX], scalar=gains[:, 2:3],
                                           in1=y[:, 4, 0:CTX], op0=ALU.mult, op1=ALU.mult)
            nc.vector.scalar_tensor_tensor(out=ckv_keys[:, CTX + PAST:KEYS], in0=pa[:, 2, CTX:T], scalar=gains[:, 2:3],
                                           in1=y[:, 4, CTX:T], op0=ALU.mult, op1=ALU.mult).then_inc(lora_ready, 1)
            dve.wait_ge(mix_loaded2, 16 * 5)
            rr = slice(NOPE, MLA_QK)

            def rotate(x, swapped, scratch):
                nc.vector.tensor_tensor(y[rr, scratch, 0:LAT], swapped, rope_e[rr, 1, :], ALU.mult)
                link(dve, dve_chain, nc.vector.tensor_tensor(x, x, rope_e[rr, 0, :], ALU.mult))
                return nc.vector.tensor_tensor(x, x, y[rr, scratch, 0:LAT], ALU.add)
            for i, (kind, h) in enumerate(BUILD):
                if kind in BY_ACT:
                    continue
                dve.wait_ge(built, i + 1)
                pair = i % 4
                if kind == "kr":
                    link(dve, dve_chain, rotate(pm[rr, PM_GATES, CTX:T], ps[rr, 2 * pair, :], 0))
                    for hh in range(MLA_HEADS):
                        nc.vector.tensor_copy(kh[rr, hh, 0:CTX], pm[rr, PM_GATES, 0:CTX])
                        ins = nc.vector.tensor_copy(kh[rr, hh, CTX + PAST:KEYS], pm[rr, PM_GATES, CTX:T])
                elif kind == "k":
                    ins = nc.vector.tensor_copy(kh[0:NOPE, h, :].rearrange("p (n t) -> p n t", n=2),
                                                ps[0:NOPE, 2 * pair:2 * pair + 2, 0:KEYS // 2])
                else:
                    ins = rotate(qh[rr, h, CTX:T], ps[rr, 2 * pair, :], 1 + h % 2)
                ins.then_inc(built_dve, 1)
            dve.wait_ge(out_stored, 32)
            dve_attention(dve, 0)
            dve.wait_ge(o_done, len(MLA_GROUPS))
            R = slice(0, ROWS)
            B, A, M, G, F, SCR = range(6)
            nc.vector.tensor_scalar(rows[R, F, :], tmp[R, 1, :], row_bias[R, 1:2], None, ALU.add).then_inc(gate_rows, 1)
            link(dve, dve_chain, nc.vector.tensor_scalar(rows[R, A, :], tmp[R, 0, :], row_bias[R, 0:1], None, ALU.add))
            nc.vector.memset(m_in[:], 0.0)
            nc.vector.memset(rows[R, B, :], 0.0)
            nc.vector.memset(rows[R, M, :], 0.0)
            dve.wait_ge(gate_act, 1)
            link(dve, dve_chain, nc.vector.scalar_tensor_tensor(out=rows[R, F, :], in0=rows[R, F, :], scalar=0.0,
                                                                in1=rows[R, SCR, :], op0=ALU.min, op1=ALU.subtract))

            def seen(row, d, c):
                if d == 0:
                    return rows[0:M_HEADS, row, c * P:(c + 1) * P], rows[0:M_HEADS, row, (c + 1) * P - 1:(c + 1) * P]
                part = rows[32:32 + M_HEADS, row, c * P:(c + 1) * P]
                return part[:, ::-1], rows[32:32 + M_HEADS, row, c * P:c * P + 1]
            for d in range(2):
                for c in range(CHUNKS):
                    f = seen(F, d, c)[0]
                    ins = nc.vector.tensor_tensor_scan(out=seen(B, d, c)[0], data0=f, data1=seen(M, d, c)[0],
                                                       initial=0.0, op0=ALU.add, op1=ALU.add)
            link(dve, dve_chain, ins)
            nc.vector.tensor_tensor(rows[R, A, :], rows[R, A, :], rows[R, B, :], ALU.subtract)
            nc.vector.tensor_copy(m_in[0:M_HEADS, 1:2], row_bias[0:M_HEADS, 2:3])
            link(dve, dve_chain, nc.vector.tensor_copy(m_in[32:32 + M_HEADS, 4:5], row_bias[32:32 + M_HEADS, 2:3]))
            for step in range(5):
                for d, order in ((0, (1, 2, 3, 4, 0)), (1, (4, 3, 2, 1, 0))):
                    c = order[step]
                    r = slice(32 * d, 32 * d + M_HEADS)
                    a = seen(A, d, c)[0]
                    ins = nc.vector.tensor_tensor_scan(out=seen(M, d, c)[0], data0=a, data1=a,
                                                       initial=m_in[r, c:c + 1], op0=ALU.max, op1=ALU.max)
                link(dve, dve_chain, ins)
                for d, order in ((0, (2, 3, 4, 7, 6)), (1, (3, 2, 1, 7, 6))):
                    c = ((1, 2, 3, 4, 0), (4, 3, 2, 1, 0))[d][step]
                    to = order[step]
                    r = slice(32 * d, 32 * d + M_HEADS)
                    ins = nc.vector.tensor_tensor(m_in[r, to:to + 1], seen(B, d, c)[1], seen(M, d, c)[1], ALU.add)
                link(dve, dve_chain, ins)
            nc.vector.tensor_scalar(rows3[R, 0, :], rows[R, M, :], -1.0, None, ALU.mult)
            for c in range(CHUNKS):
                nc.vector.tensor_scalar(rows3[R, 1, c * P:(c + 1) * P], rows[R, M, c * P:(c + 1) * P], -1.0,
                                        m_in[R, c:c + 1], ALU.mult, ALU.add)
            nc.vector.scalar_tensor_tensor(out=rows3[R, 2, :], in0=rows[R, B, :], scalar=-1.0, in1=rows[R, M, :],
                                           op0=ALU.mult, op1=ALU.subtract).then_inc(rows_ready, 1)
            dve.wait_ge(turn_act, 2 * CHUNKS + 1)
            dve.wait_ge(mix_loaded3, 32)

            def weights(u):
                (head, d), rs, blocks = ML_UNITS[u], ml_rows(ML_UNITS[u]), ml_blocks(ML_UNITS[u])
                dve.wait_ge(m_ready, u + 1)
                for b, (h, d_b, c) in enumerate(blocks):
                    cols, row = slice(b * P, (b + 1) * P), 32 * d_b + h
                    ins = nc.vector.scalar_tensor_tensor(out=decay[:, cols], in0=ps[:, M_BANK, cols],
                                                         scalar=acol[:, c, row:row + 1], in1=causal[:, d_b, :],
                                                         op0=ALU.add, op1=ALU.add)
                ins.then_inc(decay_arg, 1)
                dve.wait_ge(gate_act, 1 + u + 1)
                if head is not None:
                    nc.vector.tensor_tensor(q_inter[rs, head % 2, d, :], pm[rs, PM_Q + head // 2, CTX:T],
                                            g_inter[rs, u % 2, :], ALU.mult)
                dve.wait_ge(decay_ready, u + 1)
                nc.vector.scalar_tensor_tensor(out=weigh[:, u % 2, :], in0=ps[:, KQ_BANK, :], scalar=M_DK ** -0.5,
                                               in1=decay[:], op0=ALU.mult, op1=ALU.mult)
                for b, (h, d_b, c) in enumerate(blocks):
                    last = (b + 1) * P - 1 if d_b == 0 else b * P
                    ins = nc.vector.tensor_scalar(k_w[:, b, :], ktok[:, c, h * M_DK:(h + 1) * M_DK],
                                                  decay[:, last:last + 1], M_DK ** -0.5, ALU.mult, ALU.mult)
                ins.then_inc(weigh_ready, 1)

            def states(u):
                (head, d), rs = ML_UNITS[u], ml_rows(ML_UNITS[u])
                if head is None:
                    dve.wait_ge(gain_ready, u + 1)
                    nc.vector.tensor_copy(state_out[rs].rearrange("p d a v -> p d (a v)"),
                                          ps[rs, G_BANK:G_BANK + 2, :]).then_inc(state_ready, 1)
                    return
                order = ml_order(d)
                link(dve, dve_chain, nc.vector.tensor_copy(state[rs, order[0], :], state0[rs, d, head // 2, :]))
                dve.wait_ge(gain_ready, u + 1)
                for j in range(3):
                    c, nxt = order[j], order[j + 1]
                    last = c * P - 1 if d == 0 else (c - 1) * P
                    ins = nc.vector.scalar_tensor_tensor(out=state[rs, nxt, :], in0=state[rs, c, :],
                                                         scalar=g_inter[rs, u % 2, last:last + 1],
                                                         in1=gain_cols(j)[rs], op0=ALU.mult, op1=ALU.add)
                    if j < 2:
                        link(dve, dve_chain, ins)
                ins.then_inc(state_ready, 1)

            def divisor(u):
                den = ps[:, NUM_BANK + 2 * (u % 2) + 1, :]
                dve.wait_ge(numden_ready, u + 1)
                if u:
                    dve.wait_ge(head_done, u)
                link(dve, dve_chain, nc.vector.tensor_tensor(hs[:], den, floor_m[:, u % 2, :], ALU.max))
                link(dve, dve_chain, nc.vector.scalar_tensor_tensor(out=hs[:], in0=den, scalar=-1.0, in1=hs[:],
                                                                    op0=ALU.mult, op1=ALU.max))

            def quotient(u):
                head, d = ML_UNITS[u]
                num = ps[:, NUM_BANK + 2 * (u % 2), :]
                link(dve, dve_chain, nc.vector.reciprocal(hs[:], hs[:]))
                if head is None:
                    link(dve, dve_chain, nc.vector.tensor_tensor(hs[:], num, hs[:], ALU.mult))
                    by = hs[:].rearrange("p (d h t) -> p d h t", h=2, t=P)
                    nc.vector.tensor_tensor(hm[:, d:M_HEADS:2, 0:CTX], by[:, 0], by[:, 1], ALU.add).then_inc(head_done, 1)
                elif d == 0:
                    nc.vector.tensor_tensor(hm[:, head, CTX:T], num, hs[:], ALU.mult).then_inc(head_done, 1)
                else:
                    link(dve, dve_chain, nc.vector.tensor_tensor(hs[:], num, hs[:], ALU.mult))
                    nc.vector.tensor_tensor(hm[:, head, CTX:T], hm[:, head, CTX:T], hs[:], ALU.add).then_inc(head_done, 1)
            dve.wait_ge(ml_filled, 1)
            for u in range(len(ML_UNITS)):
                weights(u)
                if u:
                    divisor(u - 1)
                states(u)
                if u:
                    quotient(u - 1)
            divisor(len(ML_UNITS) - 1)
            quotient(len(ML_UNITS) - 1)
            for h in range(M_HEADS):
                dve.wait_ge(hm_rstd, h + 1)
                link(dve, dve_chain, nc.vector.scalar_tensor_tensor(
                    out=hm[:, h, :], in0=hm[:, h, :], scalar=gains[:, 3 + h:4 + h],
                    in1=scratch(h), op0=ALU.mult, op1=ALU.mult))
                nc.vector.tensor_tensor(hm[:, h, :], hm[:, h, :], pm[:, PM_O + h, :], ALU.mult).then_inc(hm_f, 1)
            for h in range(M_HEADS):
                dve.wait_ge(hm_hi, h + 1)
                nc.vector.tensor_tensor(hx_lo[:, 4 + h, :], hm[:, h, :], hx_hi[:, 4 + h, :].bitcast(F32),
                                        ALU.subtract).then_inc(mix_ready, 1)

        def sp_mixer_loads(sp, s):
            sp.wait_ge(w_used, s["chunk"])
            if s["layer"] == 0:
                sp.dma_start(w_qb[:], io["w_qb"]).then_inc(mix_loaded, 16)
                for h in range(MLA_HEADS):
                    sp.dma_start(kh[NOPE:MLA_QK, h, CTX:CTX + PAST], io["krope_old"]).then_inc(mix_loaded, 16)
            else:
                for e in range(2):
                    sp.dma_start(v_old[:, :, :, 2 * e, :], io["v_old"][:, e]).then_inc(mix_loaded, 16)
                for dst, name in ((k_old, "k_old"), (rope_o, "rope_o"), (swap_o, "swap_o")):
                    sp.dma_start(dst[:], io[name]).then_inc(mix_loaded, 16)

        def sp_mixer_loads2(sp, s):
            sp.wait_ge(w_used, s["chunk"] + 2 * s["tiles_in"])
            if s["layer"] == 0:
                for dst, name in ((rope_e, "rope_e"), (swap_e, "swap_e"), (pick_rows, "pick_rows"), (w_kvb, "w_kvb")):
                    sp.dma_start(dst[:], io[name]).then_inc(mix_loaded2, 16)
                sp.dma_start(ckv_keys[:, CTX:CTX + PAST], io["ckv_old"]).then_inc(mix_loaded2, 16)
                sp.wait_ge(lora_ready, 3)
                sp.dma_start(io["out_ckv"], ckv_keys[:, 0:CTX]).then_inc(out_stored, 16)
                sp.dma_start(io["out_krope"], pm[NOPE:MLA_QK, PM_GATES, 0:CTX]).then_inc(out_stored, 16)
                sp.wait_ge(o_done, len(MLA_GROUPS))
                sp.dma_start(onehot[0:ROWS], io["onehot"]).then_inc(mix_loaded3, 16)
                sp.dma_start(state0[:], io["state0"]).then_inc(mix_loaded3, 16)
                sp.wait_ge(head_done, len(ML_UNITS))
                sp.dma_start(io["out_state"], state_out[:]).then_inc(out_stored, 16)
                sp.dma_start(io["out_m"], m_in[0:ROWS, 6:7]).then_inc(out_stored, 16)
            else:
                sp.wait_ge(proj_done, 16 + 12)
                sp.dma_start(io["out_kv"], po[:, 8:12, 0:CTX]).then_inc(out_stored, 16)

        @block.sync
        def _(sp):
            for dst, name in ((cond, "cond"), (norm_g, "norm_g"), (ada_bias, "ada_b"), (pick, "pick"),
                              (neg_sink[:, 0:S_HEADS], "sinks"), (gains, "gains"), (row_bias, "row_bias"), (ident, "ident"),
                              (causal, "causal")):
                sp.dma_start(dst if name == "sinks" else dst[:], io[name]).then_inc(in_loaded, 16)

            def load(c, slot, src, tiles, wait=True):
                if wait:
                    sp.wait_ge(lo_done, c - 1)
                sp.dma_start(w_raw[:, slot, 0:tiles * P], src).then_inc(raw_ready[slot], 16)

            for q in range(ADA_SLOTS):
                sp.dma_start(ada_raw[:, q], ada_w[q]).then_inc(ada_loaded[q], 16)
            for k in range(KT):
                sp.dma_start(xT[:, k, :], io["x"][:, k, :]).then_inc(x_loaded, 16)
            with sp.Fori(1, ADA_GROUPS // ADA_SLOTS) as i:
                for q in range(ADA_SLOTS):
                    sp.wait_ge(ada_lo_done, 8 * i + (2 * q - 6))
                    sp.dma_start(ada_raw[:, q], ada_w[4 * i + q]).then_inc(ada_loaded[q], 16)
            chunk = 0
            for s in SUBS:
                if s["kind"] == "ffn":
                    f = s["f"]
                    if chunk == 0:
                        for q in range(2):
                            load(q, q, ffn_gu[f, 0, q], 8, wait=False)
                    with sp.Fori(int(chunk == 0), FT) as b:
                        for q in range(2):
                            load(2 * b + (chunk + q), q, ffn_gu[f, b, q], 8)
                    chunk += 2 * FT
                    with sp.Fori(0, KT) as b:
                        for q in range(2):
                            load(2 * b + (chunk + q), q, ffn_dn[f, b, q], 11)
                    chunk += 2 * KT
                else:
                    name = ("even", "odd")[s["layer"]]
                    for q in range(2):
                        load(chunk + q, q, io[name + "_in"][q], 8)
                    sp_mixer_loads(sp, s)
                    with sp.Fori(1, s["tiles_in"]) as b:
                        for q in range(2):
                            load(2 * b + (chunk + q), q, io[name + "_in"][2 * b + q], 8)
                    chunk += 2 * s["tiles_in"]
                    for q in range(2):
                        load(chunk + q, q, io[name + "_out"][q], 8)
                    sp_mixer_loads2(sp, s)
                    with sp.Fori(1, KT // 2) as b:
                        for q in range(2):
                            load(2 * b + (chunk + q), q, io[name + "_out"][2 * b + q], 8)
                    chunk += KT
            for k in range(KT):
                sp.wait_ge(x_ready[k % 2], KT // 2 * (len(SUBS) - 1) + k // 2 + 1)
                sp.dma_start(io["y"][:, k, :], xT[:, k, :]).then_inc(out_stored, 16)
            sp.wait_ge(out_stored, 16 * (KT + N_OUT))

        @block.scalar
        def _(act):
            act.wait_ge(in_loaded, CONSTS)
            act.wait_ge(const_ready, 1)
            nc.scalar.copy(ones_r[:], ones[:]).then_inc(attn_const, 1)
            nc.scalar.copy(ident_b[:], ident[:]).then_inc(attn_const, 1)
            for i in range(4):
                nc.scalar.copy(causal_b[:, :, i, :], causal[:]).then_inc(attn_const, 1)
            nc.scalar.activation(cond_silu[:], cond[:], ACT.Silu).then_inc(cond_act, 1)
            act.wait_ge(cond_act, 1)
            act.wait_ge(cond_ready, 1)
            nc.scalar.copy(cond_hl[:, :, 0:2], cond_silu[:]).then_inc(cond_act, 1)

            def ada_split(g, q, peeled=False):
                act.wait_ge(ada_loaded[q], 16 if peeled else 4 * g + (16 - 4 * q))
                if not (peeled and q < 2):
                    act.wait_ge(ada_used, g - 1)
                for e in range(2):
                    ks = slice(4 * e, 4 * e + 4)
                    nc.scalar.copy(ada_hi[:, q % 2, ks, :], ada_raw[:, q, ks, :]).then_inc(ada_hi_done, 1)

            def ada_rows(g, q, peeled=False):
                act.wait_ge(ada_used, g + 1)
                if not (peeled and q < 2):
                    act.wait_ge(col_ready, g - 1)
                nc.scalar.copy(mod_rows[:, q % 2, :], ps[:, q % 2, :]).then_inc(row_ready, 1)
            for q in range(ADA_SLOTS):
                ada_split(q, q, peeled=True)
                if q:
                    ada_rows(q - 1, q - 1, peeled=True)
            with act.Fori(1, ADA_GROUPS // ADA_SLOTS) as i:
                for q in range(ADA_SLOTS):
                    ada_split(4 * i + q, q)
                    ada_rows(4 * i + (q - 1), (q - 1) % 4)
            ada_rows(ADA_GROUPS - 1, 3)
            for q in range(2):
                split_hi(act, q, q, 8, wait_used=False)

            chunk = 0
            for si, s in enumerate(SUBS):
                n = si

                def rms(count, sums, value):
                    act.wait_ge(sums, value)
                    link(act, act_chain, nc.scalar.activation(halves(rstd[:]), bank_pair(0), ACT.Ln,
                                                              bias=eps_col[:, 0:1], scale=1.0 / D))
                    nc.scalar.activation(rstd[:], rstd[:], ACT.Exp, scale=-0.5).then_inc(rstd_ready, 1)

                gate0 = (s["layer"] * NMOD + s["idx"] + 2) * KT

                def evacuate_gated(buf, k, pair, gate0):
                    for bank, a, b, ci in ((0, 0, CTX, 0), (0, CTX, TH, 1), (1, TH, T, 1)):
                        nc.scalar.activation(buf[:, k, a:b], ps[:, 2 * pair + bank, a - bank * TH:b - bank * TH],
                                             ACT.Identity, scale=mods[:, bass.ds(gate0 + k, 1), ci:ci + 1].rearrange(
                                                 "p j c -> p (j c)"))

                def squares(n):
                    for k in range(KT):
                        if n == 0:
                            act.wait_ge(x_loaded, 16 * KT)
                        else:
                            act.wait_ge(x_ready[k % 2], KT // 2 * (n - 1) + k // 2 + 1)
                        if KT * n + k >= 2:
                            act.wait_ge(xsq_used, KT * n + k - 1)
                        nc.scalar.activation(tmp[:, k % 2, :], xT[:, k, :], ACT.Square).then_inc(xsq_ready, 1)

                squares(n)
                rms(2 * n, xsq_used, KT * (n + 1))
                for k in range(KT):
                    act.wait_ge(pre_ready, KT * n + k + 1)
                    for ci, (a, b) in enumerate(GROUPS):
                        last = nc.scalar.activation(hx_hi[:, k, a:b], tmp[:, k % 2, a:b], ACT.Identity,
                                                    bias=mod_col(s["layer"], s["idx"], k, ci))
                    last.then_inc(hxhi_ready, 1)
                if s["kind"] == "ffn":
                    g0 = s["gu0"]

                    def gu_block(m, par, next_tiles, chunk=chunk, g0=g0):
                        for q in (2, 3):
                            split_hi(act, 2 * m + (chunk + q), q % 2, next_tiles)
                        act.wait_ge(w_used, 2 * m + (chunk + 2))
                        nc.scalar.activation(halves(silu_g[:, par, :]), bank_pair(2 * par),
                                             ACT.Silu).then_inc(silu_done, 1)
                        act.wait_ge(mul_done, m + (g0 + 1))
                        nc.scalar.copy(halves(hh_hi[:, m, :]), bank_pair(2 * par + 1)).then_inc(hhi_done, 1)
                    with act.Fori(0, FT // 2 - 1) as i:
                        for par in range(2):
                            gu_block(2 * i + par, par, 8)
                    gu_block(FT - 2, 0, 8)
                    gu_block(FT - 1, 1, 11)
                    chunk += 2 * FT

                    def dn_block(b, par, next_tiles, chunk=chunk, n=n, gate0=gate0):
                        if next_tiles:
                            for q in (2, 3):
                                split_hi(act, 2 * b + (chunk + q), q % 2, next_tiles)
                        act.wait_ge(w_used, 2 * b + (chunk + 2))
                        evacuate_gated(y, b, 2 * par, gate0)
                        act.wait_ge(ssq_done, b + ((KT + 1) * n + 1))
                        nc.scalar.activation(halves(sq[:, par, :]), bank_pair(2 * par),
                                             ACT.Square).then_inc(sq_ready, 1)
                    with act.Fori(0, KT // 2 - 1) as i:
                        for par in range(2):
                            dn_block(2 * i + par, par, 11)
                    dn_block(KT - 2, 0, 11)
                    dn_block(KT - 1, 1, 8 if si + 1 < len(SUBS) else 0)
                    chunk += 2 * KT
                else:
                    nblk = s["tiles_in"]
                    for b in range(nblk):
                        for q in (2, 3):
                            split_hi(act, 2 * b + chunk + q, q % 2, 8)
                        for q in range(2):
                            t = 2 * b + q
                            act.wait_ge(w_used, chunk + t + 1)
                            func, out = ACT.Copy, None
                            if s["layer"] == 1:
                                out = po[:, t, :]
                            elif t < 3:
                                out = pa[:, t, :]
                            else:
                                out = pm[:, t - 3, :]
                                func = ACT.Sigmoid if t - 3 >= PM_O else ACT.Copy
                            nc.scalar.activation(halves(out), bank_pair(2 * (b % 2) + q), func).then_inc(proj_done, 1)
                    chunk += 2 * nblk
                    act_mixer(act, s)
                    act.wait_ge(out_stored, 16 * (4 + s["layer"]))
                    for b in range(KT // 2):
                        if b < KT // 2 - 1 or si + 1 < len(SUBS):
                            for q in (2, 3):
                                split_hi(act, 2 * b + chunk + q, q % 2, 8)
                        for q in range(2):
                            t = 2 * b + q
                            act.wait_ge(w_used, chunk + t + 1)
                            evacuate_gated(y_m, t, 2 * (b % 2) + q, gate0)
                            act.wait_ge(ssq_done, t + ((KT + 1) * n + 1))
                            nc.scalar.activation(halves(sq_m[:, t % 2, :]), bank_pair(2 * (b % 2) + q),
                                                 ACT.Square).then_inc(sq_ready, 1)
                    chunk += KT
                rms(2 * n + 1, msq_ready, n + 1)

        @block.vector
        def _(dve):
            nc.vector.memset(cond_hl[:].bitcast(F32), 0.0).then_inc(cond_ready, 1)
            nc.vector.memset(ones[:], 1.0).then_inc(const_ready, 1)
            nc.vector.memset(eps_col[:], EPS).then_inc(const_ready, 1)
            nc.vector.memset(sink_half[:], 0.0).then_inc(dve_chain, 1)
            chained[dve_chain.name] = 1
            dve.wait_ge(dve_chain, 1)
            nc.vector.memset(sink_half[:, 1, :], 1.0)
            nc.vector.memset(one_col[:], 1.0).then_inc(const_ready, 1)
            dve.wait_ge(cond_act, 2)
            nc.vector.tensor_tensor(cond_hl[:, :, 2:4], cond_silu[:], cond_hl[:, :, 0:2].bitcast(F32),
                                    ALU.subtract).then_inc(cond_ready, 1)

            def ada_split(g, q):
                for e in range(2):
                    dve.wait_ge(ada_hi_done, 2 * g + (e + 1))
                    ks = slice(4 * e, 4 * e + 4)
                    nc.vector.tensor_tensor(ada_lo[:, q % 2, ks, :], ada_raw[:, q, ks, :],
                                            ada_hi[:, q % 2, ks, :].bitcast(F32), ALU.subtract).then_inc(ada_lo_done, 1)

            def ada_add(g, q):
                dve.wait_ge(col_ready, g + 1)
                cols = ps[:, 2 + q % 2, 0:8].rearrange("p (j c) -> p j c", c=2)
                nc.vector.tensor_tensor(mods[:, bass.ds(4 * g, 4), :], cols, ada_bias[:, bass.ds(4 * g, 4), :],
                                        ALU.add).then_inc(mod_added, 1)
            dve.wait_ge(in_loaded, CONSTS)
            for q in range(ADA_SLOTS):
                ada_split(q, q)
                if q >= 2:
                    ada_add(q - 2, q)
            with dve.Fori(1, ADA_GROUPS // ADA_SLOTS) as i:
                for q in range(ADA_SLOTS):
                    ada_split(4 * i + q, q)
                    ada_add(4 * i + (q - 2), q)
            for q in range(2):
                ada_add(ADA_GROUPS - 2 + q, q)
            for q in range(2):
                split_lo(dve, q, q, 8, wait_used=False)
            dve.wait_ge(mod_added, ADA_GROUPS)
            nc.vector.tensor_scalar(neg_sink[:, S_HEADS:], neg_sink[:, 0:S_HEADS], -HEAD ** 0.5, None, ALU.mult)
            for layer in range(2):
                for sub in range(3):
                    for ci in range(2):
                        j = (layer * NMOD + 3 * sub + 1) * KT
                        last = nc.vector.scalar_tensor_tensor(out=mods[:, j:j + KT, ci], in0=mods[:, j:j + KT, ci],
                                                              scalar=1.0, in1=norm_g[:, layer, 2 * sub, :],
                                                              op0=ALU.add, op1=ALU.mult)
                        j += KT
                        last = nc.vector.scalar_tensor_tensor(out=mods[:, j:j + KT, ci], in0=mods[:, j:j + KT, ci],
                                                              scalar=1.0 if sub == 1 else 0.5,
                                                              in1=norm_g[:, layer, 2 * sub + 1, :],
                                                              op0=ALU.mult, op1=ALU.mult)
            last.then_inc(mods_ready, 1)
            dve.wait_ge(mods_ready, 1)

            chunk = 0
            for si, s in enumerate(SUBS):
                n = si
                dve.wait_ge(rstd_ready, 2 * n + 1)

                def scaled(k):
                    if k >= 2:
                        dve.wait_ge(hx_ready, KT * n + k - 1)
                    for ci, (a, b) in enumerate(GROUPS):
                        last = nc.vector.scalar_tensor_tensor(out=tmp[:, k % 2, a:b], in0=xT[:, k, a:b],
                                                              scalar=mod_col(s["layer"], s["idx"] + 1, k, ci),
                                                              in1=rstd[:, a:b], op0=ALU.mult, op1=ALU.mult)
                    last.then_inc(pre_ready, 1)

                def low(k):
                    dve.wait_ge(hxhi_ready, KT * n + k + 1)
                    for ci, (a, b) in enumerate(GROUPS):
                        last = nc.vector.scalar_tensor_tensor(out=hx_lo[:, k, a:b], in0=tmp[:, k % 2, a:b],
                                                              scalar=mod_col(s["layer"], s["idx"], k, ci),
                                                              in1=hx_hi[:, k, a:b].bitcast(F32), op0=ALU.add,
                                                              op1=ALU.subtract)
                    last.then_inc(hx_ready, 1)
                scaled(0)
                for k in range(1, KT):
                    scaled(k)
                    low(k - 1)
                low(KT - 1)
                if s["kind"] == "ffn":
                    g0 = s["gu0"]

                    def gu_block(m, par, next_tiles, chunk=chunk, g0=g0):
                        for q in (2, 3):
                            split_lo(dve, 2 * m + (chunk + q), q % 2, next_tiles)
                        dve.wait_ge(silu_done, m + (g0 + 1))
                        nc.vector.tensor_tensor(bank_pair(2 * par + 1), bank_pair(2 * par + 1),
                                                halves(silu_g[:, par, :]), ALU.mult).then_inc(mul_done, 1)
                        dve.wait_ge(hhi_done, m + (g0 + 1))
                        nc.vector.tensor_tensor(halves(hh_lo[:, m, :]), bank_pair(2 * par + 1),
                                                halves(hh_hi[:, m, :]).bitcast(F32),
                                                ALU.subtract).then_inc(block_free, 1)
                    with dve.Fori(0, FT // 2 - 1) as i:
                        for par in range(2):
                            gu_block(2 * i + par, par, 8)
                    gu_block(FT - 2, 0, 8)
                    gu_block(FT - 1, 1, 11)
                    chunk += 2 * FT
                    nc.vector.memset(ssq[:], 0.0).then_inc(ssq_done, 1)

                    def dn_block(b, par, next_tiles, chunk=chunk, n=n):
                        if next_tiles:
                            for q in (2, 3):
                                split_lo(dve, 2 * b + (chunk + q), q % 2, next_tiles)
                        dve.wait_ge(sq_ready, b + (KT * n + 1))
                        dve.wait_ge(ssq_done, b + ((KT + 1) * n + 1))
                        nc.vector.tensor_tensor(ssq[:], ssq[:], sq[:, par, :], ALU.add).then_inc(ssq_done, 1)
                    with dve.Fori(0, KT // 2 - 1) as i:
                        for par in range(2):
                            dn_block(2 * i + par, par, 11)
                    dn_block(KT - 2, 0, 11)
                    dn_block(KT - 1, 1, 8 if si + 1 < len(SUBS) else 0)
                    chunk += 2 * KT
                else:
                    nblk = s["tiles_in"]
                    for b in range(nblk):
                        for q in (2, 3):
                            split_lo(dve, 2 * b + chunk + q, q % 2, 8)
                    chunk += 2 * nblk
                    dve_mixer(dve, s)
                    for b in range(KT // 2):
                        if b < KT // 2 - 1 or si + 1 < len(SUBS):
                            for q in (2, 3):
                                split_lo(dve, 2 * b + chunk + q, q % 2, 8)
                        if b == 0:
                            dve.wait_ge(out_stored, 16 * (4 + s["layer"]))
                            nc.vector.memset(ssq_m[:], 0.0).then_inc(ssq_done, 1)
                        for q in range(2):
                            t = 2 * b + q
                            dve.wait_ge(sq_ready, KT * n + t + 1)
                            dve.wait_ge(ssq_done, t + ((KT + 1) * n + 1))
                            nc.vector.tensor_tensor(ssq_m[:], ssq_m[:], sq_m[:, t % 2, :], ALU.add).then_inc(ssq_done, 1)
                    chunk += KT
                yb = y if s["kind"] == "ffn" else y_m
                dve.wait_ge(rstd_ready, 2 * n + 2)

                def scaled_y(k):
                    nc.vector.tensor_tensor(yb[:, k, :], yb[:, k, :], rstd[:], ALU.mult).then_inc(y_scaled, 1)

                def added(k):
                    dve.wait_ge(y_scaled, KT * n + k + 1)
                    nc.vector.tensor_tensor(xT[:, k, :], xT[:, k, :], yb[:, k, :], ALU.add).then_inc(x_ready[0], 1)
                for k in range(KT):
                    scaled_y(k)
                    if k % 2:
                        added(k - 1)

        @block.gpsimd
        def _(pool):
            for n, s in enumerate(SUBS):
                if s["kind"] == "mix" and s["layer"] == 0:
                    pool.wait_ge(o_done, len(MLA_GROUPS))
                    nc.gpsimd.memset(state[:], 0.0)
                    nc.gpsimd.memset(q_inter[:], 0.0)
                    nc.gpsimd.memset(vaug[:, :, :, P:], 1.0).then_inc(ml_filled, 1)
                yb = y if s["kind"] == "ffn" else y_m
                for k in range(1, KT, 2):
                    pool.wait_ge(y_scaled, KT * n + k + 1)
                    nc.gpsimd.tensor_tensor(xT[:, k, :], xT[:, k, :], yb[:, k, :], ALU.add).then_inc(x_ready[1], 1)

        @block.tensor
        def _(pe):
            pe.wait_ge(const_ready, 2)
            pe.wait_ge(cond_ready, 2)

            def ada_products(g, q, peeled=False):
                if not (peeled and q < 2):
                    pe.wait_ge(row_ready, g - 1)
                for k in range(KT):
                    if k % 4 == 0:
                        pe.wait_ge(ada_lo_done, 2 * g + (k // 4 + 1))
                    for part in (ada_hi, ada_lo):
                        last = nc.tensor.matmul(ps[:, q % 2, :], cond_hl[:, k, :], part[:, q % 2, k, :],
                                                start=(k == 0 and part is ada_hi),
                                                stop=(k == KT - 1 and part is ada_lo))
                last.then_inc(ada_used, 1)

            def ada_columns(g, q, peeled=False):
                pe.wait_ge(row_ready, g + 1)
                if not (peeled and q < 2):
                    pe.wait_ge(mod_added, g - 1)
                for j in range(4):
                    last = nc.tensor.matmul(ps[:, 2 + q % 2, 2 * j:2 * j + 2], mod_rows[:, q % 2, j * P:(j + 1) * P],
                                            pick[:], start=True, stop=True)
                last.then_inc(col_ready, 1)
            for q in range(ADA_SLOTS):
                ada_products(q, q, peeled=True)
                if q:
                    ada_columns(q - 1, q - 1, peeled=True)
            with pe.Fori(1, ADA_GROUPS // ADA_SLOTS) as i:
                for q in range(ADA_SLOTS):
                    ada_products(4 * i + q, q)
                    ada_columns(4 * i + (q - 1), (q - 1) % 4)
            ada_columns(ADA_GROUPS - 1, 3)
            pe.wait_ge(mod_added, ADA_GROUPS)

            def tile_product(out_bank, q, hi, lo, t, k, start, stop):
                wh = w_hi[:, q, t * P:(t + 1) * P]
                wl = w_lo[:, q, t * P:(t + 1) * P]
                for w, a in ((wh, hi), (wh, lo), (wl, hi)):
                    for h in range(2):
                        last = nc.tensor.matmul(ps[:, out_bank + h, 0:TH], w, a[:, k, h * TH:(h + 1) * TH],
                                                start=(start and w is wh and a is hi), stop=(stop and w is wl))
                return last

            def product(out_bank, q, hi, lo, k0, tiles, first, last_chunk):
                for t in range(tiles):
                    last = tile_product(out_bank, q, hi, lo, t, k0 + t, first and t == 0, last_chunk and t == tiles - 1)
                last.then_inc(w_used, 1)

            def first_products(chunk, ready):
                pe.wait_ge(lo_done, chunk + 2)
                for t in range(KT):
                    pe.wait_ge(*ready(t))
                    for q in range(2):
                        last = tile_product(2 * q, q, hx_hi, hx_lo, t, t, t == 0, t == KT - 1)
                        if t == KT - 1:
                            last.then_inc(w_used, 1)

            chunk = 0
            for si, s in enumerate(SUBS):
                n = si
                for k in range(KT):
                    pe.wait_ge(xsq_ready, KT * n + k + 1)
                    for h in range(2):
                        last = nc.tensor.matmul(ps[:, h, 0:TH], ones[:], tmp[:, k % 2, h * TH:(h + 1) * TH],
                                                start=(k == 0), stop=(k == KT - 1))
                    last.then_inc(xsq_used, 1)
                pe.wait_ge(rstd_ready, 2 * n + 1)
                if s["kind"] == "ffn":
                    g0 = s["gu0"]

                    def gu_block(m, par, wait_free=True, chunk=chunk, g0=g0, n=n):
                        for q in range(2):
                            pe.wait_ge(lo_done, 2 * m + (chunk + q + 1))
                            if q == 0 and wait_free:
                                pe.wait_ge(block_free, m + (g0 - 1))
                            product(4 * par + 2 * q, q, hx_hi, hx_lo, 0, 8, True, True)
                    first_products(chunk, lambda t, n=n: (hx_ready, KT * n + t + 1))
                    gu_block(1, 1, wait_free=False)
                    with pe.Fori(1, FT // 2) as i:
                        for par in range(2):
                            gu_block(2 * i + par, par)
                    chunk += 2 * FT
                    pe.wait_ge(block_free, g0 + FT - 1)

                    def dn_block(b, par, wait_free=True, chunk=chunk, n=n, whole=g0 + FT):
                        for q in range(2):
                            pe.wait_ge(lo_done, 2 * b + (chunk + q + 1))
                            if q == 1 and not wait_free:
                                pe.wait_ge(block_free, whole)
                            if q == 0 and wait_free:
                                pe.wait_ge(sq_ready, b + (KT * n - 1))
                            product(4 * par, q, hh_hi, hh_lo, 11 * q, 11, q == 0, q == 1)
                    dn_block(0, 0, wait_free=False)
                    dn_block(1, 1, wait_free=False)
                    with pe.Fori(1, KT // 2) as i:
                        for par in range(2):
                            dn_block(2 * i + par, par)
                    chunk += 2 * KT
                else:
                    first_products(chunk, lambda t, n=n: (hx_ready, KT * n + t + 1))
                    for b in range(1, s["tiles_in"]):
                        for q in range(2):
                            pe.wait_ge(lo_done, chunk + 2 * b + q + 1)
                            if q == 0 and b >= 2:
                                pe.wait_ge(proj_done, 16 * s["layer"] + 2 * (b - 1))
                            product(4 * (b % 2) + 2 * q, q, hx_hi, hx_lo, 0, 8, True, True)
                    chunk += 2 * s["tiles_in"]
                    pe.wait_ge(proj_done, 16 * s["layer"] + 2 * s["tiles_in"])
                    pe_mixer(pe, s)
                    n_mla, n_swa = len(MLA_GROUPS), len(SWA_GROUPS)
                    if s["layer"] == 0:
                        first_products(chunk, lambda t: (o_done, n_mla) if t < 4 else (mix_ready, t - 3))
                    else:
                        first_products(chunk, lambda t: (o_done, n_mla + n_swa // (2 if t < 4 else 1)))
                    for b in range(1, KT // 2):
                        for q in range(2):
                            pe.wait_ge(lo_done, chunk + 2 * b + q + 1)
                            if q == 0 and b >= 2:
                                pe.wait_ge(sq_ready, KT * n + 2 * (b - 1))
                            product(4 * (b % 2) + 2 * q, q, hx_hi, hx_lo, 0, 8, True, True)
                    chunk += KT
                pe.wait_ge(ssq_done, (KT + 1) * (n + 1))
                pe.wait_ge(sq_ready, KT * (n + 1))
                sums = ssq if s["kind"] == "ffn" else ssq_m
                for h in range(2):
                    last = nc.tensor.matmul(ps[:, h, 0:TH], ones[:], sums[:, h * TH:(h + 1) * TH],
                                            start=True, stop=True)
                last.then_inc(msq_ready, 1)


def lay_out(inp):
    import numpy as np
    f = {k: np.asarray(v) for k, v in inp.items()}
    c = np.ascontiguousarray
    x = np.concatenate([f["x_prompt"][0], f["x_sample"][0]], 0)
    out = {"x": c(x.T.reshape(KT, P, T).transpose(1, 0, 2))}
    out["cond"] = c(np.stack([f["c_ctx"], f["c"][0]], -1).reshape(KT, P, 2).transpose(1, 0, 2))
    out["norm_g"] = c(f["norm_g"].reshape(2, 6, KT, P).transpose(3, 0, 1, 2))
    b = f["ada_b"].reshape(2 * NMOD * KT, P).T
    out["ada_b"] = c(np.stack([b, b], -1))
    pick = np.zeros((P, 2), np.float32)
    pick[[0, 2], 0] = 1
    pick[[1, 3], 1] = 1
    out["pick"] = pick
    w = f["ada_w"].reshape(2, KT, P, ADA_GROUPS // 2, 512).transpose(0, 3, 2, 1, 4)
    out["ada_w"] = c(w).reshape(ADA_GROUPS, P, KT, 512)
    def gu(w):
        return w.reshape(4, KT, P, FT, P).transpose(0, 3, 2, 1, 4)
    out["ffn_gu"] = c(np.stack([gu(f["ffn_w_gate"]), gu(f["ffn_w_up"])], 2)).reshape(4, FT, 2, P, 1024)
    w = f["ffn_w_down"].reshape(4, 2, 11, P, KT, P).transpose(0, 4, 1, 3, 2, 5)
    out["ffn_dn"] = c(w).reshape(4, KT, 2, P, SLOT)

    def tiles(w):
        n = w.shape[1] // P
        return c(w.reshape(KT, P, n, P).transpose(2, 1, 0, 3)).reshape(n, P, KT * P)

    w = f["even_w_in"][0]
    o = np.cumsum([0, Q_LORA, P, ROPE, M_HEADS * M_DK, M_HEADS * M_DK, M_HEADS * M_DV, M_HEADS * M_DV, 4 * M_HEADS])
    gates = np.zeros((D, P), np.float32)
    gates[:, 0:16] = w[:, o[7]:o[8]]
    gates[:, NOPE:MLA_QK] = w[:, o[2]:o[3]]
    out["even_in"] = tiles(np.concatenate([w[:, o[0]:o[2]], gates, w[:, o[3]:o[7]]], 1))
    out["even_out"] = tiles(f["even_w_out"][0])
    out["w_qb"] = c(f["mla_w_qb"][0].reshape(2, P, -1).transpose(1, 0, 2))
    kvb = f["mla_w_kvb"][0].reshape(P, MLA_HEADS, 2, 64)
    out["w_kvb"] = c(kvb.transpose(0, 2, 1, 3)).reshape(P, 2, -1)
    out["ckv_old"] = c(f["cache_mla_ckv"][0, 0].T)
    out["krope_old"] = c(f["cache_mla_krope"][0, 0].T)
    def rope(rot):
        nf = rot // 4
        inv = 10000.0 ** (-np.arange(nf, dtype=np.float32) / np.float32(nf))
        t = np.arange(LAT)
        cos, sin = np.zeros((rot, LAT), np.float32), np.zeros((rot, LAT), np.float32)
        swap = np.zeros((rot, rot), np.float32)
        for j in range(rot):
            axis, second, i = j // (2 * nf), j // nf % 2, j % nf
            ang = ((t // 64, t % 64)[axis]).astype(np.float32) * inv[i].astype(np.float32)
            cos[j] = np.cos(ang)
            sin[j] = np.sin(ang) * (1 if second else -1)
            swap[(j - nf) if second else (j + nf), j] = 1
        return cos, sin, swap
    cos, sin, swap = rope(ROPE)
    out["rope_e"] = np.zeros((P, 2, LAT), np.float32)
    out["rope_e"][NOPE:MLA_QK, 0], out["rope_e"][NOPE:MLA_QK, 1] = cos, sin
    out["swap_e"] = np.zeros((P, ROPE), np.float32)
    out["swap_e"][NOPE:MLA_QK] = swap
    cos, sin, swap = rope(HEAD)
    out["rope_o"] = c(np.stack([np.concatenate([cos, cos]), np.concatenate([sin, sin])], 1))
    out["swap_o"] = np.zeros((P, P), np.float32)
    out["swap_o"][0:64, 0:64] = out["swap_o"][64:128, 64:128] = swap
    pr = np.zeros((P, 2, ROWS), np.float32)
    for d in range(2):
        for h in range(M_HEADS):
            for j in range(2):
                pr[8 * d + 4 * j + h, j, 32 * d + h] = 1
    out["pick_rows"] = pr
    rb = np.zeros((P, 3), np.float32)
    gb, m0 = f["mlstm_gate_b"][0].reshape(2, 2, M_HEADS), f["state_mlstm_m"][0, 0]
    for d in range(2):
        rb[32 * d:32 * d + M_HEADS, 0] = gb[d, 0]
        rb[32 * d:32 * d + M_HEADS, 1] = gb[d, 1]
        rb[32 * d:32 * d + M_HEADS, 2] = m0[d]
    out["row_bias"] = rb
    oh = np.zeros((ROWS, 8, P), np.float32)
    for d in range(2):
        for h in range(M_HEADS):
            oh[32 * d + h, 4 * d + h] = 1
    out["onehot"] = oh
    st = np.zeros((2, M_HEADS, M_DK, 2 * P), np.float32)
    st[..., 0:P] = f["state_mlstm_C"][0, 0]
    st[..., P:] = f["state_mlstm_n"][0, 0][..., None]
    out["state0"] = c(st.reshape(2, 2, P, 2 * P).transpose(2, 0, 1, 3))
    g = np.zeros((P, 8), np.float32)
    g[:, 0:2] = f["mla_g_qa"][0].reshape(2, P).T
    g[:, 2] = f["mla_g_kva"][0]
    g[:, 3:7] = f["mlstm_g_out"][0].reshape(M_HEADS, P).T
    out["gains"] = g
    out["ident"] = np.eye(P, dtype=np.float32)
    i = np.arange(P)
    out["causal"] = c(np.stack([np.where(i[None] >= i[:, None], 0, NEG), np.where(i[None] <= i[:, None], 0, NEG)],
                               1).astype(np.float32))
    order = [4 * (2 * p + half) + m for p in range(2) for m in range(4) for half in range(2)]
    w = f["odd_w_in"][0]
    wq = w[:, 0:D].reshape(D, S_HEADS, HEAD)[:, order].reshape(D, D)
    out["odd_in"] = tiles(np.concatenate([wq, w[:, D:]], 1))
    out["odd_out"] = tiles(f["odd_w_out"][0].reshape(S_HEADS, HEAD, D)[order].reshape(D, D))
    out["k_old"] = c(f["cache_swa_k"][0, 0].reshape(2, 2, PAST, HEAD).transpose(1, 3, 0, 2)).reshape(P, 2, PAST)
    v = f["cache_swa_v"][0, 0].reshape(2, 2, PAST // P, P, HEAD)
    out["v_old"] = c(v.transpose(3, 1, 2, 0, 4))
    sk = np.broadcast_to(f["swa_sink"][0], (P, S_HEADS))
    out["sinks"] = c(sk)
    return out


OUTS = {"y": (P, KT, T), "out_ckv": (P, CTX), "out_krope": (ROPE, CTX), "out_state": (P, 2, 2, 2 * P),
        "out_m": (ROWS, 1), "out_kv": (P, 4, CTX)}


def hand_back(r):
    import numpy as np
    c = np.ascontiguousarray
    y = r["y"].transpose(1, 0, 2).reshape(D, T).T
    st = r["out_state"].reshape(2, M_DK, 2, 2, 2 * P).transpose(2, 3, 0, 1, 4).reshape(1, 1, 2, M_HEADS, M_DK, 2 * P)
    m = np.stack([r["out_m"][0:M_HEADS, 0], r["out_m"][32:32 + M_HEADS, 0]])[None, None]
    kv = r["out_kv"].reshape(2, HEAD, 2, 2, CTX).transpose(2, 3, 0, 4, 1).reshape(2, 1, 1, KV_HEADS, CTX, HEAD)
    return (c(y[0:CTX])[None], c(y[CTX:])[None], c(r["out_ckv"].T)[None, None], c(r["out_krope"].T)[None, None],
            c(st[..., 0:P]), c(st[..., P]), c(m), c(kv[0]), c(kv[1]))


def kernel(**inputs):
    import concourse.bacc as _bacc
    from concourse.bass_utils import run_bass_kernel_spmd as _run

    nc = _bacc.Bacc("TRN2", target_bir_lowering=False, num_devices=1, dynamic_dma_scratch_size=1024)
    arrays = {"in_" + k: v for k, v in lay_out(inputs).items()}
    io = {k[3:]: nc.dram_tensor(k, v.shape, mybir.dt.from_np(v.dtype), kind="ExternalInput").ap()
          for k, v in arrays.items()}
    for name, shape in OUTS.items():
        io[name] = nc.dram_tensor("res_" + name, shape, F32, kind="ExternalOutput").ap()
    build(nc, io)
    r = _run(nc, [arrays], core_ids=[0])
    return hand_back({name: r.results[0]["res_" + name] for name in OUTS})
```
